# Optimizing a Trainium2 kernel written in Bass

```python
import jax, jax.numpy as jnp
from jax import lax
import numpy as np

D_MODEL = 2048
BATCH = 1
SEQ = 256
DEPTH = 1

N_MIXERS = 4
N_META = 16
D_FF = 5632
DEEPNORM_ALPHA = (2 * DEPTH) ** 0.25
DEEPNORM_BETA = (8 * DEPTH) ** -0.25
LN_EPS = 1e-5
RWKV_HEAD_DIM = 64
RWKV_HEADS = D_MODEL // RWKV_HEAD_DIM
RWKV_DECAY_LORA = max(32, int(round(1.8 * D_MODEL ** 0.5 / 32)) * 32)
RWKV_AAA_LORA = max(32, int(round(1.8 * D_MODEL ** 0.5 / 32)) * 32)
RWKV_GATE_LORA = max(32, int(round(0.6 * D_MODEL ** 0.8 / 32)) * 32)
RWKV_GN_EPS = 64e-5
RG_BLOCKS = 16
D_RNN = ((4 * D_MODEL // 3) // (RG_BLOCKS * 8)) * RG_BLOCKS * 8
RG_BLOCK_DIM = D_RNN // RG_BLOCKS
RG_C = 8.0
CONV_W = 4
FOX_HEAD_DIM = 128
FOX_HEADS = D_MODEL // FOX_HEAD_DIM
FOX_BLOCK = 128
ML_HEADS = 8
ML_QK = D_MODEL // 2
ML_V = D_MODEL
ML_DQK = ML_QK // ML_HEADS
ML_DV = ML_V // ML_HEADS
ML_CHUNK = 64
ML_EPS = 1e-6

kernel_name = 'hybrid_interleaved_rwkv7_rglru_fox_mlstm'

def layer_norm(x, g, b):
    xf = x.astype(jnp.float32)
    mu = jnp.mean(xf, -1, keepdims=True)
    var = jnp.mean(jnp.square(xf - mu), -1, keepdims=True)
    return ((xf - mu) * lax.rsqrt(var + LN_EPS) * g + b).astype(x.dtype)

def post_norm(x, y, g, b):
    return layer_norm(DEEPNORM_ALPHA * x + y, g, b)

def swiglu_ffn(x, w_in, w_out):
    gate, up = jnp.split(x @ w_in, 2, axis=-1)
    return (jax.nn.silu(gate) * up) @ w_out

def token_shift(x):
    return jnp.pad(x, ((0, 0), (1, 0), (0, 0)))[:, :-1]

def rwkv7_time_mix(x, mix, w_rkv, w0, w1, w2, a0, a1, a2, g1, g2, k_k, k_a, r_k, gn_g, gn_b, w_o):
    B, L, _ = x.shape
    H, N = RWKV_HEADS, RWKV_HEAD_DIM
    xx = token_shift(x) - x
    xs = x[None] + xx[None] * mix[:, None, None, :]
    r, k, v = jnp.einsum('sbld,sde->sble', xs[:3], w_rkv)
    w_log = -jax.nn.softplus(-(w0 + jnp.tanh(xs[3] @ w1) @ w2)) - 0.5
    a = jax.nn.sigmoid(a0 + (xs[4] @ a1) @ a2)
    g = jax.nn.sigmoid(xs[5] @ g1) @ g2
    heads = lambda t: t.reshape(B, L, H, N).astype(jnp.float32)
    kk = heads(k * k_k)
    kk = kk * lax.rsqrt(jnp.sum(kk * kk, -1, keepdims=True) + 1e-12)
    k = k * (1 + (a - 1) * k_a)
    r_h, k_h, v_h, a_h = heads(r), heads(k), heads(v), heads(a)
    decay = jnp.exp(-jnp.exp(heads(w_log)))

    def step(S, inp):
        r_t, w_t, k_t, v_t, kk_t, b_t = inp
        sa = jnp.einsum('bhvk,bhk->bhv', S, -kk_t)
        S = S * w_t[:, :, None, :] + sa[..., None] * b_t[:, :, None, :] + v_t[..., None] * k_t[:, :, None, :]
        return S, jnp.einsum('bhvk,bhk->bhv', S, r_t)

    tm = lambda t: jnp.moveaxis(t, 1, 0)
    S0 = jnp.zeros((B, H, N, N), jnp.float32)
    _, y = lax.scan(step, S0, (tm(r_h), tm(decay), tm(k_h), tm(v_h), tm(kk), tm(kk * a_h)))
    y = jnp.moveaxis(y, 0, 1)
    mu = jnp.mean(y, -1, keepdims=True)
    var = jnp.mean(jnp.square(y - mu), -1, keepdims=True)
    y = ((y - mu) * lax.rsqrt(var + RWKV_GN_EPS)).reshape(B, L, D_MODEL) * gn_g + gn_b
    bonus = jnp.sum(r_h * k_h * r_k, -1, keepdims=True) * v_h
    y = (y + bonus.reshape(B, L, D_MODEL)) * g
    return y.astype(x.dtype) @ w_o

def _linear_recurrence_combine(left, right):
    a_l, b_l = left
    a_r, b_r = right
    return (a_l * a_r, a_r * b_l + b_r)

def rglru_block(x, w_in, conv_w, conv_b, w_a, b_a, w_x, b_x, lam, w_o):
    B, L, _ = x.shape
    gate_br, u = jnp.split(x @ w_in, 2, axis=-1)
    up = jnp.pad(u, ((0, 0), (CONV_W - 1, 0), (0, 0)))
    uc = conv_b + sum(up[:, j:j + L] * conv_w[j] for j in range(CONV_W))
    ub = uc.reshape(B, L, RG_BLOCKS, RG_BLOCK_DIM)
    r = jax.nn.sigmoid(jnp.einsum('blnc,ncd->blnd', ub, w_a).reshape(B, L, D_RNN) + b_a)
    i = jax.nn.sigmoid(jnp.einsum('blnc,ncd->blnd', ub, w_x).reshape(B, L, D_RNN) + b_x)
    log_a = (-RG_C * r * jax.nn.softplus(-lam)).astype(jnp.float32)
    a = jnp.exp(log_a)
    b = jnp.sqrt(-jnp.expm1(2.0 * log_a)) * (i * uc).astype(jnp.float32)
    _, hs = lax.associative_scan(_linear_recurrence_combine, (a, b), axis=1)
    y = jax.nn.gelu(gate_br) * hs.astype(x.dtype)
    return y @ w_o

def fox_attention(x, w_in, b_f, w_o):
    B, L, _ = x.shape
    H, Dh = FOX_HEADS, FOX_HEAD_DIM
    q, k, v, fl = jnp.split(x @ w_in, [D_MODEL, 2 * D_MODEL, 3 * D_MODEL], axis=-1)
    heads = lambda t: t.reshape(B, L, H, Dh).transpose(0, 2, 1, 3)
    q, k, v = heads(q), heads(k), heads(v)
    logf = jax.nn.log_sigmoid((fl + b_f).astype(jnp.float32))
    c = jnp.cumsum(logf, axis=1).transpose(0, 2, 1)
    scale = Dh ** -0.5
    pos = jnp.arange(L)

    def attend(qb, cq, q_pos, kk, vv, ck, k_pos):
        s = jnp.einsum('bhqd,bhkd->bhqk', qb, kk).astype(jnp.float32) * scale
        s = s + cq[..., :, None] - ck[..., None, :]
        s = jnp.where(k_pos[None, :] <= q_pos[:, None], s, -jnp.inf)
        p = jax.nn.softmax(s, axis=-1)
        return jnp.einsum('bhqk,bhkd->bhqd', p.astype(vv.dtype), vv)

    m = N_META
    o_meta = attend(q[:, :, :m], c[:, :, :m], pos[:m], k[:, :, :m], v[:, :, :m], c[:, :, :m], pos[:m])
    nb = (L - m) // FOX_BLOCK
    qb = q[:, :, m:].reshape(B, H, nb, FOX_BLOCK, Dh).transpose(2, 0, 1, 3, 4)
    cb = c[:, :, m:].reshape(B, H, nb, FOX_BLOCK).transpose(2, 0, 1, 3)

    def block(args):
        qi, ci, bi = args
        q_pos = m + bi * FOX_BLOCK + jnp.arange(FOX_BLOCK)
        return attend(qi, ci, q_pos, k, v, c, pos)

    o_real = lax.map(block, (qb, cb, jnp.arange(nb)))
    o_real = o_real.transpose(1, 2, 0, 3, 4).reshape(B, H, L - m, Dh)
    o = jnp.concatenate([o_meta, o_real], axis=2).transpose(0, 2, 1, 3).reshape(B, L, D_MODEL)
    return o @ w_o

def mlstm_chunk(state, inp):
    C, n, m = state
    q, k, v, ig, lf = inp
    Lc = q.shape[2]
    b = jnp.cumsum(lf, axis=-1)
    causal = jnp.tril(jnp.ones((Lc, Lc), dtype=bool))
    dmat = jnp.where(causal, b[..., :, None] - b[..., None, :] + ig[..., None, :], -jnp.inf)
    inter = b + m[..., None]
    m_t = jnp.maximum(inter, jnp.max(dmat, axis=-1))
    w_intra = jnp.exp(dmat - m_t[..., None])
    w_inter = jnp.exp(inter - m_t)
    s = jnp.einsum('bhtd,bhsd->bhts', q, k) * w_intra
    num = jnp.einsum('bhts,bhsv->bhtv', s, v) + w_inter[..., None] * jnp.einsum('bhtd,bhdv->bhtv', q, C)
    den = jnp.sum(s, -1) + w_inter * jnp.einsum('bhtd,bhd->bht', q, n)
    h = num / jnp.maximum(jnp.abs(den), jnp.exp(-m_t))[..., None]
    b_end = b[..., -1]
    d_end = b_end[..., None] - b + ig
    m_new = jnp.maximum(b_end + m, jnp.max(d_end, axis=-1))
    w_s = jnp.exp(d_end - m_new[..., None])
    carry = jnp.exp(b_end + m - m_new)
    C_new = carry[..., None, None] * C + jnp.einsum('bhs,bhsd,bhsv->bhdv', w_s, k, v)
    n_new = carry[..., None] * n + jnp.einsum('bhs,bhsd->bhd', w_s, k)
    return (C_new, n_new, m_new), h

def mlstm_block(x, w_in, b_if, norm_g, w_o):
    B, L, _ = x.shape
    H = ML_HEADS
    splits = [ML_QK, 2 * ML_QK, 2 * ML_QK + ML_V, 2 * ML_QK + 2 * ML_V, 2 * ML_QK + 2 * ML_V + H]
    q, k, v, o, ig, fg = jnp.split(x @ w_in, splits, axis=-1)
    heads = lambda t, d: t.reshape(B, L, H, d).transpose(0, 2, 1, 3).astype(jnp.float32)
    q = heads(q, ML_DQK)
    k = heads(k, ML_DQK) * (ML_DQK ** -0.5)
    v = heads(v, ML_DV)
    ig = (ig + b_if[0]).astype(jnp.float32).transpose(0, 2, 1)
    lf = jax.nn.log_sigmoid((fg + b_if[1]).astype(jnp.float32)).transpose(0, 2, 1)
    state0 = (jnp.zeros((B, H, ML_DQK, ML_DV), jnp.float32),
              jnp.zeros((B, H, ML_DQK), jnp.float32),
              jnp.zeros((B, H), jnp.float32))
    m = N_META
    state, h_meta = mlstm_chunk(state0, (q[:, :, :m], k[:, :, :m], v[:, :, :m], ig[:, :, :m], lf[:, :, :m]))
    nc = (L - m) // ML_CHUNK
    chunks = lambda t: jnp.moveaxis(t[:, :, m:].reshape((B, H, nc, ML_CHUNK) + t.shape[3:]), 2, 0)
    _, h_real = lax.scan(mlstm_chunk, state, (chunks(q), chunks(k), chunks(v), chunks(ig), chunks(lf)))
    h_real = jnp.moveaxis(h_real, 0, 2).reshape(B, H, L - m, ML_DV)
    h = jnp.concatenate([h_meta, h_real], axis=2)
    h = h * lax.rsqrt(jnp.mean(jnp.square(h), -1, keepdims=True) + ML_EPS)
    h = h.transpose(0, 2, 1, 3).reshape(B, L, ML_V) * norm_g
    y = (h * jax.nn.sigmoid(o)).astype(x.dtype)
    return y @ w_o

def setup_inputs(seed: int = 0) -> dict:
    key = jax.random.key(seed)
    ks = jax.random.split(key, 48)
    counter = [0]

    def nxt():
        counter[0] += 1
        return ks[counter[0] - 1]

    def nrm(shape, scale):
        return jax.random.normal(nxt(), shape, jnp.float32) * scale

    def unif(shape, lo, hi):
        return jax.random.uniform(nxt(), shape, jnp.float32, lo, hi)

    D = D_MODEL
    beta = DEEPNORM_BETA
    a_target = unif((D_RNN,), 0.9, 0.999)
    s_lam = a_target ** (1.0 / RG_C)
    return {
        'x': nrm((BATCH, SEQ, D), 1.0),
        'meta_tokens': nrm((N_META, D), 1.0),
        'ln_g': 1.0 + nrm((DEPTH, 3, D), 0.02),
        'ln_b': nrm((DEPTH, 3, D), 0.02),
        'ffn_in': nrm((DEPTH, 2, D, 2 * D_FF), D ** -0.5),
        'ffn_out': nrm((DEPTH, 2, D_FF, D), beta * D_FF ** -0.5),
        'rwkv_mix': unif((6, D), 0.0, 1.0),
        'rwkv_w_rkv': nrm((3, D, D), D ** -0.5),
        'rwkv_w0': unif((D,), -6.5, -1.5),
        'rwkv_w1': nrm((D, RWKV_DECAY_LORA), D ** -0.5),
        'rwkv_w2': nrm((RWKV_DECAY_LORA, D), 0.1 * RWKV_DECAY_LORA ** -0.5),
        'rwkv_a0': nrm((D,), 0.1),
        'rwkv_a1': nrm((D, RWKV_AAA_LORA), D ** -0.5),
        'rwkv_a2': nrm((RWKV_AAA_LORA, D), 0.1 * RWKV_AAA_LORA ** -0.5),
        'rwkv_g1': nrm((D, RWKV_GATE_LORA), D ** -0.5),
        'rwkv_g2': nrm((RWKV_GATE_LORA, D), RWKV_GATE_LORA ** -0.5),
        'rwkv_k_k': 0.85 + nrm((D,), 0.05),
        'rwkv_k_a': 1.0 + nrm((D,), 0.05),
        'rwkv_r_k': nrm((RWKV_HEADS, RWKV_HEAD_DIM), 0.1),
        'rwkv_gn_g': 1.0 + nrm((D,), 0.02),
        'rwkv_gn_b': nrm((D,), 0.02),
        'rwkv_w_o': nrm((D, D), beta * D ** -0.5),
        'rg_w_in': nrm((D, 2 * D_RNN), D ** -0.5),
        'rg_conv_w': nrm((CONV_W, D_RNN), 0.5),
        'rg_conv_b': nrm((D_RNN,), 0.02),
        'rg_w_a': nrm((RG_BLOCKS, RG_BLOCK_DIM, RG_BLOCK_DIM), RG_BLOCK_DIM ** -0.5),
        'rg_b_a': nrm((D_RNN,), 0.1),
        'rg_w_x': nrm((RG_BLOCKS, RG_BLOCK_DIM, RG_BLOCK_DIM), RG_BLOCK_DIM ** -0.5),
        'rg_b_x': nrm((D_RNN,), 0.1),
        'rg_lambda': jnp.log(s_lam) - jnp.log1p(-s_lam),
        'rg_w_o': nrm((D_RNN, D), beta * D_RNN ** -0.5),
        'fox_w_in': nrm((D, 3 * D + FOX_HEADS), D ** -0.5),
        'fox_b_f': 2.0 + nrm((FOX_HEADS,), 0.5),
        'fox_w_o': nrm((D, D), beta * D ** -0.5),
        'ml_w_in': nrm((D, 2 * ML_QK + 2 * ML_V + 2 * ML_HEADS), D ** -0.5),
        'ml_b_if': jnp.stack([nrm((ML_HEADS,), 0.1), 3.0 + nrm((ML_HEADS,), 0.5)]),
        'ml_norm_g': 1.0 + nrm((ML_V,), 0.02),
        'ml_w_o': nrm((ML_V, D), beta * ML_V ** -0.5),
    }

def reference(x, meta_tokens, ln_g, ln_b, ffn_in, ffn_out,
              rwkv_mix, rwkv_w_rkv, rwkv_w0, rwkv_w1, rwkv_w2, rwkv_a0, rwkv_a1, rwkv_a2,
              rwkv_g1, rwkv_g2, rwkv_k_k, rwkv_k_a, rwkv_r_k, rwkv_gn_g, rwkv_gn_b, rwkv_w_o,
              rg_w_in, rg_conv_w, rg_conv_b, rg_w_a, rg_b_a, rg_w_x, rg_b_x, rg_lambda, rg_w_o,
              fox_w_in, fox_b_f, fox_w_o,
              ml_w_in, ml_b_if, ml_norm_g, ml_w_o):
    B = x.shape[0]
    meta = jnp.broadcast_to(meta_tokens.astype(x.dtype)[None], (B, N_META, D_MODEL))
    h = jnp.concatenate([meta, x], axis=1)
    for layer in range(DEPTH):
        h = post_norm(h, 0.5 * swiglu_ffn(h, ffn_in[layer, 0], ffn_out[layer, 0]), ln_g[layer, 0], ln_b[layer, 0])
        kind = layer % N_MIXERS
        if kind == 0:
            y = rwkv7_time_mix(h, rwkv_mix, rwkv_w_rkv, rwkv_w0, rwkv_w1, rwkv_w2, rwkv_a0, rwkv_a1, rwkv_a2,
                               rwkv_g1, rwkv_g2, rwkv_k_k, rwkv_k_a, rwkv_r_k, rwkv_gn_g, rwkv_gn_b, rwkv_w_o)
        elif kind == 1:
            y = rglru_block(h, rg_w_in, rg_conv_w, rg_conv_b, rg_w_a, rg_b_a, rg_w_x, rg_b_x, rg_lambda, rg_w_o)
        elif kind == 2:
            y = fox_attention(h, fox_w_in, fox_b_f, fox_w_o)
        else:
            y = mlstm_block(h, ml_w_in, ml_b_if, ml_norm_g, ml_w_o)
        h = post_norm(h, y, ln_g[layer, 1], ln_b[layer, 1])
        h = post_norm(h, 0.5 * swiglu_ffn(h, ffn_in[layer, 1], ffn_out[layer, 1]), ln_g[layer, 2], ln_b[layer, 2])
    return h[:, N_META:]


_drawn_inputs = setup_inputs


def setup_inputs(seed=0):
    import zlib

    import numpy as np

    out = dict(_drawn_inputs(seed))
    spreads = {}
    factors = {'rwkv_w1': 8.0,
     'rwkv_w2': 8.0,
     'rwkv_a0': 4.981,
     'rwkv_a1': 4.991,
     'rwkv_a2': 5.008,
     'rwkv_k_k': 4.924,
     'rwkv_k_a': 3.987,
     'rwkv_gn_g': 8.0,
     'rwkv_gn_b': 8.0}
    for name, (base, spread) in spreads.items():
        noise = np.random.default_rng([zlib.crc32(name.encode()), seed]).standard_normal(out[name].shape)
        drawn = base * np.exp(spread * noise) if base else spread * noise
        out[name] = __import__('jax').numpy.asarray(drawn.astype(out[name].dtype))
    for name, factor in factors.items():
        out[name] = (out[name] * factor).astype(out[name].dtype)
    return out
```

```python
from contextlib import ExitStack
from math import exp

import numpy as np
import concourse.bass as bass
from concourse import mybir

F32 = mybir.dt.float32
F32R = mybir.dt.float32r
ALU = mybir.AluOpType
ACT = mybir.ActivationFunctionType

P = 128
D = 2048
D_FF = 5632
SEQ = 256
N_META = 16
L = SEQ + N_META
KD = D // P
KF = D_FF // P
HEAD = 64
CHUNK = 64
PAD = CHUNK - N_META
NCH = (L + PAD) // CHUNK
LP = NCH * CHUNK
LORA = 96
GATE = 256
ALPHA = 2.0 ** 0.25
LN_EPS = 1e-5
GN_EPS = 64e-5
DECAY = exp(-0.5)

RING = 4
KB = 4
WIDE = 256
LEVELS = [2, 4, 8, 16, 32]

VECTORS = ["ln_g", "ln_b", "rwkv_mix", "rwkv_w0", "rwkv_a0", "rwkv_k_k", "rwkv_k_a", "rwkv_r_k",
           "rwkv_gn_g", "rwkv_gn_b"]
V_LN_G, V_LN_B, V_MIX, V_W0, V_A0, V_KK, V_KA, V_RK, V_GN_G, V_GN_B = 0, 3, 6, 12, 13, 14, 15, 16, 17, 18
NVEC = 19


def constants():
    p = np.arange(P)
    head, s = p // CHUNK, p % CHUNK
    t = np.arange(CHUNK)
    same = (head[:, None] == np.arange(2)[None, :]).astype(np.float32)[:, :, None]
    c = {
        "ident": np.eye(P),
        "stack_i": s[:, None] == t[None, :],
        "ones_mean": np.full((P, P), 1.0 / D),
        "head_sum": head[:, None] == head[None, :],
        "head_mean": (head[:, None] == head[None, :]) / HEAD,
        "bd": same * np.ones((1, 1, CHUNK)),
        "bd_strict": same * (s[:, None] < t[None, :])[:, None, :],
        "incl": s[:, None] <= t[None, :],
        "bd_i": same * (s[:, None] == t[None, :])[:, None, :],
        "off1": (s[:, None] // 2 == t[None, :] // 2) & (s[:, None] > t[None, :]),
        "restart": np.broadcast_to(np.arange(LP) % CHUNK != 0, (P, LP)),
    }
    for b in [1] + LEVELS:
        up = (s[:, None] // (2 * b) == t[None, :] // (2 * b)) & (s[:, None] // b < t[None, :] // b)
        c[f"offT{b}"] = same * up[:, None, :]
    return {k: np.ascontiguousarray(np.asarray(v, np.float32).reshape(P, -1)) for k, v in c.items()}


class Group:

    def __init__(self, weight, column, step, width=WIDE):
        self.weight, self.column, self.step, self.width = weight, column, step, width


class Phase:

    def __init__(self, name, steps, nb, groups, rhs, tok, ready, side=None):
        self.name, self.steps, self.nb, self.groups = name, steps, nb, groups
        self.rhs, self.tok, self.ready, self.side = rhs, tok, ready, side
        self.n = tok.stop - tok.start
        self.kind = name.rstrip("01")


def number(phases):
    block, uses = 0, [0] * RING
    count = {"staged": 0, "pairs": 0, "added": 0, "projected": 0}
    for ph in phases:
        ph.block0, ph.uses0 = block, list(uses)
        ph.staged0, ph.pairs0 = count["staged"], count["pairs"]
        ph.added0, ph.projected0 = count["added"], count["projected"]
        ph.blocks = ph.nb * len(ph.groups)
        ph.per_group = [len(range(s, ph.nb, RING)) for s in range(RING)]
        block += ph.steps * ph.blocks
        for s in range(RING):
            uses[s] += ph.steps * len(ph.groups) * ph.per_group[s]
        n = ph.steps * len(ph.groups)
        if ph.kind == "in":
            count["staged"] += ph.steps
            count["pairs"] += ph.steps
        elif ph.kind in ("out", "w_o"):
            count["staged"] += n
            count["added"] += n
        else:
            count["projected"] += n
        ph.end = block


def wait(eng, sem, value):
    if not isinstance(value, int) or value > 0:
        eng.wait_ge(sem, value)


def rwkv_layer(nc, x, meta, w, vec, const, out):
    with ExitStack() as ctx:
        def sem(name):
            return ctx.enter_context(nc.semaphore(name))

        XBYTES = KD * L * 4
        ARENA = 2 * (KD + KF) * L * 4
        start = (nc.sbuf_base + 31) // 32 * 32
        fixed = [start]

        def sb(name, shape, dt=F32):
            n = int(np.prod(shape[1:])) * 4
            t = nc.alloc_sbuf_tensor_at(name, shape, dt, offset=fixed[0])
            fixed[0] += (n + 31) // 32 * 32
            return t

        X = sb("X", [P, KD, L])
        RAW = sb("RAW", [P, RING, KB, WIDE])
        WH = sb("WH", [P, RING, KB, WIDE], F32R)
        WL = sb("WL", [P, RING, KB, WIDE], F32R)
        C = {k: sb("c_" + k, [P, n]) for k, n in CONST_COLUMNS.items()}
        PAR = sb("PAR", [P, NVEC, KD])
        HALF = sb("HALF", [P, 2, KD])
        STAGE = sb("STAGE", [P, 2, L])
        HV = sb("HV", [P, 2, L])
        RS = sb("RS", [P, L])
        at0 = fixed[0]
        assert at0 + ARENA <= nc.sbuf_usable_end, (at0 + ARENA, nc.sbuf_usable_end)

        def at(name, shape, offset, dt=F32):
            n = int(np.prod(shape[1:])) * 4
            assert offset + n <= ARENA, (name, offset, n)
            return nc.alloc_sbuf_tensor_at(name, shape, dt, offset=at0 + offset)

        XA = at("XA", [P, 2, KD, L], 0, F32R)
        H = at("H", [P, 2, KF, L], 2 * XBYTES, F32R)
        TOKS = at("TOKS", [P, 3, D], 2 * XBYTES)
        VROWS = at("VROWS", [P, 3, P], 2 * XBYTES + 12 * D)
        SQ = at("SQ", [P, KD, L], 2 * XBYTES)
        OUT = at("OUT", [P, 2, D], 2 * XBYTES)
        XS = at("XS", [P, 2, 2, KD, L], 0, F32R)
        KVR = at("KVR", [P, 3, KD, L], 4 * XBYTES)
        XX = KVR[:, 2]
        LH = at("LH", [P, 4, L], 7 * XBYTES)
        XT = at("XT", [P, L], 7 * XBYTES + 16 * L)
        YA = at("YA", [P, 2, KD, SEQ], 0, F32R)
        PS = ctx.enter_context(nc.psum_tensor("PS", [P, 8, 512], F32))

        cursor = [0]

        def tmp(name, *shape):
            t = at(name, [P, *shape], cursor[0])
            cursor[0] += int(np.prod(shape)) * 4
            assert cursor[0] <= 4 * XBYTES, name
            return t

        CC, BD = (NCH, CHUNK), (NCH, 2, CHUNK)
        KP, RP, VP = tmp("KP", *CC), tmp("RP", *CC), tmp("VP", *CC)
        LWD, AA, TH = tmp("LWD", *CC), tmp("AA", *CC), tmp("TH", *CC)
        SQK, RN, KK = tmp("SQK", *CC), tmp("RN", *CC), tmp("KK", *CC)
        CUM, CM = tmp("CUM", *CC), tmp("CM", *CC)
        E, EI = tmp("E", *CC), tmp("EI", *CC)
        AC, RC, BC, K2, KH = (tmp(n, *CC) for n in ("AC", "RC", "BC", "K2", "KH"))
        ABD, BBD, KBD, VBD = (tmp(n, *BD) for n in ("ABD", "BBD", "KBD", "VBD"))
        LT, GAK, BTB, KTB, VTB = (tmp(n, *BD) for n in ("LT", "GAK", "BTB", "KTB", "VTB"))
        ZBD, TTB, OFF = (tmp(n, *BD) for n in ("ZBD", "TTB", "OFF"))
        GRB, GRK, VT, ZC, TC, TTC = (tmp(n, *CC) for n in ("GRB", "GRK", "VT", "ZC", "TC", "TTC"))
        SC, RHS, UC, ST = (tmp(n, CHUNK) for n in ("SC", "RHS", "UC", "ST"))
        SBD, UBD = tmp("SBD", 2, CHUNK), tmp("UBD", 2, CHUNK)
        YC, LW = tmp("YC", SEQ), tmp("LW", 4, P)
        PP = tmp("PP", NVEC + 2)
        YQ = HV[:, 0, 0:SEQ]
        RG = RS[:, 0:SEQ]

        const_landed, tokens_landed, vectors_landed = sem("const_landed"), sem("tokens_landed"), sem("vectors_landed")
        raw_landed = [sem(f"raw_landed{s}") for s in range(RING)]
        hi_made, lo_made, blocks_multiplied = sem("hi_made"), sem("lo_made"), sem("blocks_multiplied")
        stage_filled, residual_added, projected = sem("stage_filled"), sem("residual_added"), sem("projected")
        hv_made, h_hi_made, h_lo_made = sem("hv_made"), sem("h_hi_made"), sem("h_lo_made")
        x_hi_made, x_lo_made = sem("x_hi_made"), sem("x_lo_made")
        turned, turned_copied, params_copied, params_halved = (
            sem("turned"), sem("turned_copied"), sem("params_copied"), sem("params_halved"))
        ln_mean, ln_centred, ln_squared, ln_var = sem("ln_mean"), sem("ln_centred"), sem("ln_squared"), sem("ln_var")
        ln_eps_added, ln_rooted, ln_inverted = sem("ln_eps_added"), sem("ln_rooted"), sem("ln_inverted")
        ln_scaled, ln_shifted = sem("ln_scaled"), sem("ln_shifted")
        xx_made, mix_made, mix_hi_made, mix_lo_made = sem("xx_made"), sem("mix_made"), sem("mix_hi_made"), sem("mix_lo_made")
        y_hi_made, y_lo_made = sem("y_hi_made"), sem("y_lo_made")
        out_turned, out_copied, out_stored = sem("out_turned"), sem("out_copied"), sem("out_stored")

        ALL, REAL = slice(0, L), slice(N_META, L)

        def ffn(f, tok):
            win, wout = w["ffn_in"][f], w["ffn_out"][f]
            return [
                Phase(f"in{f}", KF // 2, KD // KB, [Group(win, 0, WIDE), Group(win, D_FF, WIDE)],
                      lambda h, k: XA[:, h, k, tok], tok, lambda j: (x_lo_made, KD * f + KB * (j + 1))),
                Phase(f"out{f}", KD // 4, KF // KB, [Group(wout, 0, 2 * WIDE), Group(wout, WIDE, 2 * WIDE)],
                      lambda h, k: H[:, h, k, tok], tok, lambda j: (h_lo_made, KF // 2 * f + KB // 2 * (j + 1)))]

        def mixed(buf):
            return lambda h, k: XS[:, buf, h, k, :]

        def mix_ready(v):
            return lambda j: (mix_lo_made, KD * v + KB * (j + 1))

        def square(name, weight, rhs, tok, ready, side=None):
            return Phase(name, KD // 4, KD // KB, [Group(weight, 0, 2 * WIDE), Group(weight, WIDE, 2 * WIDE)],
                         rhs, tok, ready, side)

        MIXES = [3, 4, 5, 1, 2, 0]
        wkv = w["rwkv_w_rkv"]
        in0, out0 = ffn(0, ALL)
        lora_w = Phase("lora_w", 1, KD // KB, [Group(w["rwkv_w1"], 0, 0, LORA)], mixed(0), ALL, mix_ready(0))
        lora_a = Phase("lora_a", 1, KD // KB, [Group(w["rwkv_a1"], 0, 0, LORA)], mixed(1), ALL, mix_ready(1))
        lora_g = Phase("lora_g", 1, KD // KB, [Group(w["rwkv_g1"], 0, 0, GATE)], mixed(0), ALL, mix_ready(2))
        proj_k = square("k", wkv[1], mixed(1), ALL, mix_ready(3), side=4)
        proj_v = square("v", wkv[2], mixed(0), ALL, mix_ready(4), side=5)
        proj_r = square("r", wkv[0], mixed(1), ALL, mix_ready(5))
        w_o = square("w_o", w["rwkv_w_o"], lambda h, k: YA[:, h, k, :], REAL, lambda j: (y_lo_made, KB * (j + 1)))
        in1, out1 = ffn(1, REAL)
        phases = [in0, out0, lora_w, lora_a, lora_g, proj_k, proj_v, proj_r, w_o, in1, out1]
        number(phases)
        mix_free = {2: lora_w, 3: lora_a, 4: lora_g, 5: proj_k}
        SLOT = {"k": 0, "v": 1, "r": 2}

        def loop(eng, ph, body):
            body(0, True)
            if ph.steps > 1:
                with eng.Fori(1, ph.steps) as t:
                    body(t, False)

        def block_of(ph, t, g, j):
            return ph.block0 + t * ph.blocks + g * ph.nb + j

        def load_blocks(sp, ph):
            def body(t, first):
                for g, grp in enumerate(ph.groups):
                    for j in range(ph.nb):
                        slot = j % RING
                        wait(sp, lo_made, block_of(ph, t, g, j) - 2)
                        rows = grp.weight[j * KB * P:(j + 1) * KB * P, :].rearrange("(k p) n -> p k n", p=P)
                        sp.dma_start(RAW[:, slot, :, 0:grp.width],
                                     rows[:, :, bass.ds(grp.column + t * grp.step, grp.width)])\
                          .then_inc(raw_landed[slot], 16)
            loop(sp, ph, body)

        def split_hi(act, ph, t, g, j):
            slot, width = j % RING, ph.groups[g].width
            use = ph.uses0[slot] + (t * len(ph.groups) + g) * ph.per_group[slot] + j // RING
            act.wait_ge(raw_landed[slot], 16 * use + 16)
            wait(act, blocks_multiplied, block_of(ph, t, g, j) - 2)
            nc.scalar.activation(WH[:, slot, :, 0:width], RAW[:, slot, :, 0:width], ACT.Copy).then_inc(hi_made, 1)

        def split_lo(dve, ph, t, g, j):
            slot, width = j % RING, ph.groups[g].width
            dve.wait_ge(hi_made, block_of(ph, t, g, j) + 1)
            wait(dve, blocks_multiplied, block_of(ph, t, g, j) - 2)
            nc.vector.tensor_tensor(WL[:, slot, :, 0:width], RAW[:, slot, :, 0:width],
                                    WH[:, slot, :, 0:width].bitcast(F32), ALU.subtract).then_inc(lo_made, 1)

        def wait_for_banks(pe, ph, t, g):
            turn = 2 * t + g - 1
            if isinstance(turn, int):
                turn = max(turn, 0)
            if ph.kind == "in":
                if g == 0:
                    wait(pe, stage_filled, ph.staged0 + t)
                else:
                    wait(pe, hv_made, ph.pairs0 + t)
            elif ph.kind in ("out", "w_o"):
                wait(pe, stage_filled, ph.staged0 + turn)
            else:
                wait(pe, projected, ph.projected0 + turn)

        def multiply(pe, ph):
            def body(t, first):
                for g, grp in enumerate(ph.groups):
                    wait_for_banks(pe, ph, t, g)
                    for j in range(ph.nb):
                        slot = j % RING
                        if first and g == 0:
                            pe.wait_ge(*ph.ready(j))
                        pe.wait_ge(lo_made, block_of(ph, t, g, j) + 1)
                        for m in range(0, grp.width, P):
                            mw = min(P, grp.width - m)
                            o = PS[0:mw, 2 * g + m // P, 0:ph.n]
                            for k in range(KB):
                                kk = j * KB + k
                                hi, lo = WH[:, slot, k, m:m + mw], WL[:, slot, k, m:m + mw]
                                nc.tensor.matmul(o, hi, ph.rhs(0, kk), start=(kk == 0), stop=False)
                                nc.tensor.matmul(o, hi, ph.rhs(1, kk), start=False, stop=False)
                                mm = nc.tensor.matmul(o, lo, ph.rhs(0, kk), start=False,
                                                      stop=(kk == ph.nb * KB - 1))
                        mm.then_inc(blocks_multiplied, 1)
            loop(pe, ph, body)

        def epilogue_act(act, ph, t, g):
            ps = PS[:, 2 * g:2 * g + 2, 0:ph.n]
            if ph.kind == "in" and g == 1:
                act.wait_ge(hv_made, ph.pairs0 + t + 1)
                nc.scalar.activation(H[:, 0, bass.ds(2 * t, 2), ph.tok], HV[:, :, 0:ph.n], ACT.Copy)\
                  .then_inc(h_hi_made, 1)
                return
            act.wait_ge(blocks_multiplied, block_of(ph, t, g, ph.nb))
            if ph.kind == "in":
                wait(act, hv_made, ph.pairs0 + t)
                nc.scalar.activation(STAGE[:, :, 0:ph.n], ps, ACT.Silu).then_inc(stage_filled, 1)
            elif ph.kind in ("out", "w_o"):
                wait(act, residual_added, ph.added0 + 2 * t + g)
                nc.scalar.activation(STAGE[:, :, 0:ph.n], ps, ACT.Copy, scale=0.5 if ph.kind == "out" else 1.0)\
                  .then_inc(stage_filled, 1)
            elif ph.kind == "lora_w":
                nc.scalar.activation(LH[0:LORA, 0, :], PS[0:LORA, 0, 0:L], ACT.Tanh).then_inc(projected, 1)
            elif ph.kind == "lora_a":
                nc.scalar.activation(LH[0:LORA, 1, :], PS[0:LORA, 0, 0:L], ACT.Copy).then_inc(projected, 1)
            elif ph.kind == "lora_g":
                nc.scalar.activation(LH[:, 2:4, :], ps, ACT.Sigmoid).then_inc(projected, 1)
            else:
                nc.scalar.activation(KVR[:, SLOT[ph.kind], bass.ds(4 * t + 2 * g, 2), :], ps, ACT.Copy)\
                  .then_inc(projected, 1)

        def epilogue_dve(dve, ph, t, g):
            if ph.kind == "in" and g == 1:
                dve.wait_ge(blocks_multiplied, block_of(ph, t, g, ph.nb))
                dve.wait_ge(stage_filled, ph.staged0 + t + 1)
                wait(dve, h_lo_made, ph.pairs0 + t)
                nc.vector.tensor_tensor(HV[:, :, 0:ph.n], STAGE[:, :, 0:ph.n],
                                        PS[:, 2:4, 0:ph.n], ALU.mult).then_inc(hv_made, 1)
            elif ph.kind in ("out", "w_o"):
                dve.wait_ge(stage_filled, ph.staged0 + 2 * t + g + 1)
                xt = X[:, bass.ds(4 * t + 2 * g, 2), ph.tok]
                nc.vector.scalar_tensor_tensor(out=xt, in0=xt, scalar=ALPHA, in1=STAGE[:, :, 0:ph.n],
                                               op0=ALU.mult, op1=ALU.add).then_inc(residual_added, 1)

        def split_hidden(dve, ph, t):
            dve.wait_ge(h_hi_made, ph.pairs0 + t + 1)
            to = bass.ds(2 * t, 2)
            nc.vector.tensor_tensor(H[:, 1, to, ph.tok], HV[:, :, 0:ph.n], H[:, 0, to, ph.tok].bitcast(F32),
                                    ALU.subtract).then_inc(h_lo_made, 1)

        def with_epilogues(eng, ph, split, epilogue, late=None, side=None):
            last = len(ph.groups) - 1

            def body(t, first):
                for g in range(last + 1):
                    for j in range(ph.nb):
                        split(eng, ph, t, g, j)
                        before = not first or g > 0
                        if j == 1 and before:
                            epilogue(eng, ph, t if g else t - 1, g - 1 if g else last)
                        if j == 2 and before and late and g == 0:
                            late(eng, ph, t - 1)
                        if side and ph.side is not None and j % 2:
                            side(eng, ph.side, 4 * t + 2 * g + j // 2)
            loop(eng, ph, body)
            epilogue(eng, ph, ph.steps - 1, last)
            if late:
                late(eng, ph, ph.steps - 1)

        def mix_dve(dve, v, k):
            if v in mix_free:
                dve.wait_ge(blocks_multiplied, mix_free[v].end)
            wait(dve, mix_lo_made, KD * v + k)
            nc.vector.scalar_tensor_tensor(out=XT[:], in0=XX[:, k, :], scalar=PAR[:, V_MIX + MIXES[v], ds1(k)],
                                           in1=X[:, k, :], op0=ALU.mult, op1=ALU.add).then_inc(mix_made, 1)
            dve.wait_ge(mix_hi_made, KD * v + k + 1)
            nc.vector.tensor_tensor(XS[:, v % 2, 1, k, :], XT[:], XS[:, v % 2, 0, k, :].bitcast(F32),
                                    ALU.subtract).then_inc(mix_lo_made, 1)

        def mix_act(act, v, k):
            act.wait_ge(mix_made, KD * v + k + 1)
            nc.scalar.activation(XS[:, v % 2, 0, k, :], XT[:], ACT.Copy).then_inc(mix_hi_made, 1)

        def ds1(k):
            return bass.ds(k, 1)

        QUARTERS = 4
        QK = KD // QUARTERS

        def ln_pe(pe, n, tok):
            N = tok.stop - tok.start
            pe.wait_ge(residual_added, KD // 2 * (n + 1))
            for k in range(KD):
                mm = nc.tensor.matmul(PS[:, 4, 0:N], C["ones_mean"][:], X[:, k, tok], start=(k == 0), stop=(k == KD - 1))
            mm.then_inc(ln_mean, 1)
            for q in range(QUARTERS):
                pe.wait_ge(ln_squared, QUARTERS * n + q + 1)
                for k in range(q * QK, (q + 1) * QK):
                    mm = nc.tensor.matmul(PS[:, 5, 0:N], C["ones_mean"][:], SQ[:, k, 0:N],
                                          start=(k == 0), stop=(k == KD - 1))
            mm.then_inc(ln_var, 1)

        def ln_act(act, n, tok):
            N = tok.stop - tok.start
            for q in range(QUARTERS):
                act.wait_ge(ln_centred, QUARTERS * n + q + 1)
                nc.scalar.activation(SQ[:, q * QK:(q + 1) * QK, 0:N], X[:, q * QK:(q + 1) * QK, tok], ACT.Square)\
                  .then_inc(ln_squared, 1)
            act.wait_ge(ln_eps_added, n + 1)
            nc.scalar.activation(RS[:, 0:N], RS[:, 0:N], ACT.Sqrt).then_inc(ln_rooted, 1)

        def ln_dve(dve, n, tok):
            N = tok.stop - tok.start
            dve.wait_ge(ln_mean, n + 1)
            for q in range(QUARTERS):
                xq = X[:, q * QK:(q + 1) * QK, tok]
                nc.vector.tensor_tensor(xq, xq, PS[:, 4:5, 0:N].to_broadcast((P, QK, N)), ALU.subtract)\
                  .then_inc(ln_centred, 1)
            dve.wait_ge(ln_var, n + 1)
            nc.vector.tensor_scalar(RS[:, 0:N], PS[:, 5, 0:N], LN_EPS, None, ALU.add).then_inc(ln_eps_added, 1)
            dve.wait_ge(ln_rooted, n + 1)
            nc.vector.reciprocal(RS[:, 0:N], RS[:, 0:N]).then_inc(ln_inverted, 1)
            dve.wait_ge(ln_inverted, n + 1)
            for k in range(KD):
                nc.vector.scalar_tensor_tensor(out=X[:, k, tok], in0=X[:, k, tok], scalar=PAR[:, V_LN_G + n, k:k + 1],
                                               in1=RS[:, 0:N], op0=ALU.mult, op1=ALU.mult).then_inc(ln_scaled, 1)
            for k in range(KD):
                dve.wait_ge(ln_scaled, KD * n + k + 1)
                nc.vector.tensor_scalar(X[:, k, tok], X[:, k, tok], PAR[:, V_LN_B + n, k:k + 1], None, ALU.add)\
                  .then_inc(ln_shifted, 1)

        def split_x_act(act, f, tok):
            for k in range(KD):
                if f == 0:
                    act.wait_ge(turned_copied, 3 * (k // 4 + 1))
                else:
                    act.wait_ge(ln_shifted, KD + k + 1)
                nc.scalar.activation(XA[:, 0, k, tok], X[:, k, tok], ACT.Copy).then_inc(x_hi_made, 1)

        def split_x_dve(dve, f, tok):
            for k in range(KD):
                dve.wait_ge(x_hi_made, KD * f + k + 1)
                nc.vector.tensor_tensor(XA[:, 1, k, tok], X[:, k, tok], XA[:, 0, k, tok].bitcast(F32), ALU.subtract)\
                  .then_inc(x_lo_made, 1)

        TOK_ROWS = [P, P, L - 2 * P]

        names = """pair_done lora_landed vectors_picked k_padded r_padded v_padded zw_made za_made zg_made
            w_tanh a_tanh decay_made a_made k_squared norm_summed norm_eps norm_rooted norm_inverted kk_made
            cum_made prev_made e_made ei_made em_made ac_made rc_made b_plain bc_made ka_made k2_made kh_made
            bonus_rk_made bd_copied g_ready lt_masked gak_masked grb_masked grk_masked t_first tt_first ttb_first
            v_turned b_turned k_turned vt_copied vtb_masked btb_masked ktb_masked off_made z_ready z_copied
            zbd_masked t_ready tt_ready t_added tt_added ttb_masked rhs_ready rhs_copied u_ready u_copied ubd_masked
            y_ready s_ready s_added s_scaled sbd_masked y_taken gn_mean gn_centred gn_squared gn_var gn_eps gn_rooted
            gn_inverted gn_scaled gn_shifted bonus_ready bonus_scaled bonus_added zeros_set off1_masked ttc_first""".split()
        S = {n: sem(n) for n in names}
        NL = len(LEVELS)

        def flat(t):
            return t[:].rearrange("p c t -> p (c t)")

        def real(t):
            return flat(t)[:, PAD:LP]

        def heads(t, c):
            return t[:, c].rearrange("p h t -> p (h t)")

        def spread(ap):
            return ap.rearrange("p (c o) t -> p c o t", o=1).to_broadcast((P, NCH, 2, CHUNK))

        def masked(name):
            return C[name][:].rearrange("p (o h t) -> p o h t", o=1, h=2).to_broadcast((P, NCH, 2, CHUNK))

        def plain(name):
            return C[name][:].rearrange("p (o t) -> p o t", o=1).to_broadcast((P, NCH, CHUNK))

        def bank(b):
            return PS[:, b, 0:LP].rearrange("p (c t) -> p c t", c=NCH)

        def each_chunk(b, lhs, rhs):
            for c in range(NCH):
                mm = nc.tensor.matmul(bank(b)[:, c], lhs(c), rhs(c), start=True, stop=True)
            return mm

        W0, A0 = NVEC, NVEC + 1

        def scan_sp(sp):
            with sp.Fori(0, KD) as p:
                sp.wait_ge(S["pair_done"], p + 1)
                cols = bass.ds(P * p, P)
                sp.dma_start(LW[0:LORA, 0, :], w["rwkv_w2"][:, cols]).then_inc(S["lora_landed"], 16)
                sp.dma_start(LW[0:LORA, 1, :], w["rwkv_a2"][:, cols]).then_inc(S["lora_landed"], 16)
                sp.dma_start(LW[:, 2:4, :], w["rwkv_g2"].rearrange("(k p) n -> p k n", p=P)[:, :, cols])\
                  .then_inc(S["lora_landed"], 16)

        def scan_act(act):
            A = nc.scalar.activation
            with act.Fori(0, KD) as p:
                act.wait_ge(S["pair_done"], p + 1)
                for n, src, dst in (("k_padded", 0, KP), ("r_padded", 2, RP), ("v_padded", 1, VP)):
                    A(real(dst), KVR[:, src, p, :], ACT.Copy).then_inc(S[n], 1)
                act.wait_ge(S["vectors_picked"], p + 1)
                act.wait_ge(S["zw_made"], p + 1)
                A(real(LWD), PS[:, 4, 0:L], ACT.Tanh, bias=PP[:, W0:W0 + 1], scale=0.5).then_inc(S["w_tanh"], 1)
                act.wait_ge(S["za_made"], p + 1)
                A(real(AA), PS[:, 5, 0:L], ACT.Tanh, bias=PP[:, A0:A0 + 1], scale=0.5).then_inc(S["a_tanh"], 1)
                act.wait_ge(S["k_padded"], p + 1)
                A(flat(SQK), flat(KP), ACT.Square, scale=PP[:, V_KK:V_KK + 1]).then_inc(S["k_squared"], 1)
                act.wait_ge(S["norm_eps"], p + 1)
                A(flat(RN), flat(RN), ACT.Sqrt).then_inc(S["norm_rooted"], 1)
                act.wait_ge(S["cum_made"], p + 1)
                A(flat(E), flat(CUM), ACT.Exp).then_inc(S["e_made"], 1)
                A(flat(EI), flat(CUM), ACT.Exp, scale=-1.0).then_inc(S["ei_made"], 1)
                act.wait_ge(S["prev_made"], p + 1)
                A(flat(CM), flat(CM), ACT.Exp).then_inc(S["em_made"], 1)
                for ready, src, dst in (("v_padded", VP, VBD), ("ac_made", AC, ABD), ("bc_made", BC, BBD),
                                        ("kh_made", KH, KBD)):
                    act.wait_ge(S[ready], p + 1)
                    for h in range(2):
                        rows = slice(HEAD * h, HEAD * (h + 1))
                        A(dst[rows, :, h, :], src[rows], ACT.Copy).then_inc(S["bd_copied"], 1)
                act.wait_ge(S["vtb_masked"], p + 1)
                A(VT[:], bank(5), ACT.Copy).then_inc(S["vt_copied"], 1)
                for l in range(NL):
                    act.wait_ge(S["z_ready"], NL * p + l + 1)
                    A(ZC[:], bank(0), ACT.Copy).then_inc(S["z_copied"], 1)
                for c in range(NCH):
                    act.wait_ge(S["rhs_ready"], NCH * p + c + 1)
                    A(RHS[:], PS[:, 3, 0:CHUNK], ACT.Copy).then_inc(S["rhs_copied"], 1)
                    act.wait_ge(S["u_ready"], NCH * p + c + 1)
                    A(UC[:], PS[:, 4, 0:CHUNK], ACT.Copy).then_inc(S["u_copied"], 1)
                act.wait_ge(S["gn_centred"], p + 1)
                A(YQ, YC[:], ACT.Square).then_inc(S["gn_squared"], 1)
                act.wait_ge(S["gn_eps"], p + 1)
                A(RG, RG, ACT.Sqrt).then_inc(S["gn_rooted"], 1)

        def scan_pool(pool):
            pool.wait_ge(const_landed, 16 * len(CONST_COLUMNS))
            pool.wait_ge(blocks_multiplied, proj_r.end)
            for t in (KP, RP, VP, LWD, AA, ABD, BBD, KBD, VBD):
                nc.gpsimd.memset(t[:], 0.0).then_inc(S["zeros_set"], 1)
            with pool.Fori(0, KD) as p:
                pool.wait_ge(S["lt_masked"], p + 1)
                for l, b in enumerate(LEVELS):
                    pool.wait_ge(S["z_ready"], NL * p + l) if l else None
                    nc.gpsimd.tensor_tensor(OFF[:], LT[:], masked(f"offT{b}"), ALU.mult).then_inc(S["off_made"], 1)

        def scan_pe(pe):
            M = nc.tensor.matmul
            with pe.Fori(0, KD) as p:
                pe.wait_ge(S["pair_done"], p + 1)
                pe.wait_ge(S["lora_landed"], 48 * p + 48)
                M(PS[:, 4, 0:L], LW[0:LORA, 0, :], LH[0:LORA, 0, :], start=True, stop=True).then_inc(S["zw_made"], 1)
                M(PS[:, 5, 0:L], LW[0:LORA, 1, :], LH[0:LORA, 1, :], start=True, stop=True).then_inc(S["za_made"], 1)
                for k in range(2):
                    mm = M(PS[:, 6, 0:SEQ], LW[:, 2 + k, :], LH[:, 2 + k, REAL], start=(k == 0), stop=(k == 1))
                mm.then_inc(S["zg_made"], 1)
                pe.wait_ge(S["k_squared"], p + 1)
                M(PS[:, 7, 0:LP], C["head_sum"][:], flat(SQK), start=True, stop=True).then_inc(S["norm_summed"], 1)
                pe.wait_ge(S["a_made"], p + 1)
                pe.wait_ge(S["bd_copied"], 8 * p + 2)
                each_chunk(5, lambda c: heads(VBD, c), lambda c: C["stack_i"][:]).then_inc(S["v_turned"], 1)
                pe.wait_ge(S["decay_made"], p + 1)
                pe.wait_ge(S["bc_made"], p + 1)
                pe.wait_ge(S["rc_made"], p + 1)
                pe.wait_ge(S["bd_copied"], 8 * p + 4)
                each_chunk(4, lambda c: heads(ABD, c), lambda c: BC[:, c]).then_inc(S["g_ready"], 1)
                pe.wait_ge(S["bd_copied"], 8 * p + 6)
                each_chunk(0, lambda c: heads(BBD, c), lambda c: AC[:, c]).then_inc(S["g_ready"], 1)
                each_chunk(2, lambda c: heads(BBD, c), lambda c: RC[:, c]).then_inc(S["g_ready"], 1)
                pe.wait_ge(S["norm_inverted"], p + 1)
                each_chunk(7, lambda c: heads(BBD, c), lambda c: C["stack_i"][:]).then_inc(S["b_turned"], 1)
                pe.wait_ge(S["bd_copied"], 8 * p + 8)
                each_chunk(1, lambda c: heads(KBD, c), lambda c: AC[:, c]).then_inc(S["g_ready"], 1)
                each_chunk(3, lambda c: heads(KBD, c), lambda c: RC[:, c]).then_inc(S["g_ready"], 1)
                pe.wait_ge(S["t_first"], p + 1)
                each_chunk(4, lambda c: heads(KBD, c), lambda c: C["stack_i"][:]).then_inc(S["k_turned"], 1)
                for l in range(NL):
                    pe.wait_ge(S["off_made"], NL * p + l + 1)
                    if l == 0:
                        pe.wait_ge(S["tt_first"], p + 1)
                        pe.wait_ge(S["ttb_first"], p + 1)
                    else:
                        pe.wait_ge(S["t_added"], (NL - 1) * p + l)
                        pe.wait_ge(S["ttb_masked"], NL * p + l)
                    each_chunk(0, lambda c: heads(OFF, c), lambda c: TC[:, c]).then_inc(S["z_ready"], 1)
                    if l < NL - 1:
                        if l == 0:
                            pe.wait_ge(S["gak_masked"], p + 1)
                        pe.wait_ge(S["z_copied"], NL * p + l + 1)
                        each_chunk(1, lambda c: heads(TTB, c), lambda c: ZC[:, c]).then_inc(S["t_ready"], 1)
                    if l == 0:
                        pe.wait_ge(S["grb_masked"], p + 1)
                    pe.wait_ge(S["zbd_masked"], NL * p + l + 1)
                    each_chunk(2, lambda c: heads(ZBD, c), lambda c: TTC[:, c]).then_inc(S["tt_ready"], 1)
                pe.wait_ge(S["ttb_masked"], NL * p + NL)
                pe.wait_ge(S["vt_copied"], p + 1)
                pe.wait_ge(S["vtb_masked"], p + 1)
                pe.wait_ge(S["btb_masked"], p + 1)
                pe.wait_ge(S["ktb_masked"], p + 1)
                pe.wait_ge(S["grk_masked"], p + 1)
                pe.wait_ge(S["bonus_rk_made"], p + 1)
                M(PS[:, 7, 0:SEQ], C["head_sum"][:], flat(SQK)[:, CHUNK:LP], start=True, stop=True)\
                    .then_inc(S["bonus_ready"], 1)
                for c in range(NCH):
                    if c:
                        pe.wait_ge(S["s_scaled"], (NCH - 1) * p + c)
                        M(PS[:, 3, 0:CHUNK], heads(ABD, c), SC[:], start=True, stop=False)
                    M(PS[:, 3, 0:CHUNK], heads(GAK, c), VT[:, c], start=(c == 0), stop=True).then_inc(S["rhs_ready"], 1)
                    pe.wait_ge(S["rhs_copied"], NCH * p + c + 1)
                    M(PS[:, 4, 0:CHUNK], heads(TTB, c), RHS[:], start=True, stop=True).then_inc(S["u_ready"], 1)
                    if c:
                        y = PS[:, 0, CHUNK * (c - 1):CHUNK * c]
                        pe.wait_ge(S["sbd_masked"], (NCH - 1) * p + c)
                        M(y, SBD[:].rearrange("p h t -> p (h t)"), RC[:, c], start=True, stop=False)
                        M(y, heads(VTB, c), GRK[:, c], start=False, stop=False)
                        pe.wait_ge(S["ubd_masked"], (NCH - 1) * p + c)
                        M(y, UBD[:].rearrange("p h t -> p (h t)"), GRB[:, c], start=False, stop=True)\
                            .then_inc(S["y_ready"], 1)
                    pe.wait_ge(S["u_copied"], NCH * p + c + 1)
                    if c < NCH - 1:
                        M(PS[:, 5, 0:CHUNK], heads(KTB, c), VT[:, c], start=True, stop=False)
                        M(PS[:, 5, 0:CHUNK], heads(BTB, c), UC[:], start=False, stop=True).then_inc(S["s_ready"], 1)
                pe.wait_ge(S["y_taken"], p + 1)
                M(PS[:, 1, 0:SEQ], C["head_mean"][:], YC[:], start=True, stop=True).then_inc(S["gn_mean"], 1)
                pe.wait_ge(S["gn_squared"], p + 1)
                M(PS[:, 2, 0:SEQ], C["head_mean"][:], YQ, start=True, stop=True).then_inc(S["gn_var"], 1)

        def scan_dve(dve):
            TT, TS, STT = nc.vector.tensor_tensor, nc.vector.tensor_scalar, nc.vector.scalar_tensor_tensor
            dve.wait_ge(projected, proj_r.projected0 + KD // 2)
            dve.wait_ge(S["zeros_set"], 9)
            dve.sem_inc(S["pair_done"], 1)

            def pp(v):
                return PP[:, v:v + 1]

            with dve.Fori(0, KD) as p:
                dve.wait_ge(S["pair_done"], p + 1)
                nc.vector.tensor_copy(PP[:, 0:NVEC], PAR[:, :, p])
                nc.vector.tensor_copy(PP[:, NVEC:NVEC + 2], HALF[:, :, p]).then_inc(S["vectors_picked"], 1)
                dve.wait_ge(S["w_tanh"], p + 1)
                TS(real(LWD), real(LWD), -DECAY / 2, -DECAY / 2, ALU.mult, ALU.add).then_inc(S["decay_made"], 1)
                dve.wait_ge(S["decay_made"], p + 1)
                nc.vector.tensor_tensor_scan(flat(CUM), C["restart"][:], flat(LWD), 0.0, ALU.mult, ALU.add)\
                    .then_inc(S["cum_made"], 1)
                dve.wait_ge(S["cum_made"], p + 1)
                TT(flat(CM), flat(CUM), flat(LWD), ALU.subtract).then_inc(S["prev_made"], 1)
                dve.wait_ge(S["a_tanh"], p + 1)
                TS(real(AA), real(AA), 0.5, 0.5, ALU.mult, ALU.add).then_inc(S["a_made"], 1)
                dve.wait_ge(S["norm_summed"], p + 1)
                TS(flat(RN), PS[:, 7, 0:LP], 1e-12, None, ALU.add).then_inc(S["norm_eps"], 1)
                dve.wait_ge(S["a_made"], p + 1)
                dve.wait_ge(S["vectors_picked"], p + 1)
                TS(flat(TH), flat(AA), 1.0, pp(V_KA), ALU.subtract, ALU.mult).then_inc(S["ka_made"], 1)
                dve.wait_ge(S["ka_made"], p + 1)
                dve.wait_ge(S["k_padded"], p + 1)
                STT(out=flat(K2), in0=flat(TH), scalar=1.0, in1=flat(KP), op0=ALU.add, op1=ALU.mult).then_inc(S["k2_made"], 1)
                dve.wait_ge(S["norm_rooted"], p + 1)
                nc.vector.reciprocal(flat(RN), flat(RN)).then_inc(S["norm_inverted"], 1)
                dve.wait_ge(S["norm_inverted"], p + 1)
                STT(out=flat(KK), in0=flat(KP), scalar=pp(V_KK), in1=flat(RN), op0=ALU.mult, op1=ALU.mult).then_inc(S["kk_made"], 1)
                dve.wait_ge(S["kk_made"], p + 1)
                dve.wait_ge(S["em_made"], p + 1)
                STT(out=flat(AC), in0=flat(KK), scalar=-1.0, in1=flat(CM), op0=ALU.mult, op1=ALU.mult).then_inc(S["ac_made"], 1)
                TT(flat(BC), flat(KK), flat(AA), ALU.mult).then_inc(S["b_plain"], 1)
                dve.wait_ge(S["b_plain"], p + 1)
                TT(flat(BC), flat(BC), flat(EI), ALU.mult).then_inc(S["bc_made"], 1)
                dve.wait_ge(S["k2_made"], p + 1)
                TT(flat(KH), flat(K2), flat(EI), ALU.mult).then_inc(S["kh_made"], 1)
                dve.wait_ge(S["r_padded"], p + 1)
                TT(flat(RC), flat(RP), flat(E), ALU.mult).then_inc(S["rc_made"], 1)
                STT(out=flat(SQK), in0=flat(RP), scalar=pp(V_RK), in1=flat(K2), op0=ALU.mult, op1=ALU.mult)\
                    .then_inc(S["bonus_rk_made"], 1)
                dve.wait_ge(S["v_turned"], p + 1)
                TT(VTB[:], spread(bank(5)), masked("bd"), ALU.mult).then_inc(S["vtb_masked"], 1)
                dve.wait_ge(S["g_ready"], 5 * p + 1)
                TT(TC[:], bank(4), plain("off1"), ALU.mult).then_inc(S["t_first"], 1)
                dve.wait_ge(S["g_ready"], 5 * p + 2)
                TT(LT[:], spread(bank(0)), masked("bd_strict"), ALU.mult).then_inc(S["lt_masked"], 1)
                dve.wait_ge(S["t_first"], p + 1)
                TT(TC[:], TC[:], plain("stack_i"), ALU.add).then_inc(S["tt_first"], 1)
                dve.wait_ge(S["lt_masked"], p + 1)
                TT(TTB[:], LT[:], masked("offT1"), ALU.mult).then_inc(S["off1_masked"], 1)
                dve.wait_ge(S["off1_masked"], p + 1)
                TT(TTB[:], TTB[:], masked("bd_i"), ALU.add).then_inc(S["ttb_first"], 1)
                dve.wait_ge(S["ttb_first"], p + 1)
                TT(TTC[:], TTB[:, :, 0, :], TTB[:, :, 1, :], ALU.add).then_inc(S["ttc_first"], 1)
                dve.wait_ge(S["g_ready"], 5 * p + 3)
                TT(GRB[:], bank(2), plain("incl"), ALU.mult).then_inc(S["grb_masked"], 1)
                dve.wait_ge(S["b_turned"], p + 1)
                TT(BTB[:], spread(bank(7)), masked("bd"), ALU.mult).then_inc(S["btb_masked"], 1)
                dve.wait_ge(S["g_ready"], 5 * p + 4)
                TT(GAK[:], spread(bank(1)), masked("bd_strict"), ALU.mult).then_inc(S["gak_masked"], 1)
                for l in range(NL):
                    dve.wait_ge(S["z_copied"], NL * p + l + 1)
                    TT(ZBD[:], spread(ZC[:]), masked("bd"), ALU.mult).then_inc(S["zbd_masked"], 1)
                    if l == 0:
                        dve.wait_ge(S["g_ready"], 5 * p + 5)
                        TT(GRK[:], bank(3), plain("incl"), ALU.mult).then_inc(S["grk_masked"], 1)
                        dve.wait_ge(S["k_turned"], p + 1)
                        TT(KTB[:], spread(bank(4)), masked("bd"), ALU.mult).then_inc(S["ktb_masked"], 1)
                        dve.wait_ge(S["ttc_first"], p + 1)
                    if l < NL - 1:
                        dve.wait_ge(S["t_ready"], (NL - 1) * p + l + 1)
                        TT(TC[:], TC[:], bank(1), ALU.add).then_inc(S["t_added"], 1)
                    dve.wait_ge(S["tt_ready"], NL * p + l + 1)
                    TT(TTC[:], TTC[:], bank(2), ALU.add).then_inc(S["tt_added"], 1)
                    dve.wait_ge(S["tt_added"], NL * p + l + 1)
                    TT(TTB[:], spread(TTC[:]), masked("bd"), ALU.mult).then_inc(S["ttb_masked"], 1)
                for c in range(NCH):
                    dve.wait_ge(S["u_copied"], NCH * p + c + 1)
                    if c:
                        dve.wait_ge(S["y_ready"], (NCH - 1) * p + c - 1) if c > 1 else None
                        TT(UBD[:], UC[:].rearrange("p (o t) -> p o t", o=1).to_broadcast((P, 2, CHUNK)),
                           C["bd"][:].rearrange("p (h t) -> p h t", h=2), ALU.mult).then_inc(S["ubd_masked"], 1)
                    if c < NCH - 1:
                        dve.wait_ge(S["s_ready"], (NCH - 1) * p + c + 1)
                        end = E[:, c, CHUNK - 1:CHUNK]
                        if c:
                            dve.wait_ge(S["sbd_masked"], (NCH - 1) * p + c)
                            TT(ST[:], SC[:], PS[:, 5, 0:CHUNK], ALU.add).then_inc(S["s_added"], 1)
                        else:
                            nc.vector.tensor_copy(ST[:], PS[:, 5, 0:CHUNK]).then_inc(S["s_added"], 1)
                        dve.wait_ge(S["s_added"], (NCH - 1) * p + c + 1)
                        TS(SC[:], ST[:], end, None, ALU.mult).then_inc(S["s_scaled"], 1)
                        if c:
                            dve.wait_ge(S["y_ready"], (NCH - 1) * p + c)
                        STT(out=SBD[:], in0=ST[:].rearrange("p (o t) -> p o t", o=1).to_broadcast((P, 2, CHUNK)),
                            scalar=end, in1=C["bd"][:].rearrange("p (h t) -> p h t", h=2),
                            op0=ALU.mult, op1=ALU.mult).then_inc(S["sbd_masked"], 1)
                dve.wait_ge(S["y_ready"], (NCH - 1) * (p + 1))
                nc.vector.tensor_copy(YC[:], PS[:, 0, 0:SEQ]).then_inc(S["y_taken"], 1)
                dve.wait_ge(S["gn_mean"], p + 1)
                TT(YC[:], YC[:], PS[:, 1, 0:SEQ], ALU.subtract).then_inc(S["gn_centred"], 1)
                dve.wait_ge(S["gn_var"], p + 1)
                TS(RG, PS[:, 2, 0:SEQ], GN_EPS, None, ALU.add).then_inc(S["gn_eps"], 1)
                dve.wait_ge(S["bonus_ready"], p + 1)
                bonus = flat(TH)[:, 0:SEQ]
                TT(bonus, flat(VP)[:, CHUNK:LP], PS[:, 7, 0:SEQ], ALU.mult).then_inc(S["bonus_scaled"], 1)
                dve.wait_ge(S["gn_rooted"], p + 1)
                nc.vector.reciprocal(RG, RG).then_inc(S["gn_inverted"], 1)
                dve.wait_ge(S["gn_inverted"], p + 1)
                STT(out=YC[:], in0=YC[:], scalar=pp(V_GN_G), in1=RG, op0=ALU.mult, op1=ALU.mult).then_inc(S["gn_scaled"], 1)
                dve.wait_ge(S["gn_scaled"], p + 1)
                dve.wait_ge(S["bonus_scaled"], p + 1)
                STT(out=YC[:], in0=YC[:], scalar=pp(V_GN_B), in1=bonus, op0=ALU.add, op1=ALU.add).then_inc(S["bonus_added"], 1)
                dve.wait_ge(S["bonus_added"], p + 1)
                dve.wait_ge(S["zg_made"], p + 1)
                TT(KVR[:, 2, p, REAL], YC[:], PS[:, 6, 0:SEQ], ALU.mult).then_inc(S["pair_done"], 1)

        with nc.Block() as block:
            @block.sync
            def _(sp):
                tokens = [(TOKS[0:N_META, 0], meta), (TOKS[N_META:P, 0], x[0:P - N_META]),
                          (TOKS[:, 1], x[P - N_META:2 * P - N_META]),
                          (TOKS[0:L - 2 * P, 2], x[2 * P - N_META:SEQ])]
                for dst, src in tokens:
                    sp.dma_start(dst, src).then_inc(tokens_landed, 16)
                for name in const:
                    sp.dma_start(C[name][:], const[name]).then_inc(const_landed, 16)
                row = 0
                for v in vec:
                    for n in range(v.shape[0]):
                        r = row + n
                        sp.dma_start(VROWS[KD * (r % 8):KD * (r % 8) + KD, r // 8, :],
                                     v[n].rearrange("(k p) -> k p", p=P)).then_inc(vectors_landed, 16)
                    row += v.shape[0]
                for ph in phases[:-3]:
                    load_blocks(sp, ph)
                scan_sp(sp)
                for ph in phases[-3:]:
                    load_blocks(sp, ph)
                for i in range(2):
                    sp.wait_ge(out_copied, 4 * (i + 1))
                    sp.dma_start(out[P * i:P * (i + 1)], OUT[:, i]).then_inc(out_stored, 16)
                sp.wait_ge(out_stored, 32)

            @block.gpsimd
            def _(pool):
                scan_pool(pool)

            @block.scalar
            def _(act):
                for i in range(12):
                    kg, tt = i // 3, i % 3
                    rows = TOK_ROWS[tt]
                    act.wait_ge(turned, i + 1)
                    nc.scalar.activation(X[:, 4 * kg:4 * kg + 4, P * tt:P * tt + rows],
                                         PS[:, i % 2].rearrange("p (k t) -> p k t", k=4)[:, :, 0:rows], ACT.Copy)\
                      .then_inc(turned_copied, 1)
                split_x_act(act, 0, ALL)
                with_epilogues(act, in0, split_hi, epilogue_act)
                with_epilogues(act, out0, split_hi, epilogue_act)
                ln_act(act, 0, ALL)
                for v in (0, 1):
                    for k in range(KD):
                        mix_act(act, v, k)
                with_epilogues(act, lora_w, split_hi, epilogue_act)
                with_epilogues(act, lora_a, split_hi, epilogue_act)
                for k in range(KD):
                    mix_act(act, 2, k)
                with_epilogues(act, lora_g, split_hi, epilogue_act)
                for k in range(KD):
                    mix_act(act, 3, k)
                for ph in (proj_k, proj_v, proj_r):
                    with_epilogues(act, ph, split_hi, epilogue_act, side=mix_act)
                scan_act(act)
                act.wait_ge(S["pair_done"], KD + 1)
                for k in range(KD):
                    nc.scalar.activation(YA[:, 0, k], KVR[:, 2, k, REAL], ACT.Copy).then_inc(y_hi_made, 1)
                with_epilogues(act, w_o, split_hi, epilogue_act)
                ln_act(act, 1, REAL)
                split_x_act(act, 1, REAL)
                with_epilogues(act, in1, split_hi, epilogue_act)
                with_epilogues(act, out1, split_hi, epilogue_act)
                ln_act(act, 2, REAL)
                for i in range(8):
                    tt, kg = i // 4, i % 4
                    act.wait_ge(out_turned, i + 1)
                    nc.scalar.activation(OUT[:, tt, 4 * P * kg:4 * P * (kg + 1)], PS[:, 6 + i % 2], ACT.Copy)\
                      .then_inc(out_copied, 1)

            @block.vector
            def _(dve):
                dve.wait_ge(turned, 13)
                nc.vector.tensor_copy(PAR[:].rearrange("p v k -> p (v k)"), PS[:, 2, 0:NVEC * KD])\
                  .then_inc(params_copied, 1)
                dve.wait_ge(params_copied, 1)
                nc.vector.tensor_scalar(HALF[:], PAR[:, V_W0:V_W0 + 2], 0.5, None, ALU.mult).then_inc(params_halved, 1)
                split_x_dve(dve, 0, ALL)
                with_epilogues(dve, in0, split_lo, epilogue_dve, late=split_hidden)
                with_epilogues(dve, out0, split_lo, epilogue_dve)
                ln_dve(dve, 0, ALL)
                dve.wait_ge(ln_shifted, KD)
                nc.vector.tensor_tensor(XX[:, :, 1:L], X[:, :, 0:L - 1], X[:, :, 1:L], ALU.subtract).then_inc(xx_made, 1)
                nc.vector.tensor_scalar(XX[:, :, 0:1], X[:, :, 0:1], -1.0, None, ALU.mult).then_inc(xx_made, 1)
                dve.wait_ge(xx_made, 2)
                for v in (0, 1):
                    for k in range(KD):
                        mix_dve(dve, v, k)
                with_epilogues(dve, lora_w, split_lo, epilogue_dve)
                with_epilogues(dve, lora_a, split_lo, epilogue_dve)
                for k in range(KD):
                    mix_dve(dve, 2, k)
                with_epilogues(dve, lora_g, split_lo, epilogue_dve)
                for k in range(KD):
                    mix_dve(dve, 3, k)
                for ph in (proj_k, proj_v, proj_r):
                    with_epilogues(dve, ph, split_lo, epilogue_dve, side=mix_dve)
                scan_dve(dve)
                for k in range(KD):
                    dve.wait_ge(y_hi_made, k + 1)
                    nc.vector.tensor_tensor(YA[:, 1, k], KVR[:, 2, k, REAL], YA[:, 0, k].bitcast(F32), ALU.subtract)\
                      .then_inc(y_lo_made, 1)
                with_epilogues(dve, w_o, split_lo, epilogue_dve)
                ln_dve(dve, 1, REAL)
                split_x_dve(dve, 1, REAL)
                with_epilogues(dve, in1, split_lo, epilogue_dve, late=split_hidden)
                with_epilogues(dve, out1, split_lo, epilogue_dve)
                ln_dve(dve, 2, REAL)

            @block.tensor
            def _(pe):
                pe.wait_ge(const_landed, 16 * len(const))
                pe.wait_ge(tokens_landed, 64)
                for i in range(12):
                    kg, tt = i // 3, i % 3
                    rows = TOK_ROWS[tt]
                    if i >= 2:
                        pe.wait_ge(turned_copied, i - 1)
                    for k in range(4):
                        mm = nc.tensor.transpose(PS[:, i % 2, P * k:P * k + rows],
                                                 TOKS[0:rows, tt, P * (4 * kg + k):P * (4 * kg + k + 1)],
                                                 C["ident"][0:rows, 0:rows])
                    mm.then_inc(turned, 1)
                pe.wait_ge(vectors_landed, 16 * NVEC)
                for r in range(3):
                    rows = min(P, KD * NVEC - P * r)
                    mm = nc.tensor.transpose(PS[:, 2, P * r:P * r + rows], VROWS[0:rows, r, :],
                                             C["ident"][0:rows, 0:rows])
                mm.then_inc(turned, 1)
                pe.wait_ge(params_copied, 1)
                for ph in (in0, out0):
                    multiply(pe, ph)
                ln_pe(pe, 0, ALL)
                for ph in (lora_w, lora_a, lora_g, proj_k, proj_v, proj_r):
                    multiply(pe, ph)
                scan_pe(pe)
                multiply(pe, w_o)
                ln_pe(pe, 1, REAL)
                for ph in (in1, out1):
                    multiply(pe, ph)
                ln_pe(pe, 2, REAL)
                for i in range(8):
                    tt, kg = i // 4, i % 4
                    pe.wait_ge(ln_shifted, 2 * KD + 4 * kg + 4)
                    if i >= 2:
                        pe.wait_ge(out_copied, i - 1)
                    for k in range(4):
                        at_ = N_META + P * tt
                        mm = nc.tensor.transpose(PS[:, 6 + i % 2, P * k:P * (k + 1)], X[:, 4 * kg + k, at_:at_ + P],
                                                 C["ident"][:])
                    mm.then_inc(out_turned, 1)


CONST_COLUMNS = {k: a.shape[1] for k, a in constants().items()}


def kernel(x, meta_tokens, ln_g, ln_b, ffn_in, ffn_out, **more):
    import concourse.bacc as bacc
    from concourse.bass_utils import run_bass_kernel_spmd

    nc = bacc.Bacc("TRN2", target_bir_lowering=False, num_devices=1)
    arrays = {"x": x[0], "meta_tokens": meta_tokens, "ln_g": ln_g[0], "ln_b": ln_b[0],
              "ffn_in": ffn_in[0], "ffn_out": ffn_out[0]}
    for name in ("rwkv_w_rkv", "rwkv_w1", "rwkv_w2", "rwkv_a1", "rwkv_a2", "rwkv_g1", "rwkv_g2", "rwkv_w_o"):
        arrays[name] = more[name]
    for name in VECTORS[2:]:
        arrays[name] = more[name].reshape(-1, D)
    arrays = {n: np.ascontiguousarray(a) for n, a in arrays.items()}
    arrays |= {"c_" + n: a for n, a in constants().items()}
    aps = {n: nc.dram_tensor("in_" + n, a.shape, F32, kind="ExternalInput").ap() for n, a in arrays.items()}
    out = nc.dram_tensor("out", (SEQ, D), F32, kind="ExternalOutput").ap()
    rwkv_layer(nc, aps["x"], aps["meta_tokens"], aps, [aps[n] for n in VECTORS],
               {n[2:]: a for n, a in aps.items() if n.startswith("c_")}, out)
    result = run_bass_kernel_spmd(nc, [{"in_" + n: a for n, a in arrays.items()}], core_ids=[0])
    return result.results[0]["out"].reshape(1, SEQ, D)
```

```python
from contextlib import ExitStack
from math import exp

import numpy as np
import concourse.bass as bass
from concourse import mybir

F32 = mybir.dt.float32
F32R = mybir.dt.float32r
ALU = mybir.AluOpType
ACT = mybir.ActivationFunctionType

P = 128
D = 2048
D_FF = 5632
SEQ = 256
N_META = 16
L = SEQ + N_META
KD = D // P
KF = D_FF // P
HEAD = 64
CHUNK = 64
PAD = CHUNK - N_META
NCH = (L + PAD) // CHUNK
LP = NCH * CHUNK
LORA = 96
GATE = 256
ALPHA = 2.0 ** 0.25
LN_EPS = 1e-5
GN_EPS = 64e-5
DECAY = exp(-0.5)

RING = 4
KB = 4
WIDE = 256
LEVELS = [2, 4, 8, 16, 32]

VECTORS = ["ln_g", "ln_b", "rwkv_mix", "rwkv_w0", "rwkv_a0", "rwkv_k_k", "rwkv_k_a", "rwkv_r_k",
           "rwkv_gn_g", "rwkv_gn_b"]
V_LN_G, V_LN_B, V_MIX, V_W0, V_A0, V_KK, V_KA, V_RK, V_GN_G, V_GN_B = 0, 3, 6, 12, 13, 14, 15, 16, 17, 18
NVEC = 19


def constants():
    p = np.arange(P)
    head, s = p // CHUNK, p % CHUNK
    t = np.arange(CHUNK)
    same = (head[:, None] == np.arange(2)[None, :]).astype(np.float32)[:, :, None]
    c = {
        "ident": np.eye(P),
        "ones_mean": np.full((P, P), 1.0 / D),
        "head_sum": head[:, None] == head[None, :],
        "head_mean": (head[:, None] == head[None, :]) / HEAD,
        "bd": same * np.ones((1, 1, CHUNK)),
        "bd_strict": same * (s[:, None] < t[None, :])[:, None, :],
        "incl": s[:, None] <= t[None, :],
        "bd_i": same * (s[:, None] == t[None, :])[:, None, :],
        "restart": np.broadcast_to(np.arange(LP) % CHUNK != 0, (P, LP)),
    }
    for b in [1] + LEVELS:
        up = (s[:, None] // (2 * b) == t[None, :] // (2 * b)) & (s[:, None] // b < t[None, :] // b)
        if b == 1:
            c["offT1"] = same * up[:, None, :]
        low = (s[:, None] // (2 * b) == t[None, :] // (2 * b)) & (s[:, None] // b > t[None, :] // b)
        c[f"off{b}"] = same * low[:, None, :]
    return {k: np.ascontiguousarray(np.asarray(v, np.float32).reshape(P, -1)) for k, v in c.items()}


class Group:

    def __init__(self, weight, column, step, width=WIDE):
        self.weight, self.column, self.step, self.width = weight, column, step, width


class Phase:

    def __init__(self, name, steps, nb, groups, rhs, tok, ready, side=None):
        self.name, self.steps, self.nb, self.groups = name, steps, nb, groups
        self.rhs, self.tok, self.ready, self.side = rhs, tok, ready, side
        self.n = tok.stop - tok.start
        self.kind = name.rstrip("01")


def number(phases):
    block, uses = 0, [0] * RING
    count = {"staged": 0, "pairs": 0, "added": 0, "projected": 0}
    for ph in phases:
        ph.block0, ph.uses0 = block, list(uses)
        ph.staged0, ph.pairs0 = count["staged"], count["pairs"]
        ph.added0, ph.projected0 = count["added"], count["projected"]
        ph.blocks = ph.nb * len(ph.groups)
        ph.per_group = [len(range(s, ph.nb, RING)) for s in range(RING)]
        block += ph.steps * ph.blocks
        for s in range(RING):
            uses[s] += ph.steps * len(ph.groups) * ph.per_group[s]
        n = ph.steps * len(ph.groups)
        if ph.kind == "in":
            count["staged"] += ph.steps
            count["pairs"] += ph.steps
        elif ph.kind in ("out", "w_o"):
            count["staged"] += n
            count["added"] += n
        else:
            count["projected"] += n
        ph.end = block


def wait(eng, sem, value):
    if not isinstance(value, int) or value > 0:
        eng.wait_ge(sem, value)


def rwkv_layer(nc, x, meta, w, vec, const, out):
    with ExitStack() as ctx:
        def sem(name):
            return ctx.enter_context(nc.semaphore(name))

        XBYTES = KD * L * 4
        ARENA = 2 * (KD + KF) * L * 4
        start = (nc.sbuf_base + 31) // 32 * 32
        fixed = [start]

        def sb(name, shape, dt=F32):
            n = int(np.prod(shape[1:])) * 4
            t = nc.alloc_sbuf_tensor_at(name, shape, dt, offset=fixed[0])
            fixed[0] += (n + 31) // 32 * 32
            return t

        X = sb("X", [P, KD, L])
        RAW = sb("RAW", [P, RING, KB, WIDE])
        rings0 = fixed[0]
        WH = sb("WH", [P, RING, KB, WIDE], F32R)
        WL = sb("WL", [P, RING, KB, WIDE], F32R)
        C = {k: sb("c_" + k, [P, n]) for k, n in CONST_COLUMNS.items()}
        PAR = sb("PAR", [P, NVEC, KD])
        HALF = sb("HALF", [P, 2, KD])
        STAGE = sb("STAGE", [P, 2, L])
        HV = sb("HV", [P, 2, L])
        RS = sb("RS", [P, L])
        at0 = fixed[0]
        assert at0 + ARENA <= nc.sbuf_usable_end, (at0 + ARENA, nc.sbuf_usable_end)

        def at(name, shape, offset, dt=F32):
            n = int(np.prod(shape[1:])) * 4
            assert offset + n <= ARENA, (name, offset, n)
            return nc.alloc_sbuf_tensor_at(name, shape, dt, offset=at0 + offset)

        XA = at("XA", [P, 2, KD, L], 0, F32R)
        H = at("H", [P, 2, KF, L], 2 * XBYTES, F32R)
        TOKS = at("TOKS", [P, 3, D], 2 * XBYTES)
        VROWS = at("VROWS", [P, 3, P], 2 * XBYTES + 12 * D)
        SQ = at("SQ", [P, KD, L], 2 * XBYTES)
        OUT = at("OUT", [P, 2, D], 2 * XBYTES)
        XS = at("XS", [P, 2, 2, KD, L], 0, F32R)
        KVR = at("KVR", [P, 3, KD, L], 4 * XBYTES)
        XX = KVR[:, 2]
        LH = at("LH", [P, 4, L], 7 * XBYTES)
        XT = at("XT", [P, L], 7 * XBYTES + 16 * L)
        YA = at("YA", [P, 2, KD, SEQ], 0, F32R)
        PS = ctx.enter_context(nc.psum_tensor("PS", [P, 8, 512], F32))

        cursor = [0]

        def tmp(name, *shape):
            t = at(name, [P, *shape], cursor[0])
            cursor[0] += -(-int(np.prod(shape)) * 4 // 32) * 32
            assert cursor[0] <= 4 * XBYTES, (name, cursor[0])
            return t

        def tmp2(name, *shape):
            t = nc.alloc_sbuf_tensor_at(name, [P, *shape], F32, offset=rings0 + cursor[0])
            cursor[0] += -(-int(np.prod(shape)) * 4 // 32) * 32
            assert cursor[0] <= 2 * RING * KB * WIDE * 4, name
            return t

        CC, BD = (NCH, CHUNK), (NCH, 2, CHUNK)
        LANES = (0, 1)

        def lanes(alloc, name, *shape):
            return [alloc(f"{name}{q}", *shape) for q in LANES]

        LWD, AA, TH = (lanes(tmp, n, *CC) for n in ("LWD", "AA", "TH"))
        SQK, KK, CUM = (lanes(tmp, n, *CC) for n in ("SQK", "KK", "CUM"))
        EI, K2 = lanes(tmp, "EI", *CC), lanes(tmp, "K2", *CC)
        E = lanes(tmp, "E", NCH, CHUNK + 1)
        AR = lanes(tmp, "AR", *BD)
        ABD, BBD, KBD, VBD = (lanes(tmp, n, *BD) for n in ("ABD", "BBD", "KBD", "VBD"))
        BT, KT, VT = (lanes(tmp, n, *BD) for n in ("BT", "KT", "VT"))
        ZZ, TI, TT = VBD, BBD, KBD
        cursor[0] = 0
        LT, GAK = lanes(tmp2, "LT", *BD), lanes(tmp2, "GAK", *BD)
        GR = lanes(tmp2, "GR", NCH, 3, CHUNK)
        SS, SW = lanes(tmp2, "SS", 2, CHUNK), lanes(tmp2, "SW", 2, CHUNK)
        RHS, UU = lanes(tmp2, "RHS", 2, CHUNK), lanes(tmp2, "UU", 2, CHUNK)
        GG = lanes(tmp2, "GG", SEQ)
        LW = tmp2("LW", 4, 2 * P)
        PP = lanes(tmp2, "PP", NVEC + 2)
        RN = LWD
        YC, YQ, RG, BN = ([t[q][:].rearrange("p c t -> p (c t)")[:, CHUNK:] for q in LANES]
                          for t in (KK, SQK, AA, TH))

        const_landed, tokens_landed, vectors_landed = sem("const_landed"), sem("tokens_landed"), sem("vectors_landed")
        raw_landed = [sem(f"raw_landed{s}") for s in range(RING)]
        hi_made, lo_made, blocks_multiplied = sem("hi_made"), sem("lo_made"), sem("blocks_multiplied")
        stage_filled, residual_added, projected = sem("stage_filled"), sem("residual_added"), sem("projected")
        hv_made, h_hi_made, h_lo_made = sem("hv_made"), sem("h_hi_made"), sem("h_lo_made")
        x_hi_made, x_lo_made = sem("x_hi_made"), sem("x_lo_made")
        turned, turned_copied, params_copied, params_halved = (
            sem("turned"), sem("turned_copied"), sem("params_copied"), sem("params_halved"))
        ln_mean, ln_centred, ln_squared, ln_var = sem("ln_mean"), sem("ln_centred"), sem("ln_squared"), sem("ln_var")
        ln_eps_added, ln_rooted, ln_inverted = sem("ln_eps_added"), sem("ln_rooted"), sem("ln_inverted")
        ln_scaled, ln_shifted = sem("ln_scaled"), sem("ln_shifted")
        xx_made, mix_made, mix_hi_made, mix_lo_made = sem("xx_made"), sem("mix_made"), sem("mix_hi_made"), sem("mix_lo_made")
        y_hi_made, y_lo_made = sem("y_hi_made"), sem("y_lo_made")
        out_turned, out_copied, out_stored = sem("out_turned"), sem("out_copied"), sem("out_stored")

        ALL, REAL = slice(0, L), slice(N_META, L)

        def ffn(f, tok):
            win, wout = w["ffn_in"][f], w["ffn_out"][f]
            return [
                Phase(f"in{f}", KF // 2, KD // KB, [Group(win, 0, WIDE), Group(win, D_FF, WIDE)],
                      lambda h, k: XA[:, h, k, tok], tok, lambda j: (x_lo_made, KD * f + KB * (j + 1))),
                Phase(f"out{f}", KD // 4, KF // KB, [Group(wout, 0, 2 * WIDE), Group(wout, WIDE, 2 * WIDE)],
                      lambda h, k: H[:, h, k, tok], tok, lambda j: (h_lo_made, KF // 2 * f + KB // 2 * (j + 1)))]

        def mixed(buf):
            return lambda h, k: XS[:, buf, h, k, :]

        def mix_ready(v):
            return lambda j: (mix_lo_made, KD * v + KB * (j + 1))

        def square(name, weight, rhs, tok, ready, side=None):
            return Phase(name, KD // 4, KD // KB, [Group(weight, 0, 2 * WIDE), Group(weight, WIDE, 2 * WIDE)],
                         rhs, tok, ready, side)

        MIXES = [3, 4, 5, 1, 2, 0]
        wkv = w["rwkv_w_rkv"]
        in0, out0 = ffn(0, ALL)
        lora_w = Phase("lora_w", 1, KD // KB, [Group(w["rwkv_w1"], 0, 0, LORA)], mixed(0), ALL, mix_ready(0))
        lora_a = Phase("lora_a", 1, KD // KB, [Group(w["rwkv_a1"], 0, 0, LORA)], mixed(1), ALL, mix_ready(1))
        lora_g = Phase("lora_g", 1, KD // KB, [Group(w["rwkv_g1"], 0, 0, GATE)], mixed(0), ALL, mix_ready(2))
        proj_k = square("k", wkv[1], mixed(1), ALL, mix_ready(3), side=4)
        proj_v = square("v", wkv[2], mixed(0), ALL, mix_ready(4), side=5)
        proj_r = square("r", wkv[0], mixed(1), ALL, mix_ready(5))
        w_o = square("w_o", w["rwkv_w_o"], lambda h, k: YA[:, h, k, :], REAL, lambda j: (y_lo_made, KB * (j + 1)))
        in1, out1 = ffn(1, REAL)
        phases = [in0, out0, lora_w, lora_a, lora_g, proj_k, proj_v, proj_r, w_o, in1, out1]
        number(phases)
        mix_free = {2: lora_w, 3: lora_a, 4: lora_g, 5: proj_k}
        SLOT = {"k": 0, "v": 1, "r": 2}

        def loop(eng, ph, body):
            body(0, True)
            if ph.steps > 1:
                with eng.Fori(1, ph.steps) as t:
                    body(t, False)

        def block_of(ph, t, g, j):
            return ph.block0 + t * ph.blocks + g * ph.nb + j

        def load_blocks(sp, ph):
            def body(t, first):
                for g, grp in enumerate(ph.groups):
                    for j in range(ph.nb):
                        slot = j % RING
                        wait(sp, lo_made, block_of(ph, t, g, j) - 2)
                        rows = grp.weight[j * KB * P:(j + 1) * KB * P, :].rearrange("(k p) n -> p k n", p=P)
                        sp.dma_start(RAW[:, slot, :, 0:grp.width],
                                     rows[:, :, bass.ds(grp.column + t * grp.step, grp.width)])\
                          .then_inc(raw_landed[slot], 16)
            loop(sp, ph, body)

        def split_hi(act, ph, t, g, j):
            slot, width = j % RING, ph.groups[g].width
            use = ph.uses0[slot] + (t * len(ph.groups) + g) * ph.per_group[slot] + j // RING
            act.wait_ge(raw_landed[slot], 16 * use + 16)
            wait(act, blocks_multiplied, block_of(ph, t, g, j) - 2)
            nc.scalar.activation(WH[:, slot, :, 0:width], RAW[:, slot, :, 0:width], ACT.Copy).then_inc(hi_made, 1)

        def split_lo(dve, ph, t, g, j):
            slot, width = j % RING, ph.groups[g].width
            dve.wait_ge(hi_made, block_of(ph, t, g, j) + 1)
            wait(dve, blocks_multiplied, block_of(ph, t, g, j) - 2)
            nc.vector.tensor_tensor(WL[:, slot, :, 0:width], RAW[:, slot, :, 0:width],
                                    WH[:, slot, :, 0:width].bitcast(F32), ALU.subtract).then_inc(lo_made, 1)

        def wait_for_banks(pe, ph, t, g):
            turn = 2 * t + g - 1
            if isinstance(turn, int):
                turn = max(turn, 0)
            if ph.kind == "in":
                if g == 0:
                    wait(pe, stage_filled, ph.staged0 + t)
                else:
                    wait(pe, hv_made, ph.pairs0 + t)
            elif ph.kind in ("out", "w_o"):
                wait(pe, stage_filled, ph.staged0 + turn)
            else:
                wait(pe, projected, ph.projected0 + turn)

        def multiply(pe, ph):
            def body(t, first):
                for g, grp in enumerate(ph.groups):
                    wait_for_banks(pe, ph, t, g)
                    for j in range(ph.nb):
                        slot = j % RING
                        if first and g == 0:
                            pe.wait_ge(*ph.ready(j))
                        pe.wait_ge(lo_made, block_of(ph, t, g, j) + 1)
                        for m in range(0, grp.width, P):
                            mw = min(P, grp.width - m)
                            o = PS[0:mw, 2 * g + m // P, 0:ph.n]
                            for k in range(KB):
                                kk = j * KB + k
                                hi, lo = WH[:, slot, k, m:m + mw], WL[:, slot, k, m:m + mw]
                                nc.tensor.matmul(o, hi, ph.rhs(0, kk), start=(kk == 0), stop=False)
                                nc.tensor.matmul(o, hi, ph.rhs(1, kk), start=False, stop=False)
                                mm = nc.tensor.matmul(o, lo, ph.rhs(0, kk), start=False,
                                                      stop=(kk == ph.nb * KB - 1))
                        mm.then_inc(blocks_multiplied, 1)
            loop(pe, ph, body)

        def epilogue_act(act, ph, t, g):
            ps = PS[:, 2 * g:2 * g + 2, 0:ph.n]
            if ph.kind == "in" and g == 1:
                act.wait_ge(hv_made, ph.pairs0 + t + 1)
                nc.scalar.activation(H[:, 0, bass.ds(2 * t, 2), ph.tok], HV[:, :, 0:ph.n], ACT.Copy)\
                  .then_inc(h_hi_made, 1)
                return
            act.wait_ge(blocks_multiplied, block_of(ph, t, g, ph.nb))
            if ph.kind == "in":
                wait(act, hv_made, ph.pairs0 + t)
                nc.scalar.activation(STAGE[:, :, 0:ph.n], ps, ACT.Silu).then_inc(stage_filled, 1)
            elif ph.kind in ("out", "w_o"):
                wait(act, residual_added, ph.added0 + 2 * t + g)
                nc.scalar.activation(STAGE[:, :, 0:ph.n], ps, ACT.Copy, scale=0.5 if ph.kind == "out" else 1.0)\
                  .then_inc(stage_filled, 1)
            elif ph.kind == "lora_w":
                nc.scalar.activation(LH[0:LORA, 0, :], PS[0:LORA, 0, 0:L], ACT.Tanh).then_inc(projected, 1)
            elif ph.kind == "lora_a":
                nc.scalar.activation(LH[0:LORA, 1, :], PS[0:LORA, 0, 0:L], ACT.Copy).then_inc(projected, 1)
            elif ph.kind == "lora_g":
                nc.scalar.activation(LH[:, 2:4, :], ps, ACT.Sigmoid).then_inc(projected, 1)
            else:
                nc.scalar.activation(KVR[:, SLOT[ph.kind], bass.ds(4 * t + 2 * g, 2), :], ps, ACT.Copy)\
                  .then_inc(projected, 1)

        def epilogue_dve(dve, ph, t, g):
            if ph.kind == "in" and g == 1:
                dve.wait_ge(blocks_multiplied, block_of(ph, t, g, ph.nb))
                dve.wait_ge(stage_filled, ph.staged0 + t + 1)
                wait(dve, h_lo_made, ph.pairs0 + t)
                nc.vector.tensor_tensor(HV[:, :, 0:ph.n], STAGE[:, :, 0:ph.n],
                                        PS[:, 2:4, 0:ph.n], ALU.mult).then_inc(hv_made, 1)
            elif ph.kind in ("out", "w_o"):
                dve.wait_ge(stage_filled, ph.staged0 + 2 * t + g + 1)
                xt = X[:, bass.ds(4 * t + 2 * g, 2), ph.tok]
                nc.vector.scalar_tensor_tensor(out=xt, in0=xt, scalar=ALPHA, in1=STAGE[:, :, 0:ph.n],
                                               op0=ALU.mult, op1=ALU.add).then_inc(residual_added, 1)

        def split_hidden(dve, ph, t):
            dve.wait_ge(h_hi_made, ph.pairs0 + t + 1)
            to = bass.ds(2 * t, 2)
            nc.vector.tensor_tensor(H[:, 1, to, ph.tok], HV[:, :, 0:ph.n], H[:, 0, to, ph.tok].bitcast(F32),
                                    ALU.subtract).then_inc(h_lo_made, 1)

        def with_epilogues(eng, ph, split, epilogue, late=None, side=None):
            last = len(ph.groups) - 1

            def body(t, first):
                for g in range(last + 1):
                    for j in range(ph.nb):
                        split(eng, ph, t, g, j)
                        before = not first or g > 0
                        if j == 1 and before:
                            epilogue(eng, ph, t if g else t - 1, g - 1 if g else last)
                        if j == 2 and before and late and g == 0:
                            late(eng, ph, t - 1)
                        if side and ph.side is not None and j % 2:
                            side(eng, ph.side, 4 * t + 2 * g + j // 2)
            loop(eng, ph, body)
            epilogue(eng, ph, ph.steps - 1, last)
            if late:
                late(eng, ph, ph.steps - 1)

        def mix_dve(dve, v, k):
            if v in mix_free:
                dve.wait_ge(blocks_multiplied, mix_free[v].end)
            wait(dve, mix_lo_made, KD * v + k)
            nc.vector.scalar_tensor_tensor(out=XT[:], in0=XX[:, k, :], scalar=PAR[:, V_MIX + MIXES[v], ds1(k)],
                                           in1=X[:, k, :], op0=ALU.mult, op1=ALU.add).then_inc(mix_made, 1)
            dve.wait_ge(mix_hi_made, KD * v + k + 1)
            nc.vector.tensor_tensor(XS[:, v % 2, 1, k, :], XT[:], XS[:, v % 2, 0, k, :].bitcast(F32),
                                    ALU.subtract).then_inc(mix_lo_made, 1)

        def mix_act(act, v, k):
            act.wait_ge(mix_made, KD * v + k + 1)
            nc.scalar.activation(XS[:, v % 2, 0, k, :], XT[:], ACT.Copy).then_inc(mix_hi_made, 1)

        def ds1(k):
            return bass.ds(k, 1)

        QUARTERS = 4
        QK = KD // QUARTERS

        def ln_pe(pe, n, tok):
            N = tok.stop - tok.start
            pe.wait_ge(residual_added, KD // 2 * (n + 1))
            for k in range(KD):
                mm = nc.tensor.matmul(PS[:, 4, 0:N], C["ones_mean"][:], X[:, k, tok], start=(k == 0), stop=(k == KD - 1))
            mm.then_inc(ln_mean, 1)
            for q in range(QUARTERS):
                pe.wait_ge(ln_squared, QUARTERS * n + q + 1)
                for k in range(q * QK, (q + 1) * QK):
                    mm = nc.tensor.matmul(PS[:, 5, 0:N], C["ones_mean"][:], SQ[:, k, 0:N],
                                          start=(k == 0), stop=(k == KD - 1))
            mm.then_inc(ln_var, 1)

        def ln_act(act, n, tok):
            N = tok.stop - tok.start
            for q in range(QUARTERS):
                act.wait_ge(ln_centred, QUARTERS * n + q + 1)
                nc.scalar.activation(SQ[:, q * QK:(q + 1) * QK, 0:N], X[:, q * QK:(q + 1) * QK, tok], ACT.Square)\
                  .then_inc(ln_squared, 1)
            act.wait_ge(ln_eps_added, n + 1)
            nc.scalar.activation(RS[:, 0:N], RS[:, 0:N], ACT.Sqrt).then_inc(ln_rooted, 1)

        def ln_dve(dve, n, tok):
            N = tok.stop - tok.start
            dve.wait_ge(ln_mean, n + 1)
            for q in range(QUARTERS):
                xq = X[:, q * QK:(q + 1) * QK, tok]
                nc.vector.tensor_tensor(xq, xq, PS[:, 4:5, 0:N].to_broadcast((P, QK, N)), ALU.subtract)\
                  .then_inc(ln_centred, 1)
            dve.wait_ge(ln_var, n + 1)
            nc.vector.tensor_scalar(RS[:, 0:N], PS[:, 5, 0:N], LN_EPS, None, ALU.add).then_inc(ln_eps_added, 1)
            dve.wait_ge(ln_rooted, n + 1)
            nc.vector.reciprocal(RS[:, 0:N], RS[:, 0:N]).then_inc(ln_inverted, 1)
            dve.wait_ge(ln_inverted, n + 1)
            for k in range(KD):
                nc.vector.scalar_tensor_tensor(out=X[:, k, tok], in0=X[:, k, tok], scalar=PAR[:, V_LN_G + n, k:k + 1],
                                               in1=RS[:, 0:N], op0=ALU.mult, op1=ALU.mult).then_inc(ln_scaled, 1)
            for k in range(KD):
                dve.wait_ge(ln_scaled, KD * n + k + 1)
                nc.vector.tensor_scalar(X[:, k, tok], X[:, k, tok], PAR[:, V_LN_B + n, k:k + 1], None, ALU.add)\
                  .then_inc(ln_shifted, 1)

        def split_x_act(act, f, tok):
            for k in range(KD):
                if f == 0:
                    act.wait_ge(turned_copied, 3 * (k // 4 + 1))
                else:
                    act.wait_ge(ln_shifted, KD + k + 1)
                nc.scalar.activation(XA[:, 0, k, tok], X[:, k, tok], ACT.Copy).then_inc(x_hi_made, 1)

        def split_x_dve(dve, f, tok):
            for k in range(KD):
                dve.wait_ge(x_hi_made, KD * f + k + 1)
                nc.vector.tensor_tensor(XA[:, 1, k, tok], X[:, k, tok], XA[:, 0, k, tok].bitcast(F32), ALU.subtract)\
                  .then_inc(x_lo_made, 1)

        TOK_ROWS = [P, P, L - 2 * P]

        names = """pair_done lora_landed vectors_picked zw_made za_made zg_made gate_copied w_tanh a_tanh
            decay_made a_made k_squared norm_summed norm_eps norm_rooted norm_inverted kk_made cum_made e_made
            ei_made ac_made rc_made b_plain ka_made k2_made b_doubled a_doubled k_doubled v_doubled bonus_rk_made
            turned_ready bt_copied kt_copied vt_copied gram_ready lt_masked gak_masked grb_masked grk_masked
            ti_off ti_first tt_off tt_first z_ready z_masked t_ready ti_added tt_added
            rhs_ready rhs_copied u_ready u_copied y_ready s_ready s_made s_decayed y_taken
            gn_mean gn_centred gn_squared gn_var gn_eps gn_rooted gn_inverted gn_scaled
            bonus_ready bonus_scaled bonus_added zeros_set""".split()
        S = {n: sem(n) for n in names}
        NL = len(LEVELS)
        NY = NCH - 1
        FLAT = PS[:].rearrange("p b n -> p (b n)")

        def flat(t):
            return t[:].rearrange("p c t -> p (c t)")

        def real(t):
            return flat(t)[:, PAD:LP]

        def matrix(t, c):
            return t[:, c].rearrange("p h t -> p (h t)")

        def spread(ap):
            return ap.rearrange("p c (o t) -> p c o t", o=1).to_broadcast((P, ap.shape[1], 2, CHUNK))

        def masked(name, n=NCH):
            return C[name][:].rearrange("p (o h t) -> p o h t", o=1, h=2).to_broadcast((P, n, 2, CHUNK))

        def incl():
            return C["incl"][:].rearrange("p (o t) -> p o t", o=1).to_broadcast((P, NY, CHUNK))

        def bank(q, b, n):
            return PS[:, 4 * q + b, 0:n]

        def product(q, n, c0=0):
            at_ = 2048 * q + 2 * LP * n
            return FLAT[:, at_ + P * c0:at_ + 2 * LP].rearrange("p (c h t) -> p c h t", h=2, t=CHUNK)

        def each_chunk(q, n, lhs, rhs, c0=0):
            for c in range(c0, NCH):
                at_ = 2048 * q + 2 * LP * n + P * c
                mm = nc.tensor.matmul(FLAT[:, at_:at_ + P], lhs(c), rhs(c), start=True, stop=True)
            return mm

        def first_chunk(level):
            return 0 if LEVELS[level] < N_META else 1

        W0, A0 = NVEC, NVEC + 1

        def count(i, q, step=0, steps=1):
            return 2 * steps * i + 2 * step + q + 1

        def scan_sp(sp):
            with sp.Fori(0, KD // 2) as i:
                sp.wait_ge(S["pair_done"], count(i, 1))
                cols = bass.ds(2 * P * i, 2 * P)
                sp.dma_start(LW[0:LORA, 0, :], w["rwkv_w2"][:, cols]).then_inc(S["lora_landed"], 16)
                sp.dma_start(LW[0:LORA, 1, :], w["rwkv_a2"][:, cols]).then_inc(S["lora_landed"], 16)
                sp.dma_start(LW[:, 2:4, :], w["rwkv_g2"].rearrange("(k p) n -> p k n", p=P)[:, :, cols])\
                  .then_inc(S["lora_landed"], 16)

        def scan_act(act):
            A = nc.scalar.activation
            with act.Fori(0, KD // 2) as i:
                for q in LANES:
                    p = 2 * i + q
                    act.wait_ge(S["pair_done"], count(i, q))
                    for h in range(2):
                        rows = slice(HEAD * h, HEAD * (h + 1))
                        A(VBD[q][rows, 0, h, PAD:CHUNK], KVR[rows, 1, p, 0:N_META], ACT.Copy)\
                            .then_inc(S["v_doubled"], 1)
                        A(VBD[q][rows, 1:NCH, h, :], KVR[rows, 1, p, REAL].rearrange("p (c t) -> p c t", c=NY),
                          ACT.Copy).then_inc(S["v_doubled"], 1)
                    act.wait_ge(S["vectors_picked"], count(i, q))
                    A(real(SQK[q]), KVR[:, 0, p, :], ACT.Square, scale=PP[q][:, V_KK:V_KK + 1])\
                        .then_inc(S["k_squared"], 1)
                    act.wait_ge(S["zw_made"], count(i, q))
                    A(real(LWD[q]), bank(q, 0, L), ACT.Tanh, bias=PP[q][:, W0:W0 + 1], scale=0.5)\
                        .then_inc(S["w_tanh"], 1)
                    act.wait_ge(S["za_made"], count(i, q))
                    A(real(AA[q]), bank(q, 1, L), ACT.Tanh, bias=PP[q][:, A0:A0 + 1], scale=0.5)\
                        .then_inc(S["a_tanh"], 1)
                    act.wait_ge(S["zg_made"], count(i, q))
                    A(GG[q][:], bank(q, 2, SEQ), ACT.Copy).then_inc(S["gate_copied"], 1)
                for q in LANES:
                    act.wait_ge(S["cum_made"], count(i, q))
                    A(E[q][:, :, 1:CHUNK + 1], CUM[q][:], ACT.Exp).then_inc(S["e_made"], 1)
                    A(flat(EI[q]), flat(CUM[q]), ACT.Exp, scale=-1.0).then_inc(S["ei_made"], 1)
                for q in LANES:
                    act.wait_ge(S["norm_eps"], count(i, q))
                    A(real(RN[q]), real(RN[q]), ACT.Sqrt).then_inc(S["norm_rooted"], 1)
                for q in LANES:
                    act.wait_ge(S["turned_ready"], count(i, q))
                    A(VT[q][:], product(q, 0), ACT.Copy).then_inc(S["vt_copied"], 1)
                    A(BT[q][:], product(q, 1), ACT.Copy).then_inc(S["bt_copied"], 1)
                    A(KT[q][:], product(q, 2), ACT.Copy).then_inc(S["kt_copied"], 1)
                for c in range(NCH):
                    for q in LANES:
                        act.wait_ge(S["rhs_ready"], count(i, q, c, NCH))
                        A(RHS[q][:], bank(q, 0, P).rearrange("p (h t) -> p h t", h=2), ACT.Copy)\
                            .then_inc(S["rhs_copied"], 1)
                    for q in LANES:
                        act.wait_ge(S["u_ready"], count(i, q, c, NCH))
                        A(UU[q][:], bank(q, 1, P).rearrange("p (h t) -> p h t", h=2), ACT.Copy)\
                            .then_inc(S["u_copied"], 1)
                for q in LANES:
                    act.wait_ge(S["y_ready"], count(i, q, NY - 1, NY))
                    A(YC[q].rearrange("p (c t) -> p c t", c=NY),
                      bank(q, 2, NY * P).rearrange("p (c h t) -> p c h t", c=NY, h=2)[:, :, 1], ACT.Copy)\
                        .then_inc(S["y_taken"], 1)
                for q in LANES:
                    act.wait_ge(S["gn_centred"], count(i, q))
                    A(YQ[q], YC[q], ACT.Square).then_inc(S["gn_squared"], 1)
                for q in LANES:
                    act.wait_ge(S["gn_eps"], count(i, q))
                    A(RG[q], RG[q], ACT.Sqrt).then_inc(S["gn_rooted"], 1)

        def scan_pool(pool):
            pool.wait_ge(const_landed, 16 * len(CONST_COLUMNS))
            pool.wait_ge(blocks_multiplied, proj_r.end)
            for t in (*LWD, *AA, *TH, *SQK, *KK, *K2, *AR, *ABD, *BBD, *KBD, *VBD, *GR):
                nc.gpsimd.memset(t[:], 0.0).then_inc(S["zeros_set"], 1)
            for t in E:
                nc.gpsimd.memset(t[:], 1.0).then_inc(S["zeros_set"], 1)
            with pool.Fori(0, KD // 2) as i:
                for q in LANES:
                    for h in range(2):
                        rows = slice(HEAD * h, HEAD * (h + 1))
                        pool.wait_ge(S["k2_made"], count(i, q))
                        pool.wait_ge(S["ei_made"], count(i, q))
                        if q == 1:
                            pool.wait_ge(S["a_doubled"], count(i, 0))
                        nc.gpsimd.tensor_tensor(KBD[q][rows, :, h, :], K2[q][rows], EI[q][rows], ALU.mult)\
                            .then_inc(S["k_doubled"], 1)
                    pool.wait_ge(S["ac_made"], count(i, q))
                    pool.wait_ge(S["k_doubled"], 4 * i + 2 * q + 2)
                    nc.gpsimd.tensor_tensor(ABD[q][:], spread(AR[q][:, :, 0, :]), masked("bd"), ALU.mult)\
                        .then_inc(S["a_doubled"], 1)
                for c in range(1, NY):
                    for q in LANES:
                        pool.wait_ge(S["s_made"], count(i, q, c - 1, NY))
                        end = E[q][:, c, CHUNK:CHUNK + 1].rearrange("p (o t) -> p o t", o=1)
                        nc.gpsimd.tensor_tensor(SW[q][:], SS[q][:], end.to_broadcast((P, 2, CHUNK)), ALU.mult)\
                            .then_inc(S["s_decayed"], 1)

        def scan_pe(pe):
            M = nc.tensor.matmul
            with pe.Fori(0, KD // 2) as i:
                pe.wait_ge(S["lora_landed"], 48 * i + 48)
                for q in LANES:
                    lora = slice(P * q, P * (q + 1))
                    pe.wait_ge(S["pair_done"], count(i, q))
                    M(bank(q, 0, L), LW[0:LORA, 0, lora], LH[0:LORA, 0, :], start=True, stop=True)\
                        .then_inc(S["zw_made"], 1)
                    M(bank(q, 1, L), LW[0:LORA, 1, lora], LH[0:LORA, 1, :], start=True, stop=True)\
                        .then_inc(S["za_made"], 1)
                    for k in range(2):
                        mm = M(bank(q, 2, SEQ), LW[:, 2 + k, lora], LH[:, 2 + k, REAL], start=(k == 0), stop=(k == 1))
                    mm.then_inc(S["zg_made"], 1)
                    pe.wait_ge(S["k_squared"], count(i, q))
                    M(bank(q, 3, L), C["head_sum"][:], real(SQK[q]), start=True, stop=True)\
                        .then_inc(S["norm_summed"], 1)
                for q in LANES:
                    pe.wait_ge(S["a_tanh"], count(i, q))
                    pe.wait_ge(S["v_doubled"], 8 * i + 4 * q + 4)
                    pe.wait_ge(S["gate_copied"], count(i, q))
                    pe.wait_ge(S["norm_eps"], count(i, q))
                    each_chunk(q, 0, lambda c: matrix(VBD[q], c), lambda c: C["ident"][:])
                for q in LANES:
                    pe.wait_ge(S["b_doubled"], 4 * i + 2 * q + 2)
                    each_chunk(q, 1, lambda c: matrix(BBD[q], c), lambda c: C["ident"][:])
                    pe.wait_ge(S["k_doubled"], 4 * i + 2 * q + 2)
                    each_chunk(q, 2, lambda c: matrix(KBD[q], c), lambda c: C["ident"][:])\
                        .then_inc(S["turned_ready"], 1)
                for q in LANES:
                    pe.wait_ge(S["kt_copied"], count(i, q))
                    pe.wait_ge(S["rc_made"], count(i, q))
                    pe.wait_ge(S["ac_made"], count(i, q))
                    each_chunk(q, 1, lambda c: matrix(BBD[q], c), lambda c: matrix(AR[q], c))
                    each_chunk(q, 2, lambda c: matrix(KBD[q], c), lambda c: matrix(AR[q], c))
                    pe.wait_ge(S["a_doubled"], count(i, q))
                    each_chunk(q, 0, lambda c: matrix(ABD[q], c), lambda c: matrix(BBD[q], c))\
                        .then_inc(S["gram_ready"], 1)
                for l in range(NL):
                    c0 = first_chunk(l)
                    for q in LANES:
                        if l == 0:
                            pe.wait_ge(S["tt_first"], count(i, q))
                            pe.wait_ge(S["grk_masked"], count(i, q))
                        else:
                            pe.wait_ge(S["tt_added"], count(i, q, l - 1, NL))
                        each_chunk(q, 0, lambda c: matrix(LT[q], c), lambda c: matrix(TI[q], c), c0)\
                            .then_inc(S["z_ready"], 1)
                    for q in LANES:
                        pe.wait_ge(S["z_masked"], count(i, q, l, NL))
                        if l < NL - 1:
                            each_chunk(q, 1, lambda c: matrix(TT[q], c), lambda c: matrix(ZZ[q], c), c0)
                        each_chunk(q, 2, lambda c: matrix(ZZ[q], c), lambda c: matrix(TT[q], c), c0)\
                            .then_inc(S["t_ready"], 1)
                for c in range(NCH):
                    y = [bank(q, 2, NY * P)[:, P * (c - 1):P * c] for q in LANES]
                    for q in LANES:
                        if c == 0:
                            pe.wait_ge(S["tt_added"], count(i, q, NL - 1, NL))
                        mm = M(bank(q, 0, P), matrix(GAK[q], c), matrix(VT[q], c), start=True, stop=(c == 0))
                        if c == 0:
                            mm.then_inc(S["rhs_ready"], 1)
                        else:
                            pe.wait_ge(S["s_made"], count(i, q, c - 1, NY))
                            M(bank(q, 0, P), matrix(ABD[q], c), SS[q][:].rearrange("p h t -> p (h t)"),
                              start=False, stop=True).then_inc(S["rhs_ready"], 1)
                    for q in LANES:
                        if c:
                            M(y[q], SS[q][:].rearrange("p h t -> p (h t)"), matrix(AR[q], c), start=True, stop=False)
                            M(y[q], matrix(VT[q], c), GR[q][:, c, 1:3].rearrange("p g t -> p (g t)"),
                              start=False, stop=False)
                        pe.wait_ge(S["rhs_copied"], count(i, q, c, NCH))
                        M(bank(q, 1, P), matrix(TT[q], c), RHS[q][:].rearrange("p h t -> p (h t)"),
                          start=True, stop=True).then_inc(S["u_ready"], 1)
                    for q in LANES:
                        if c < NY:
                            M(bank(q, 3, P), matrix(KT[q], c), matrix(VT[q], c), start=True, stop=False)
                        pe.wait_ge(S["u_copied"], count(i, q, c, NCH))
                        if c < NY:
                            M(bank(q, 3, P), matrix(BT[q], c), UU[q][:].rearrange("p h t -> p (h t)"),
                              start=False, stop=True).then_inc(S["s_ready"], 1)
                        if c:
                            M(y[q], UU[q][:].rearrange("p h t -> p (h t)"),
                              GR[q][:, c, 0:2].rearrange("p g t -> p (g t)"), start=False, stop=True)\
                                .then_inc(S["y_ready"], 1)
                for q in LANES:
                    M(bank(q, 0, SEQ), C["head_sum"][:], flat(SQK[q])[:, CHUNK:LP], start=True, stop=True)\
                        .then_inc(S["bonus_ready"], 1)
                for q in LANES:
                    pe.wait_ge(S["y_taken"], count(i, q))
                    M(bank(q, 1, SEQ), C["head_mean"][:], YC[q], start=True, stop=True).then_inc(S["gn_mean"], 1)
                for q in LANES:
                    pe.wait_ge(S["gn_squared"], count(i, q))
                    M(bank(q, 3, SEQ), C["head_mean"][:], YQ[q], start=True, stop=True).then_inc(S["gn_var"], 1)

        def scan_dve(dve):
            TTEN, TS, STT = nc.vector.tensor_tensor, nc.vector.tensor_scalar, nc.vector.scalar_tensor_tensor
            dve.wait_ge(projected, proj_r.projected0 + KD // 2)
            dve.wait_ge(S["zeros_set"], 26)
            dve.sem_inc(S["pair_done"], 2)

            with dve.Fori(0, KD // 2) as i:
                def n(q):
                    return count(i, q)

                for q in LANES:
                    dve.wait_ge(S["pair_done"], n(q))
                    nc.vector.tensor_copy(PP[q][:, 0:NVEC], PAR[:, :, 2 * i + q])
                    nc.vector.tensor_copy(PP[q][:, NVEC:NVEC + 2], HALF[:, :, 2 * i + q])\
                        .then_inc(S["vectors_picked"], 1)
                for q in LANES:
                    dve.wait_ge(S["w_tanh"], n(q))
                    TS(real(LWD[q]), real(LWD[q]), -DECAY / 2, -DECAY / 2, ALU.mult, ALU.add)\
                        .then_inc(S["decay_made"], 1)
                    dve.wait_ge(S["decay_made"], n(q))
                    nc.vector.tensor_tensor_scan(flat(CUM[q]), C["restart"][:], flat(LWD[q]), 0.0,
                                                 ALU.mult, ALU.add).then_inc(S["cum_made"], 1)
                for q in LANES:
                    dve.wait_ge(S["norm_summed"], n(q))
                    dve.wait_ge(S["cum_made"], n(q))
                    TS(real(RN[q]), bank(q, 3, L), 1e-12, None, ALU.add).then_inc(S["norm_eps"], 1)
                    dve.wait_ge(S["a_tanh"], n(q))
                    TS(real(AA[q]), real(AA[q]), 0.5, 0.5, ALU.mult, ALU.add).then_inc(S["a_made"], 1)
                    dve.wait_ge(S["a_made"], n(q))
                    dve.wait_ge(S["vectors_picked"], n(q))
                    TS(real(TH[q]), real(AA[q]), 1.0, PP[q][:, V_KA:V_KA + 1], ALU.subtract, ALU.mult)\
                        .then_inc(S["ka_made"], 1)
                    dve.wait_ge(S["ka_made"], n(q))
                    STT(out=real(K2[q]), in0=real(TH[q]), scalar=1.0, in1=KVR[:, 0, 2 * i + q, :],
                        op0=ALU.add, op1=ALU.mult).then_inc(S["k2_made"], 1)
                for q in LANES:
                    dve.wait_ge(S["norm_rooted"], n(q))
                    nc.vector.reciprocal(real(RN[q]), real(RN[q])).then_inc(S["norm_inverted"], 1)
                    dve.wait_ge(S["norm_inverted"], n(q))
                    STT(out=real(KK[q]), in0=KVR[:, 0, 2 * i + q, :], scalar=PP[q][:, V_KK:V_KK + 1],
                        in1=real(RN[q]), op0=ALU.mult, op1=ALU.mult).then_inc(S["kk_made"], 1)
                    dve.wait_ge(S["kk_made"], n(q))
                    TTEN(real(TH[q]), real(KK[q]), real(AA[q]), ALU.mult).then_inc(S["b_plain"], 1)
                    dve.wait_ge(S["e_made"], n(q))
                    STT(out=AR[q][:, :, 0, :], in0=KK[q][:], scalar=-1.0, in1=E[q][:, :, 0:CHUNK],
                        op0=ALU.mult, op1=ALU.mult).then_inc(S["ac_made"], 1)
                    dve.wait_ge(S["ei_made"], n(q))
                    dve.wait_ge(S["b_plain"], n(q))
                    for h in range(2):
                        rows = slice(HEAD * h, HEAD * (h + 1))
                        TTEN(BBD[q][rows, :, h, :], TH[q][rows], EI[q][rows], ALU.mult).then_inc(S["b_doubled"], 1)
                    r = KVR[:, 2, 2 * i + q, REAL].rearrange("p (c t) -> p c t", c=NY)
                    TTEN(AR[q][:, 1:NCH, 1, :], r, E[q][:, 1:NCH, 1:CHUNK + 1], ALU.mult).then_inc(S["rc_made"], 1)
                    STT(out=SQK[q][:, 1:NCH], in0=r, scalar=PP[q][:, V_RK:V_RK + 1], in1=K2[q][:, 1:NCH],
                        op0=ALU.mult, op1=ALU.mult).then_inc(S["bonus_rk_made"], 1)
                for q in LANES:
                    dve.wait_ge(S["gram_ready"], n(q))
                    TTEN(LT[q][:], spread(product(q, 1)[:, :, 0]), masked("bd_strict"), ALU.mult)\
                        .then_inc(S["lt_masked"], 1)
                    TTEN(TI[q][:], product(q, 0), masked("off1"), ALU.mult).then_inc(S["ti_off"], 1)
                    dve.wait_ge(S["lt_masked"], n(q))
                    TTEN(TT[q][:], LT[q][:], masked("offT1"), ALU.mult).then_inc(S["tt_off"], 1)
                    dve.wait_ge(S["ti_off"], n(q))
                    TTEN(TI[q][:], TI[q][:], masked("bd_i"), ALU.add).then_inc(S["ti_first"], 1)
                    dve.wait_ge(S["tt_off"], n(q))
                    TTEN(TT[q][:], TT[q][:], masked("bd_i"), ALU.add).then_inc(S["tt_first"], 1)
                    TTEN(GR[q][:, 1:NCH, 1], product(q, 1)[:, 1:NCH, 1], incl(), ALU.mult).then_inc(S["grb_masked"], 1)
                    TTEN(GAK[q][:], spread(product(q, 2)[:, :, 0]), masked("bd_strict"), ALU.mult)\
                        .then_inc(S["gak_masked"], 1)
                    TTEN(GR[q][:, 1:NCH, 2], product(q, 2)[:, 1:NCH, 1], incl(), ALU.mult).then_inc(S["grk_masked"], 1)
                for l in range(NL):
                    c0 = first_chunk(l)
                    for q in LANES:
                        dve.wait_ge(S["z_ready"], count(i, q, l, NL))
                        TTEN(ZZ[q][:, c0:NCH], product(q, 0, c0), masked(f"off{LEVELS[l]}", NCH - c0), ALU.mult)\
                            .then_inc(S["z_masked"], 1)
                    for q in LANES:
                        dve.wait_ge(S["t_ready"], count(i, q, l, NL))
                        if l == 0:
                            dve.wait_ge(S["ti_first"], n(q))
                            dve.wait_ge(S["tt_first"], n(q))
                        else:
                            dve.wait_ge(S["tt_added"], count(i, q, l - 1, NL))
                        if l < NL - 1:
                            TTEN(TI[q][:, c0:NCH], TI[q][:, c0:NCH], product(q, 1, c0), ALU.add)\
                                .then_inc(S["ti_added"], 1)
                        TTEN(TT[q][:, c0:NCH], TT[q][:, c0:NCH], product(q, 2, c0), ALU.add)\
                            .then_inc(S["tt_added"], 1)
                for c in range(NY):
                    for q in LANES:
                        s = bank(q, 3, P).rearrange("p (h t) -> p h t", h=2)
                        end = E[q][:, c, CHUNK:CHUNK + 1]
                        dve.wait_ge(S["s_ready"], count(i, q, c, NY))
                        if c == 0:
                            TS(SS[q][:], s, end, None, ALU.mult).then_inc(S["s_made"], 1)
                        else:
                            dve.wait_ge(S["s_decayed"], count(i, q, c - 1, NY - 1))
                            STT(out=SS[q][:], in0=s, scalar=end, in1=SW[q][:], op0=ALU.mult, op1=ALU.add)\
                                .then_inc(S["s_made"], 1)
                for q in LANES:
                    dve.wait_ge(S["bonus_ready"], n(q))
                    TTEN(BN[q], KVR[:, 1, 2 * i + q, REAL], bank(q, 0, SEQ), ALU.mult).then_inc(S["bonus_scaled"], 1)
                for q in LANES:
                    dve.wait_ge(S["gn_mean"], n(q))
                    TTEN(YC[q], YC[q], bank(q, 1, SEQ), ALU.subtract).then_inc(S["gn_centred"], 1)
                for q in LANES:
                    dve.wait_ge(S["gn_var"], n(q))
                    TS(RG[q], bank(q, 3, SEQ), GN_EPS, None, ALU.add).then_inc(S["gn_eps"], 1)
                for q in LANES:
                    dve.wait_ge(S["gn_rooted"], n(q))
                    nc.vector.reciprocal(RG[q], RG[q]).then_inc(S["gn_inverted"], 1)
                    dve.wait_ge(S["gn_inverted"], n(q))
                    STT(out=YC[q], in0=YC[q], scalar=PP[q][:, V_GN_G:V_GN_G + 1], in1=RG[q],
                        op0=ALU.mult, op1=ALU.mult).then_inc(S["gn_scaled"], 1)
                    dve.wait_ge(S["gn_scaled"], n(q))
                    dve.wait_ge(S["bonus_scaled"], n(q))
                    STT(out=YC[q], in0=YC[q], scalar=PP[q][:, V_GN_B:V_GN_B + 1], in1=BN[q],
                        op0=ALU.add, op1=ALU.add).then_inc(S["bonus_added"], 1)
                    dve.wait_ge(S["bonus_added"], n(q))
                    TTEN(KVR[:, 2, 2 * i + q, REAL], YC[q], GG[q][:], ALU.mult).then_inc(S["pair_done"], 1)

        with nc.Block() as block:
            @block.sync
            def _(sp):
                tokens = [(TOKS[0:N_META, 0], meta), (TOKS[N_META:P, 0], x[0:P - N_META]),
                          (TOKS[:, 1], x[P - N_META:2 * P - N_META]),
                          (TOKS[0:L - 2 * P, 2], x[2 * P - N_META:SEQ])]
                for dst, src in tokens:
                    sp.dma_start(dst, src).then_inc(tokens_landed, 16)
                for name in const:
                    sp.dma_start(C[name][:], const[name]).then_inc(const_landed, 16)
                row = 0
                for v in vec:
                    for n in range(v.shape[0]):
                        r = row + n
                        sp.dma_start(VROWS[KD * (r % 8):KD * (r % 8) + KD, r // 8, :],
                                     v[n].rearrange("(k p) -> k p", p=P)).then_inc(vectors_landed, 16)
                    row += v.shape[0]
                for ph in phases[:-3]:
                    load_blocks(sp, ph)
                scan_sp(sp)
                for ph in phases[-3:]:
                    load_blocks(sp, ph)
                for i in range(2):
                    sp.wait_ge(out_copied, 4 * (i + 1))
                    sp.dma_start(out[P * i:P * (i + 1)], OUT[:, i]).then_inc(out_stored, 16)
                sp.wait_ge(out_stored, 32)

            @block.gpsimd
            def _(pool):
                scan_pool(pool)

            @block.scalar
            def _(act):
                for i in range(12):
                    kg, tt = i // 3, i % 3
                    rows = TOK_ROWS[tt]
                    act.wait_ge(turned, i + 1)
                    nc.scalar.activation(X[:, 4 * kg:4 * kg + 4, P * tt:P * tt + rows],
                                         PS[:, i % 2].rearrange("p (k t) -> p k t", k=4)[:, :, 0:rows], ACT.Copy)\
                      .then_inc(turned_copied, 1)
                split_x_act(act, 0, ALL)
                with_epilogues(act, in0, split_hi, epilogue_act)
                with_epilogues(act, out0, split_hi, epilogue_act)
                ln_act(act, 0, ALL)
                for v in (0, 1):
                    for k in range(KD):
                        mix_act(act, v, k)
                with_epilogues(act, lora_w, split_hi, epilogue_act)
                with_epilogues(act, lora_a, split_hi, epilogue_act)
                for k in range(KD):
                    mix_act(act, 2, k)
                with_epilogues(act, lora_g, split_hi, epilogue_act)
                for k in range(KD):
                    mix_act(act, 3, k)
                for ph in (proj_k, proj_v, proj_r):
                    with_epilogues(act, ph, split_hi, epilogue_act, side=mix_act)
                scan_act(act)
                act.wait_ge(S["pair_done"], KD + 2)
                for k in range(KD):
                    nc.scalar.activation(YA[:, 0, k], KVR[:, 2, k, REAL], ACT.Copy).then_inc(y_hi_made, 1)
                with_epilogues(act, w_o, split_hi, epilogue_act)
                ln_act(act, 1, REAL)
                split_x_act(act, 1, REAL)
                with_epilogues(act, in1, split_hi, epilogue_act)
                with_epilogues(act, out1, split_hi, epilogue_act)
                ln_act(act, 2, REAL)
                for i in range(8):
                    tt, kg = i // 4, i % 4
                    act.wait_ge(out_turned, i + 1)
                    nc.scalar.activation(OUT[:, tt, 4 * P * kg:4 * P * (kg + 1)], PS[:, 6 + i % 2], ACT.Copy)\
                      .then_inc(out_copied, 1)

            @block.vector
            def _(dve):
                dve.wait_ge(turned, 13)
                nc.vector.tensor_copy(PAR[:].rearrange("p v k -> p (v k)"), PS[:, 2, 0:NVEC * KD])\
                  .then_inc(params_copied, 1)
                dve.wait_ge(params_copied, 1)
                nc.vector.tensor_scalar(HALF[:], PAR[:, V_W0:V_W0 + 2], 0.5, None, ALU.mult).then_inc(params_halved, 1)
                split_x_dve(dve, 0, ALL)
                with_epilogues(dve, in0, split_lo, epilogue_dve, late=split_hidden)
                with_epilogues(dve, out0, split_lo, epilogue_dve)
                ln_dve(dve, 0, ALL)
                dve.wait_ge(ln_shifted, KD)
                nc.vector.tensor_tensor(XX[:, :, 1:L], X[:, :, 0:L - 1], X[:, :, 1:L], ALU.subtract).then_inc(xx_made, 1)
                nc.vector.tensor_scalar(XX[:, :, 0:1], X[:, :, 0:1], -1.0, None, ALU.mult).then_inc(xx_made, 1)
                dve.wait_ge(xx_made, 2)
                for v in (0, 1):
                    for k in range(KD):
                        mix_dve(dve, v, k)
                with_epilogues(dve, lora_w, split_lo, epilogue_dve)
                with_epilogues(dve, lora_a, split_lo, epilogue_dve)
                for k in range(KD):
                    mix_dve(dve, 2, k)
                with_epilogues(dve, lora_g, split_lo, epilogue_dve)
                for k in range(KD):
                    mix_dve(dve, 3, k)
                for ph in (proj_k, proj_v, proj_r):
                    with_epilogues(dve, ph, split_lo, epilogue_dve, side=mix_dve)
                scan_dve(dve)
                for k in range(KD):
                    dve.wait_ge(y_hi_made, k + 1)
                    nc.vector.tensor_tensor(YA[:, 1, k], KVR[:, 2, k, REAL], YA[:, 0, k].bitcast(F32), ALU.subtract)\
                      .then_inc(y_lo_made, 1)
                with_epilogues(dve, w_o, split_lo, epilogue_dve)
                ln_dve(dve, 1, REAL)
                split_x_dve(dve, 1, REAL)
                with_epilogues(dve, in1, split_lo, epilogue_dve, late=split_hidden)
                with_epilogues(dve, out1, split_lo, epilogue_dve)
                ln_dve(dve, 2, REAL)

            @block.tensor
            def _(pe):
                pe.wait_ge(const_landed, 16 * len(const))
                pe.wait_ge(tokens_landed, 64)
                for i in range(12):
                    kg, tt = i // 3, i % 3
                    rows = TOK_ROWS[tt]
                    if i >= 2:
                        pe.wait_ge(turned_copied, i - 1)
                    for k in range(4):
                        mm = nc.tensor.transpose(PS[:, i % 2, P * k:P * k + rows],
                                                 TOKS[0:rows, tt, P * (4 * kg + k):P * (4 * kg + k + 1)],
                                                 C["ident"][0:rows, 0:rows])
                    mm.then_inc(turned, 1)
                pe.wait_ge(vectors_landed, 16 * NVEC)
                for r in range(3):
                    rows = min(P, KD * NVEC - P * r)
                    mm = nc.tensor.transpose(PS[:, 2, P * r:P * r + rows], VROWS[0:rows, r, :],
                                             C["ident"][0:rows, 0:rows])
                mm.then_inc(turned, 1)
                pe.wait_ge(params_copied, 1)
                for ph in (in0, out0):
                    multiply(pe, ph)
                ln_pe(pe, 0, ALL)
                for ph in (lora_w, lora_a, lora_g, proj_k, proj_v, proj_r):
                    multiply(pe, ph)
                scan_pe(pe)
                multiply(pe, w_o)
                ln_pe(pe, 1, REAL)
                for ph in (in1, out1):
                    multiply(pe, ph)
                ln_pe(pe, 2, REAL)
                for i in range(8):
                    tt, kg = i // 4, i % 4
                    pe.wait_ge(ln_shifted, 2 * KD + 4 * kg + 4)
                    if i >= 2:
                        pe.wait_ge(out_copied, i - 1)
                    for k in range(4):
                        at_ = N_META + P * tt
                        mm = nc.tensor.transpose(PS[:, 6 + i % 2, P * k:P * (k + 1)], X[:, 4 * kg + k, at_:at_ + P],
                                                 C["ident"][:])
                    mm.then_inc(out_turned, 1)


CONST_COLUMNS = {k: a.shape[1] for k, a in constants().items()}


def kernel(x, meta_tokens, ln_g, ln_b, ffn_in, ffn_out, **more):
    import concourse.bacc as bacc
    from concourse.bass_utils import run_bass_kernel_spmd

    nc = bacc.Bacc("TRN2", target_bir_lowering=False, num_devices=1)
    arrays = {"x": x[0], "meta_tokens": meta_tokens, "ln_g": ln_g[0], "ln_b": ln_b[0],
              "ffn_in": ffn_in[0], "ffn_out": ffn_out[0]}
    for name in ("rwkv_w_rkv", "rwkv_w1", "rwkv_w2", "rwkv_a1", "rwkv_a2", "rwkv_g1", "rwkv_g2", "rwkv_w_o"):
        arrays[name] = more[name]
    for name in VECTORS[2:]:
        arrays[name] = more[name].reshape(-1, D)
    arrays = {n: np.ascontiguousarray(a) for n, a in arrays.items()}
    arrays |= {"c_" + n: a for n, a in constants().items()}
    aps = {n: nc.dram_tensor("in_" + n, a.shape, F32, kind="ExternalInput").ap() for n, a in arrays.items()}
    out = nc.dram_tensor("out", (SEQ, D), F32, kind="ExternalOutput").ap()
    rwkv_layer(nc, aps["x"], aps["meta_tokens"], aps, [aps[n] for n in VECTORS],
               {n[2:]: a for n, a in aps.items() if n.startswith("c_")}, out)
    result = run_bass_kernel_spmd(nc, [{"in_" + n: a for n, a in arrays.items()}], core_ids=[0])
    return result.results[0]["out"].reshape(1, SEQ, D)
```

```python
from contextlib import ExitStack
from math import exp

import numpy as np
import concourse.bass as bass
from concourse import mybir

F32 = mybir.dt.float32
F32R = mybir.dt.float32r
ALU = mybir.AluOpType
ACT = mybir.ActivationFunctionType

P = 128
D = 2048
D_FF = 5632
SEQ = 256
N_META = 16
L = SEQ + N_META
KD = D // P
KF = D_FF // P
HEAD = 64
CHUNK = 64
PAD = CHUNK - N_META
NCH = (L + PAD) // CHUNK
LP = NCH * CHUNK
LORA = 96
GATE = 256
ALPHA = 2.0 ** 0.25
LN_EPS = 1e-5
GN_EPS = 64e-5
DECAY = exp(-0.5)

RING = 4
KB = 4
WIDE = 256
LEVELS = [2, 4, 8, 16, 32]

VECTORS = ["ln_g", "ln_b", "rwkv_mix", "rwkv_w0", "rwkv_a0", "rwkv_k_k", "rwkv_k_a", "rwkv_r_k",
           "rwkv_gn_g", "rwkv_gn_b"]
V_LN_G, V_LN_B, V_MIX, V_W0, V_A0, V_KK, V_KA, V_RK, V_GN_G, V_GN_B = 0, 3, 6, 12, 13, 14, 15, 16, 17, 18
NVEC = 19


def constants():
    p = np.arange(P)
    head, s = p // CHUNK, p % CHUNK
    t = np.arange(CHUNK)
    same = (head[:, None] == np.arange(2)[None, :]).astype(np.float32)[:, :, None]
    c = {
        "ident": np.eye(P),
        "ones_mean": np.full((P, P), 1.0 / D),
        "head_sum": head[:, None] == head[None, :],
        "head_mean": (head[:, None] == head[None, :]) / HEAD,
        "bd": same * np.ones((1, 1, CHUNK)),
        "bd_strict": same * (s[:, None] < t[None, :])[:, None, :],
        "incl": s[:, None] <= t[None, :],
        "bd_i": same * (s[:, None] == t[None, :])[:, None, :],
        "restart": np.broadcast_to(np.arange(LP) % CHUNK != 0, (P, LP)),
    }
    for b in [1] + LEVELS:
        up = (s[:, None] // (2 * b) == t[None, :] // (2 * b)) & (s[:, None] // b < t[None, :] // b)
        if b == 1:
            c["offT1"] = same * up[:, None, :]
            continue
        low = (s[:, None] // (2 * b) == t[None, :] // (2 * b)) & (s[:, None] // b > t[None, :] // b)
        c[f"off{b}"] = same * low[:, None, :]
    return {k: np.ascontiguousarray(np.asarray(v, np.float32).reshape(P, -1)) for k, v in c.items()}


class Group:

    def __init__(self, weight, column, step, width=WIDE):
        self.weight, self.column, self.step, self.width = weight, column, step, width


class Phase:

    def __init__(self, name, steps, nb, groups, rhs, tok, ready, side=None):
        self.name, self.steps, self.nb, self.groups = name, steps, nb, groups
        self.rhs, self.tok, self.ready, self.side = rhs, tok, ready, side
        self.n = tok.stop - tok.start
        self.kind = name.rstrip("01")


def number(phases):
    block, uses = 0, [0] * RING
    count = {"staged": 0, "pairs": 0, "added": 0, "projected": 0}
    for ph in phases:
        ph.block0, ph.uses0 = block, list(uses)
        ph.staged0, ph.pairs0 = count["staged"], count["pairs"]
        ph.added0, ph.projected0 = count["added"], count["projected"]
        ph.blocks = ph.nb * len(ph.groups)
        ph.per_group = [len(range(s, ph.nb, RING)) for s in range(RING)]
        block += ph.steps * ph.blocks
        for s in range(RING):
            uses[s] += ph.steps * len(ph.groups) * ph.per_group[s]
        n = ph.steps * len(ph.groups)
        if ph.kind == "in":
            count["staged"] += ph.steps
            count["pairs"] += ph.steps
        elif ph.kind in ("out", "w_o"):
            count["staged"] += n
            count["added"] += n
        else:
            count["projected"] += n
        ph.end = block


def wait(eng, sem, value):
    if not isinstance(value, int) or value > 0:
        eng.wait_ge(sem, value)


def rwkv_layer(nc, x, meta, w, vec, const, out):
    with ExitStack() as ctx:
        def sem(name):
            return ctx.enter_context(nc.semaphore(name))

        XBYTES = KD * L * 4
        ARENA = 2 * (KD + KF) * L * 4
        start = (nc.sbuf_base + 31) // 32 * 32
        fixed = [start]

        def sb(name, shape, dt=F32):
            n = int(np.prod(shape[1:])) * 4
            t = nc.alloc_sbuf_tensor_at(name, shape, dt, offset=fixed[0])
            fixed[0] += (n + 31) // 32 * 32
            return t

        X = sb("X", [P, KD, L])
        rings0 = fixed[0]
        RAW = sb("RAW", [P, RING, KB, WIDE])
        WH = sb("WH", [P, RING, KB, WIDE], F32R)
        WL = sb("WL", [P, RING, KB, WIDE], F32R)
        C = {k: sb("c_" + k, [P, n]) for k, n in CONST_COLUMNS.items()}
        PAR = sb("PAR", [P, NVEC, KD])
        HALF = sb("HALF", [P, 2, KD])
        STAGE = sb("STAGE", [P, 2, L])
        HV = sb("HV", [P, 2, L])
        RS = sb("RS", [P, L])
        ZERO, ROOT = sb("ZERO", [P, 1]), sb("ROOT", [P, 1])
        at0 = fixed[0]
        assert at0 + ARENA <= nc.sbuf_usable_end, (at0 + ARENA, nc.sbuf_usable_end)

        def at(name, shape, offset, dt=F32):
            n = int(np.prod(shape[1:])) * 4
            assert offset + n <= ARENA, (name, offset, n)
            return nc.alloc_sbuf_tensor_at(name, shape, dt, offset=at0 + offset)

        XA = at("XA", [P, 2, KD, L], 0, F32R)
        H = at("H", [P, 2, KF, L], 2 * XBYTES, F32R)
        TOKS = at("TOKS", [P, 3, D], 2 * XBYTES)
        VROWS = at("VROWS", [P, 3, P], 2 * XBYTES + 12 * D)
        SQ = at("SQ", [P, KD, L], 2 * XBYTES)
        OUT = at("OUT", [P, 2, D], 2 * XBYTES)
        XS = at("XS", [P, 2, 2, KD, L], 0, F32R)
        KVR = at("KVR", [P, 3, KD, L], 4 * XBYTES)
        XX = KVR[:, 2]
        LORA1 = at("LORA1", [P, KD, 2 * LORA + GATE], 0)
        MIXED = KVR
        LH = at("LH", [P, 4, L], 7 * XBYTES)
        XT = at("XT", [P, 2, L], 7 * XBYTES + 16 * L)
        YA = at("YA", [P, 2, KD, SEQ], 0, F32R)
        PS = ctx.enter_context(nc.psum_tensor("PS", [P, 8, 512], F32))

        cursor = [0]

        def tmp(name, *shape):
            t = at(name, [P, *shape], cursor[0])
            cursor[0] += -(-int(np.prod(shape)) * 4 // 32) * 32
            assert cursor[0] <= 4 * XBYTES, (name, cursor[0])
            return t

        def tmp2(name, *shape):
            t = nc.alloc_sbuf_tensor_at(name, [P, *shape], F32, offset=rings0 + cursor[0])
            cursor[0] += -(-int(np.prod(shape)) * 4 // 32) * 32
            assert cursor[0] <= 3 * RING * KB * WIDE * 4, (name, cursor[0])
            return t

        CC, BD = (NCH, CHUNK), (NCH, 2, CHUNK)
        LANES = (0, 1)

        def lanes(alloc, name, *shape):
            return [alloc(f"{name}{q}", *shape) for q in LANES]

        def both(alloc, name, *shape):
            return [lanes(alloc, name + parity, *shape) for parity in ("even", "odd")]

        BBD, KBD, VBD = (lanes(tmp, n, *BD) for n in ("BBD", "KBD", "VBD"))
        LWD, TH, KK, K2 = (lanes(tmp, n, *CC) for n in ("LWD", "TH", "KK", "K2"))
        LW = tmp("LW", 4, 2 * P)
        assert cursor[0] <= 2 * XBYTES
        E = [lanes(tmp, "Eeven", NCH, CHUNK + 1)]
        AA, SQK, CUM, EI = (lanes(tmp, n, *CC) for n in ("AA", "SQK", "CUM", "EI"))
        TT, ABD = lanes(tmp, "TT", *BD), lanes(tmp, "ABD", *BD)
        TR = lanes(tmp, "TR", 3 * NCH, 2, CHUNK)
        SS = lanes(tmp, "SS", 2, CHUNK)
        PP = lanes(tmp, "PP", NVEC + 2)
        cursor[0] = 0
        LT = lanes(tmp2, "LT", *BD)
        ZZ, TI = lanes(tmp2, "ZZ", *BD), lanes(tmp2, "TI", *BD)
        RHS = lanes(tmp2, "RHS", 2, CHUNK)
        assert cursor[0] <= RING * KB * WIDE * 4
        cursor[0] = RING * KB * WIDE * 4
        E.append(lanes(tmp2, "Eodd", NCH, CHUNK + 1))
        AR = both(tmp2, "AR", *BD)
        GAK, GR = lanes(tmp2, "GAK", *BD), lanes(tmp2, "GR", NCH, 3, CHUNK)
        UU, SW = lanes(tmp2, "UU", 2, CHUNK), lanes(tmp2, "SW", 2, CHUNK)
        even_bonus, even_gate = lanes(tmp2, "BNeven", SEQ), lanes(tmp2, "GGeven", SEQ)
        BN = [[t[:] for t in even_bonus], [STAGE[:, q, 0:SEQ] for q in LANES]]
        GG = [[t[:] for t in even_gate], [HV[:, q, 0:SEQ] for q in LANES]]
        RN = LWD
        RGB = at("RGB", [P, 2, SEQ], 7 * XBYTES + 24 * L)
        RG = [RGB[:, q] for q in LANES]
        YC = [XT[:, q, 0:SEQ] for q in LANES]
        YQ = [SQK[q][:].rearrange("p c t -> p (c t)")[:, CHUNK:] for q in LANES]

        const_landed, vectors_landed = sem("const_landed"), sem("vectors_landed")
        tokens_landed = [sem("tokens_landed_half0"), sem("tokens_landed_half1")]
        zero_set, root_loaded = sem("zero_set"), sem("root_loaded")
        raw_landed = [sem(f"raw_landed{s}") for s in range(RING)]
        hi_made, lo_made, blocks_multiplied = sem("hi_made"), sem("lo_made"), sem("blocks_multiplied")
        stage_filled, residual_added, projected = sem("stage_filled"), sem("residual_added"), sem("projected")
        hv_made, h_hi_made, h_lo_made = sem("hv_made"), sem("h_hi_made"), sem("h_lo_made")
        x_hi_made, x_lo_made = sem("x_hi_made"), sem("x_lo_made")
        turned, params_copied, params_halved = sem("turned"), sem("params_copied"), sem("params_halved")
        ln_mean, ln_centred, ln_squared, ln_var = sem("ln_mean"), sem("ln_centred"), sem("ln_squared"), sem("ln_var")
        ln_eps_added, ln_rooted, ln_inverted = sem("ln_eps_added"), sem("ln_rooted"), sem("ln_inverted")
        ln_scaled, ln_shifted = sem("ln_scaled"), sem("ln_shifted")
        lora1_landed, lora_mixed, lora_summed, lora_taken = (
            sem("lora1_landed"), sem("lora_mixed"), sem("lora_summed"), sem("lora_taken"))
        xx_made, mix_made = sem("xx_made"), sem("mix_made")
        mix_hi_made, mix_lo_made = sem("mix_hi_made"), sem("mix_lo_made")
        y_hi_made, y_lo_made = sem("y_hi_made"), sem("y_lo_made")
        out_turned, out_stored = sem("out_turned"), sem("out_stored")
        out_copied_act, out_copied_dve = sem("out_copied_act"), sem("out_copied_dve")
        ident_landed, turned_copied = sem("ident_landed"), [sem("turned_even_copied"), sem("turned_odd_copied")]
        params_turned = sem("params_turned")

        ALL, REAL = slice(0, L), slice(N_META, L)

        def ffn(f, tok):
            win, wout = w["ffn_in"][f], w["ffn_out"][f]
            return [
                Phase(f"in{f}", KF // 2, KD // KB, [Group(win, 0, WIDE), Group(win, D_FF, WIDE)],
                      lambda h, k: XA[:, h, k, tok], tok, lambda k: (x_lo_made, KD * f + k + 1)),
                Phase(f"out{f}", KD // 4, KF // KB, [Group(wout, 0, 2 * WIDE), Group(wout, WIDE, 2 * WIDE)],
                      lambda h, k: H[:, h, k, tok], tok, lambda k: (h_lo_made, KF // 2 * f + k // 2 + 1))]

        def mixed(buf, tok):
            return lambda h, k: XS[:, buf, h, k, tok]

        def mix_ready(v):
            return lambda k: (mix_lo_made, KD * v + k + 1)

        def square(name, weight, rhs, tok, ready, side=None):
            return Phase(name, KD // 4, KD // KB, [Group(weight, 0, 2 * WIDE), Group(weight, WIDE, 2 * WIDE)],
                         rhs, tok, ready, side)

        MIXES = [1, 2, 0]
        MIX_W, MIX_A, MIX_G = 3, 4, 5
        wkv = w["rwkv_w_rkv"]
        in0, out0 = ffn(0, ALL)
        proj_k = square("k", wkv[1], mixed(1, ALL), ALL, mix_ready(0), side=1)
        proj_v = square("v", wkv[2], mixed(0, ALL), ALL, mix_ready(1), side=2)
        proj_r = square("r", wkv[0], mixed(1, REAL), REAL, mix_ready(2))
        w_o = square("w_o", w["rwkv_w_o"], lambda h, k: YA[:, h, k, :], REAL, lambda k: (y_lo_made, k + 1))
        in1, out1 = ffn(1, REAL)
        phases = [in0, out0, proj_k, proj_v, proj_r, w_o, in1, out1]
        number(phases)
        SLOT = {"k": 0, "v": 1, "r": 2}

        def loop(eng, ph, body):
            body(0, True)
            if ph.steps > 1:
                with eng.Fori(1, ph.steps) as t:
                    body(t, False)

        def block_of(ph, t, g, j):
            return ph.block0 + t * ph.blocks + g * ph.nb + j

        def load_blocks(sp, ph, between=None):
            def body(t, first):
                for g, grp in enumerate(ph.groups):
                    for j in range(ph.nb):
                        if first and g == 0 and j == AHEAD and between:
                            between()
                        slot = j % RING
                        wait(sp, lo_made, block_of(ph, t, g, j) - 2)
                        rows = grp.weight[j * KB * P:(j + 1) * KB * P, :].rearrange("(k p) n -> p k n", p=P)
                        sp.dma_start(RAW[:, slot, :, 0:grp.width],
                                     rows[:, :, bass.ds(grp.column + t * grp.step, grp.width)])\
                          .then_inc(raw_landed[slot], 16)
            loop(sp, ph, body)

        def split_hi(act, ph, t, g, j):
            slot, width = j % RING, ph.groups[g].width
            use = ph.uses0[slot] + (t * len(ph.groups) + g) * ph.per_group[slot] + j // RING
            act.wait_ge(raw_landed[slot], 16 * use + 16)
            wait(act, blocks_multiplied, block_of(ph, t, g, j) - 2)
            nc.scalar.activation(WH[:, slot, :, 0:width], RAW[:, slot, :, 0:width], ACT.Copy).then_inc(hi_made, 1)

        def split_lo(dve, ph, t, g, j):
            slot, width = j % RING, ph.groups[g].width
            dve.wait_ge(hi_made, block_of(ph, t, g, j) + 1)
            wait(dve, blocks_multiplied, block_of(ph, t, g, j) - 2)
            nc.vector.tensor_tensor(WL[:, slot, :, 0:width], RAW[:, slot, :, 0:width],
                                    WH[:, slot, :, 0:width].bitcast(F32), ALU.subtract).then_inc(lo_made, 1)

        def wait_for_banks(pe, ph, t, g):
            turn = 2 * t + g - 1
            if isinstance(turn, int) and ph.kind not in ("v", "r"):
                turn = max(turn, 0)
            if ph.kind == "in":
                if g == 0:
                    wait(pe, stage_filled, ph.staged0 + t)
                else:
                    wait(pe, hv_made, ph.pairs0 + t)
            elif ph.kind in ("out", "w_o"):
                wait(pe, stage_filled, ph.staged0 + turn)
            else:
                wait(pe, projected, ph.projected0 + turn)

        def multiply(pe, ph, before_block=None):
            def body(t, first):
                for g, grp in enumerate(ph.groups):
                    wait_for_banks(pe, ph, t, g)
                    for j in range(ph.nb):
                        slot = j % RING
                        if first and before_block:
                            before_block(g, j)
                        pe.wait_ge(lo_made, block_of(ph, t, g, j) + 1)
                        for m in range(0, grp.width, P):
                            mw = min(P, grp.width - m)
                            o = PS[0:mw, 2 * g + m // P, 0:ph.n]
                            for k in range(KB):
                                kk = j * KB + k
                                if first and g == 0 and m == 0:
                                    pe.wait_ge(*ph.ready(kk))
                                hi, lo = WH[:, slot, k, m:m + mw], WL[:, slot, k, m:m + mw]
                                nc.tensor.matmul(o, hi, ph.rhs(0, kk), start=(kk == 0), stop=False)
                                nc.tensor.matmul(o, hi, ph.rhs(1, kk), start=False, stop=False)
                                mm = nc.tensor.matmul(o, lo, ph.rhs(0, kk), start=False,
                                                      stop=(kk == ph.nb * KB - 1))
                        mm.then_inc(blocks_multiplied, 1)
                    if ph.kind in ("out", "w_o") and (g or not first):
                        sum_residual(pe, ph, t if g else t - 1, 1 - g, start=first)
            loop(pe, ph, body)

        def sum_residual(pe, ph, t, g, start=False, stop=False):
            pe.wait_ge(residual_added, ph.added0 + 2 * t + g + 1)
            for i in range(2):
                mm = nc.tensor.matmul(PS[:, 4, 0:ph.n], C["ones_mean"][:], X[:, tile_at(4 * t + 2 * g + i), ph.tok],
                                      start=start and i == 0, stop=stop and i == 1)
            return mm

        def tile_at(k):
            return k if isinstance(k, int) else bass.ds(k, 1)

        def epilogue_act(act, ph, t, g):
            ps = PS[:, 2 * g:2 * g + 2, 0:ph.n]
            if ph.kind == "in" and g == 1:
                act.wait_ge(hv_made, ph.pairs0 + t + 1)
                nc.scalar.activation(H[:, 0, bass.ds(2 * t, 2), ph.tok], HV[:, :, 0:ph.n], ACT.Copy)\
                  .then_inc(h_hi_made, 1)
                return
            act.wait_ge(blocks_multiplied, block_of(ph, t, g, ph.nb))
            if ph.kind == "in":
                wait(act, hv_made, ph.pairs0 + t)
                nc.scalar.activation(STAGE[:, :, 0:ph.n], ps, ACT.Silu).then_inc(stage_filled, 1)
            elif ph.kind in ("out", "w_o"):
                wait(act, residual_added, ph.added0 + 2 * t + g)
                nc.scalar.activation(STAGE[:, :, 0:ph.n], ps, ACT.Copy, scale=0.5 if ph.kind == "out" else 1.0)\
                  .then_inc(stage_filled, 1)
            else:
                nc.scalar.activation(KVR[:, SLOT[ph.kind], bass.ds(4 * t + 2 * g, 2), ph.tok], ps, ACT.Copy)\
                  .then_inc(projected, 1)

        def epilogue_dve(dve, ph, t, g):
            if ph.kind == "in" and g == 1:
                dve.wait_ge(blocks_multiplied, block_of(ph, t, g, ph.nb))
                dve.wait_ge(stage_filled, ph.staged0 + t + 1)
                wait(dve, h_lo_made, ph.pairs0 + t)
                nc.vector.tensor_tensor(HV[:, :, 0:ph.n], STAGE[:, :, 0:ph.n],
                                        PS[:, 2:4, 0:ph.n], ALU.mult).then_inc(hv_made, 1)
            elif ph.kind in ("out", "w_o"):
                dve.wait_ge(stage_filled, ph.staged0 + 2 * t + g + 1)
                xt = X[:, bass.ds(4 * t + 2 * g, 2), ph.tok]
                nc.vector.scalar_tensor_tensor(out=xt, in0=xt, scalar=ALPHA, in1=STAGE[:, :, 0:ph.n],
                                               op0=ALU.mult, op1=ALU.add).then_inc(residual_added, 1)

        def split_hidden(dve, ph, t):
            dve.wait_ge(h_hi_made, ph.pairs0 + t + 1)
            to = bass.ds(2 * t, 2)
            nc.vector.tensor_tensor(H[:, 1, to, ph.tok], HV[:, :, 0:ph.n], H[:, 0, to, ph.tok].bitcast(F32),
                                    ALU.subtract).then_inc(h_lo_made, 1)

        AHEAD = 3

        def with_epilogues(eng, ph, split, epilogue, late=None, side=None, ahead=0, after=None, close=True):
            last = len(ph.groups) - 1

            def body(t, first):
                for g in range(last + 1):
                    for j in range(ph.nb):
                        k = 4 * t + 2 * g + j // 2
                        mixes = side and ph.side is not None and j % 2
                        if mixes and eng is nc.vector:
                            mix_dve(eng, ph.side, k, j // 2)
                        if not (first and g == 0 and j < ahead):
                            split(eng, ph, t, g, j)
                        before = not first or g > 0
                        if j == 1 and before:
                            epilogue(eng, ph, t if g else t - 1, g - 1 if g else last)
                        if j == 2 and before and late and g == 0:
                            late(eng, ph, t - 1)
                        if after and not before:
                            if j == 1:
                                epilogue(eng, after, after.steps - 1, len(after.groups) - 1)
                            if j == 2 and after.kind == "in" and eng is nc.vector:
                                split_hidden(eng, after, after.steps - 1)
                        if mixes:
                            side(eng, ph.side, k, j // 2)
            loop(eng, ph, body)
            if close:
                epilogue(eng, ph, ph.steps - 1, last)

        def mix_tile(dve, to, vector, k):
            return nc.vector.scalar_tensor_tensor(out=to, in0=XX[:, k, :], scalar=PAR[:, V_MIX + vector, bass.ds(k, 1)],
                                                  in1=X[:, k, :], op0=ALU.mult, op1=ALU.add)

        def mix_dve(dve, v, k, half):
            if v == 1:
                dve.wait_ge(lora_summed, KD + 1)
            if v == 2:
                dve.wait_ge(blocks_multiplied, proj_k.end)
            wait(dve, mix_lo_made, KD * v + k - 1)
            mix_tile(dve, XT[:, half], MIXES[v], k).then_inc(mix_made, 1)

        def mix_lo_dve(dve, v, k, half):
            dve.wait_ge(mix_hi_made, KD * v + k + 1)
            buf = (v + 1) % 2
            nc.vector.tensor_tensor(XS[:, buf, 1, k, :], XT[:, half], XS[:, buf, 0, k, :].bitcast(F32),
                                    ALU.subtract).then_inc(mix_lo_made, 1)

        def mix_act(act, v, k, half):
            act.wait_ge(mix_made, KD * v + k + 1)
            nc.scalar.activation(XS[:, (v + 1) % 2, 0, k, :], XT[:, half], ACT.Copy).then_inc(mix_hi_made, 1)

        def lora_pe(pe):
            pe.wait_ge(lora1_landed, 48)
            pe.wait_ge(params_copied, 1)
            for k in range(KD):
                pe.wait_ge(lora_mixed, 2 * k + 2)
                nc.tensor.matmul(PS[0:LORA, 6, 0:L], LORA1[:, k, 0:LORA], MIXED[:, 0, k],
                                 start=(k == 0), stop=(k == KD - 1))
                nc.tensor.matmul(PS[0:LORA, 7, 0:L], LORA1[:, k, LORA:2 * LORA], MIXED[:, 1, k],
                                 start=(k == 0), stop=(k == KD - 1)).then_inc(lora_summed, 1)
            for k in range(KD):
                pe.wait_ge(lora_mixed, 2 * KD + k + 1)
                for m in range(2):
                    at_ = 2 * LORA + P * m
                    mm = nc.tensor.matmul(PS[:, 4 + m, 0:L], LORA1[:, k, at_:at_ + P], MIXED[:, 0, k],
                                          start=(k == 0), stop=(k == KD - 1))
            mm.then_inc(lora_summed, 1)

        def shift_pool(pool):
            for k in range(KD):
                pool.wait_ge(ln_shifted, k + 1)
                nc.gpsimd.tensor_tensor(XX[:, k, 1:L], X[:, k, 0:L - 1], X[:, k, 1:L], ALU.subtract)\
                  .then_inc(xx_made, 1)
                nc.gpsimd.tensor_tensor(XX[:, k, 0:1], ZERO[:], X[:, k, 0:1], ALU.subtract).then_inc(xx_made, 1)

        def lora_dve(dve):
            for k in range(3):
                scale_dve(dve, 0, k, ALL)
            for k in range(KD):
                if k + 3 < KD:
                    scale_dve(dve, 0, k + 3, ALL)
                dve.wait_ge(xx_made, 2 * k + 2)
                mix_tile(dve, MIXED[:, 0, k], MIX_W, k).then_inc(lora_mixed, 1)
                mix_tile(dve, MIXED[:, 1, k], MIX_A, k).then_inc(lora_mixed, 1)
            for k in range(KD):
                dve.wait_ge(lora_summed, k + 1)
                mix_tile(dve, MIXED[:, 0, k], MIX_G, k).then_inc(lora_mixed, 1)

        def lora_act(act):
            act.wait_ge(lora_summed, KD)
            nc.scalar.activation(LH[0:LORA, 0, :], PS[0:LORA, 6, 0:L], ACT.Tanh).then_inc(lora_taken, 1)
            nc.scalar.activation(LH[0:LORA, 1, :], PS[0:LORA, 7, 0:L], ACT.Copy).then_inc(lora_taken, 1)
            act.wait_ge(lora_summed, KD + 1)
            nc.scalar.activation(LH[:, 2:4, :], PS[:, 4:6, 0:L], ACT.Sigmoid).then_inc(lora_taken, 1)

        PARTS = 8
        PK = KD // PARTS

        def ln_pe(pe, n, ph):
            N = ph.n
            sum_residual(pe, ph, ph.steps - 1, 1, stop=True).then_inc(ln_mean, 1)
            for q in range(PARTS):
                pe.wait_ge(ln_squared, PARTS * n + q + 1)
                for k in range(q * PK, (q + 1) * PK):
                    mm = nc.tensor.matmul(PS[:, 5, 0:N], C["ones_mean"][:], SQ[:, k, 0:N],
                                          start=(k == 0), stop=(k == KD - 1))
            mm.then_inc(ln_var, 1)

        def ln_act(act, n, tok, between=None):
            N = tok.stop - tok.start
            for q in range(PARTS):
                act.wait_ge(ln_centred, PARTS * n + q + 1)
                nc.scalar.activation(SQ[:, q * PK:(q + 1) * PK, 0:N], X[:, q * PK:(q + 1) * PK, tok], ACT.Square)\
                  .then_inc(ln_squared, 1)
            if between:
                between()
            act.wait_ge(zero_set, 1)
            nc.scalar.activation(ROOT[:], ZERO[:], ACT.Sqrt).then_inc(root_loaded, 1)
            act.wait_ge(ln_eps_added, n + 1)
            nc.scalar.activation(RS[:, 0:N], RS[:, 0:N], ACT.Sqrt).then_inc(ln_rooted, 1)

        def shift_act(act, n, k, tok):
            act.wait_ge(ln_scaled, KD * n + k + 1)
            nc.scalar.activation(X[:, k, tok], X[:, k, tok], ACT.Identity, bias=PAR[:, V_LN_B + n, k:k + 1])\
              .then_inc(ln_shifted, 1)

        def ln_dve(dve, n, tok, between=None):
            N = tok.stop - tok.start
            dve.wait_ge(ln_mean, n + 1)
            for q in range(PARTS):
                xq = X[:, q * PK:(q + 1) * PK, tok]
                nc.vector.tensor_tensor(xq, xq, PS[:, 4:5, 0:N].to_broadcast((P, PK, N)), ALU.subtract)\
                  .then_inc(ln_centred, 1)
            if between:
                between()
            dve.wait_ge(ln_var, n + 1)
            nc.vector.tensor_scalar(RS[:, 0:N], PS[:, 5, 0:N], LN_EPS, None, ALU.add).then_inc(ln_eps_added, 1)
            dve.wait_ge(ln_rooted, n + 1)
            nc.vector.reciprocal(RS[:, 0:N], RS[:, 0:N]).then_inc(ln_inverted, 1)
            dve.wait_ge(ln_inverted, n + 1)

        def scale_dve(dve, n, k, tok):
            nc.vector.scalar_tensor_tensor(out=X[:, k, tok], in0=X[:, k, tok], scalar=PAR[:, V_LN_G + n, k:k + 1],
                                           in1=RS[:, 0:tok.stop - tok.start], op0=ALU.mult, op1=ALU.mult)\
              .then_inc(ln_scaled, 1)

        def x_hi_act(act, f, k, tok):
            nc.scalar.activation(XA[:, 0, k, tok], X[:, k, tok], ACT.Copy).then_inc(x_hi_made, 1)

        def x_lo_dve(dve, f, k, tok):
            dve.wait_ge(x_hi_made, KD * f + k + 1)
            nc.vector.tensor_tensor(XA[:, 1, k, tok], X[:, k, tok], XA[:, 0, k, tok].bitcast(F32), ALU.subtract)\
              .then_inc(x_lo_made, 1)

        OUT_BY_DVE = 5

        def out_copied(i):
            return (out_copied_dve, i + 1) if i < OUT_BY_DVE else (out_copied_act, i + 1 - OUT_BY_DVE)

        def out_piece(i):
            return OUT[:, i % 2, 4 * P * (i // 2):4 * P * (i // 2 + 1)]

        TOK_ROWS = [P, P, L - 2 * P]

        def turned_source(i):
            kg, tt = i // 3, i % 3
            return PS[:, 4 + i % 4].rearrange("p (k t) -> p k t", k=4)[:, :, 0:TOK_ROWS[tt]]

        def turned_target(i):
            kg, tt = i // 3, i % 3
            return X[:, 4 * kg:4 * kg + 4, P * tt:P * tt + TOK_ROWS[tt]]

        def wait_for_x(eng, kg):
            eng.wait_ge(turned_copied[0], (3 * kg + 4) // 2)
            eng.wait_ge(turned_copied[1], (3 * kg + 3) // 2)

        def y_hi_act(act, k):
            nc.scalar.activation(YA[:, 0, k], KVR[:, 2, k, REAL], ACT.Copy).then_inc(y_hi_made, 1)

        def y_lo_dve(dve, k):
            dve.wait_ge(y_hi_made, k + 1)
            nc.vector.tensor_tensor(YA[:, 1, k], KVR[:, 2, k, REAL], YA[:, 0, k].bitcast(F32), ALU.subtract)\
              .then_inc(y_lo_made, 1)

        names = """pair_done lora_landed vectors_picked zw_made za_made zg_made gate_copied w_tanh a_tanh
            decay_made a_made k_squared norm_summed norm_eps norm_rooted norm_inverted kk_made cum_made e_made
            ei_made ac_made rc_made b_plain ka_made k2_made b_doubled a_doubled k_doubled v_doubled bonus_rk_made
            turned_ready turned_taken gram_ready lt_masked gak_masked grb_masked grk_masked gram_taken
            tt_turned ti_made tt_off tt_first z_ready z_masked t_ready tt_added
            rhs_ready rhs_copied u_ready u_copied y_ready s_ready s_made s_decayed y_taken
            gn_mean gn_centred gn_squared gn_var gn_eps gn_rooted gn_inverted gn_scaled
            bonus_ready bonus_scaled bonus_added blocks_cleared pads_cleared ones_set""".split()
        S = {n: sem(n) for n in names}
        NI = KD // 2
        NL = len(LEVELS)
        NY = NCH - 1
        TURNS = [list(range(c, min(c + 4, 3 * NCH))) for c in range(0, 3 * NCH, 4)]
        FLAT = PS[:].rearrange("p b n -> p (b n)")

        def flat(t):
            return t[:].rearrange("p c t -> p (c t)")

        def real(t):
            return flat(t)[:, PAD:LP]

        def matrix(t, c):
            return t[:, c].rearrange("p h t -> p (h t)")

        def square_of(t):
            return t[:].rearrange("p h t -> p (h t)")

        def spread(ap):
            return ap.rearrange("p c (o t) -> p c o t", o=1).to_broadcast((P, ap.shape[1], 2, CHUNK))

        def masked(name, n=NCH):
            return C[name][:].rearrange("p (o h t) -> p o h t", o=1, h=2).to_broadcast((P, n, 2, CHUNK))

        def incl():
            return C["incl"][:].rearrange("p (o t) -> p o t", o=1).to_broadcast((P, NY, CHUNK))

        def bank(q, b, n):
            return PS[:, 4 * q + b, 0:n]

        def product(q, n, c0=0):
            at_ = 2048 * q + 2 * LP * n
            return FLAT[:, at_ + P * c0:at_ + 2 * LP].rearrange("p (c h t) -> p c h t", h=2, t=CHUNK)

        def each_chunk(q, n, lhs, rhs, c0=0):
            for c in range(c0, NCH):
                at_ = 2048 * q + 2 * LP * n + P * c
                mm = nc.tensor.matmul(FLAT[:, at_:at_ + P], lhs(c), rhs(c), start=True, stop=True)
            return mm

        def first_chunk(level):
            return 0 if LEVELS[level] < N_META else 1

        def pair_chunks(which, p):
            return KVR[:, which, p, REAL].rearrange("p (c t) -> p c t", c=NY)

        W0, A0 = NVEC, NVEC + 1

        def count(i, q, step=0, steps=1):
            return 2 * steps * i + 2 * step + q + 1

        def iterations(eng, middle):
            middle(0, 0, True, False)
            with eng.Fori(0, NI // 2 - 1) as m:
                middle(2 * m + 1, 1, False, False)
                middle(2 * m + 2, 0, False, False)
            middle(NI - 1, 1, False, True)

        def scan_sp(sp):
            def second_lora(i):
                cols = bass.ds(2 * P * i, 2 * P)
                sp.dma_start(LW[0:LORA, 0, :], w["rwkv_w2"][:, cols]).then_inc(S["lora_landed"], 16)
                sp.dma_start(LW[0:LORA, 1, :], w["rwkv_a2"][:, cols]).then_inc(S["lora_landed"], 16)
                sp.dma_start(LW[:, 2:4, :], w["rwkv_g2"].rearrange("(k p) n -> p k n", p=P)[:, :, cols])\
                  .then_inc(S["lora_landed"], 16)

            sp.wait_ge(blocks_multiplied, proj_v.end)
            second_lora(0)
            with sp.Fori(1, NI) as i:
                sp.wait_ge(S["zg_made"], count(i - 1, 1))
                second_lora(i)

        def scan_act(act):
            A = nc.scalar.activation

            def w_tanh(f, q):
                act.wait_ge(S["vectors_picked"], count(f, q))
                act.wait_ge(S["zw_made"], count(f, q))
                A(real(LWD[q]), bank(q, 3, L), ACT.Tanh, bias=PP[q][:, W0:W0 + 1], scale=0.5).then_inc(S["w_tanh"], 1)

            def a_tanh(f, q):
                act.wait_ge(S["za_made"], count(f, q))
                A(real(AA[q]), bank(q, 3, L), ACT.Tanh, bias=PP[q][:, A0:A0 + 1], scale=0.5).then_inc(S["a_tanh"], 1)

            def k_squared(f, q):
                act.wait_ge(S["vectors_picked"], count(f, q))
                A(real(SQK[q]), KVR[:, 0, 2 * f + q, :], ACT.Square, scale=PP[q][:, V_KK:V_KK + 1])\
                    .then_inc(S["k_squared"], 1)

            def exps(f, q, parity):
                act.wait_ge(S["cum_made"], count(f, q))
                A(E[parity][q][:, :, 1:CHUNK + 1], CUM[q][:], ACT.Exp).then_inc(S["e_made"], 1)
                A(flat(EI[q]), flat(CUM[q]), ACT.Exp, scale=-1.0).then_inc(S["ei_made"], 1)

            def norm_root(f, q):
                act.wait_ge(S["norm_eps"], count(f, q))
                A(real(RN[q]), real(RN[q]), ACT.Sqrt).then_inc(S["norm_rooted"], 1)

            def gate(f, q, parity):
                act.wait_ge(S["zg_made"], count(f, q))
                A(GG[parity][q], bank(q, 3, SEQ), ACT.Copy).then_inc(S["gate_copied"], 1)

            def v_double(f, q):
                for h in range(2):
                    rows = slice(HEAD * h, HEAD * (h + 1))
                    A(VBD[q][rows, 0, h, PAD:CHUNK], KVR[rows, 1, 2 * f + q, 0:N_META], ACT.Copy)\
                        .then_inc(S["v_doubled"], 1)
                    A(VBD[q][rows, 1:NCH, h, :], KVR[rows, 1, 2 * f + q, REAL].rearrange("p (c t) -> p c t", c=NY),
                      ACT.Copy).then_inc(S["v_doubled"], 1)

            def take_gram(i, q):
                act.wait_ge(S["lt_masked"], count(i, q))
                A(RAW_RB[q], product(q, 1)[:, 1:NCH, 1], ACT.Copy).then_inc(S["gram_taken"], 1)
                A(RAW_K[q], product(q, 2), ACT.Copy).then_inc(S["gram_taken"], 1)

            def take_t(i, q, l):
                c0 = first_chunk(l)
                act.wait_ge(S["tt_turned"], count(i, q, l, NL))
                A(TI[q][:, c0:NCH], product(q, 1, c0), ACT.Copy).then_inc(S["ti_made"], 1)

            def take_turned(i, q, r):
                n = len(TURNS[r])
                if r in (1, 2):
                    act.wait_ge(S["grb_masked" if r == 1 else "grk_masked"], count(i, q))
                act.wait_ge(S["turned_ready"], count(i, q, r, len(TURNS)))
                to = TR[q][:, TURNS[r][0]:TURNS[r][-1] + 1]
                A(to.rearrange("p c h t -> p (c h t)"), bank(q, 3, P * n), ACT.Copy)\
                    .then_inc(S["turned_taken"], 1)

            def gn_square(j, q):
                act.wait_ge(S["gn_centred"], count(j, q))
                A(YQ[q], YC[q], ACT.Square).then_inc(S["gn_squared"], 1)

            def gn_root(j, q):
                act.wait_ge(S["gn_eps"], count(j, q))
                A(RG[q], RG[q], ACT.Sqrt).then_inc(S["gn_rooted"], 1)

            def middle(i, parity, first, last):
                def every(step, *arguments):
                    for q in LANES:
                        step(arguments[0], q, *arguments[1:])
                for q in LANES:
                    take_gram(i, q)
                    take_t(i, q, 0)
                every(take_turned, i, 0)
                every(take_t, i, 1)
                if not first:
                    every(gn_square, i - 1)
                every(take_turned, i, 1)
                every(take_t, i, 2)
                if not first:
                    every(gn_root, i - 1)
                every(take_turned, i, 2)
                every(take_t, i, 3)
                if not last:
                    every(w_tanh, i + 1)
                every(take_turned, i, 3)
                every(take_t, i, 4)
                if not last:
                    every(a_tanh, i + 1)
                    every(k_squared, i + 1)
                    every(exps, i + 1, 1 - parity)
                for c in range(NCH):
                    for q in LANES:
                        act.wait_ge(S["rhs_ready"], count(i, q, c, NCH))
                        A(square_of(RHS[q]), bank(q, 0, P), ACT.Copy).then_inc(S["rhs_copied"], 1)
                    for q in LANES:
                        act.wait_ge(S["u_ready"], count(i, q, c, NCH))
                        A(square_of(UU[q]), bank(q, 0, P), ACT.Copy).then_inc(S["u_copied"], 1)
                    if c == 0 and not last:
                        every(norm_root, i + 1)
                    if c == 1 and not last:
                        if not first:
                            act.wait_ge(S["pair_done"], count(i - 1, 1))
                        every(gate, i + 1, 1 - parity)
                    if c in (2, 3) and not last:
                        v_double(i + 1, c - 2)
                for q in LANES:
                    act.wait_ge(S["y_ready"], count(i, q, NY - 1, NY))
                    if not first:
                        act.wait_ge(S["pair_done"], count(i - 1, q))
                    A(YC[q].rearrange("p (c t) -> p c t", c=NY),
                      bank(q, 2, NY * P).rearrange("p (c h t) -> p c h t", c=NY, h=2)[:, :, 1], ACT.Copy)\
                        .then_inc(S["y_taken"], 1)

            act.wait_ge(S["pads_cleared"], PADS)
            act.wait_ge(S["blocks_cleared"], BLOCKS)
            act.wait_ge(S["ones_set"], 4)
            for step in (w_tanh, a_tanh, k_squared):
                for q in LANES:
                    step(0, q)
            for q in LANES:
                exps(0, q, 0)
            for q in LANES:
                v_double(0, q)
            for q in LANES:
                norm_root(0, q)
            for q in LANES:
                gate(0, q, 0)
            iterations(act, middle)
            split_hi(act, w_o, 0, 0, 0)
            for q in LANES:
                gn_square(NI - 1, q)
            for k in range(KB):
                y_hi_act(act, k)
            for q in LANES:
                gn_root(NI - 1, q)
            split_hi(act, w_o, 0, 0, 1)
            for k in range(KB, 2 * KB):
                y_hi_act(act, k)
            split_hi(act, w_o, 0, 0, 2)
            for k in range(2 * KB, KD - 2):
                y_hi_act(act, k)
            act.wait_ge(S["pair_done"], KD)
            for k in range(KD - 2, KD):
                y_hi_act(act, k)

        PADS, BLOCKS = 8, 6
        RAW_RB = [TR[q][:, NCH:NCH + 2].rearrange("p a h t -> p (a h) t") for q in LANES]
        RAW_K = [TR[q][:, 2 * NCH:3 * NCH] for q in LANES]

        def scan_pool(pool):
            PT = nc.gpsimd.tensor_tensor

            def k_double(f, q):
                pool.wait_ge(S["k2_made"], count(f, q))
                pool.wait_ge(S["ei_made"], count(f, q))
                for h in range(2):
                    rows = slice(HEAD * h, HEAD * (h + 1))
                    PT(KBD[q][rows, :, h, :], K2[q][rows], EI[q][rows], ALU.mult).then_inc(S["k_doubled"], 1)
                pool.wait_ge(S["k_doubled"], 2 * count(f, q))

            def make_r(f, q, parity):
                PT(AR[parity][q][:, 1:NCH, 1, :], pair_chunks(2, 2 * f + q), E[parity][q][:, 1:NCH, 1:CHUNK + 1],
                   ALU.mult).then_inc(S["rc_made"], 1)

            def make_b(f, q):
                pool.wait_ge(S["kk_made"], count(f, q))
                PT(real(TH[q]), real(KK[q]), real(AA[q]), ALU.mult).then_inc(S["b_plain"], 1)

            def a_double(f, q, parity):
                pool.wait_ge(S["ac_made"], count(f, q))
                PT(ABD[q][:], spread(AR[parity][q][:, :, 0, :]), masked("bd"), ALU.mult).then_inc(S["a_doubled"], 1)

            def put_out(j, q, parity):
                pool.wait_ge(S["bonus_added"], count(j, q))
                pool.wait_ge(S["gate_copied"], count(j, q))
                PT(KVR[:, 2, 2 * j + q, REAL], YC[q], GG[parity][q], ALU.mult).then_inc(S["pair_done"], 1)

            def mask_gram(i):
                for q in LANES:
                    pool.wait_ge(S["gram_taken"], 2 * count(i, q))
                    PT(GR[q][:, 1:NCH, 1], RAW_RB[q], incl(), ALU.mult).then_inc(S["grb_masked"], 1)
                for q in LANES:
                    PT(GAK[q][:], spread(RAW_K[q][:, :, 0]), masked("bd_strict"), ALU.mult)\
                        .then_inc(S["gak_masked"], 1)
                    PT(GR[q][:, 1:NCH, 2], RAW_K[q][:, 1:NCH, 1], incl(), ALU.mult).then_inc(S["grk_masked"], 1)

            def middle(i, parity, first, last):
                mask_gram(i)
                if not first:
                    for q in LANES:
                        put_out(i - 1, q, 1 - parity)
                for c in range(1, NY):
                    for q in LANES:
                        end = E[parity][q][:, c, CHUNK:CHUNK + 1].rearrange("p (o t) -> p o t", o=1)
                        pool.wait_ge(S["s_made"], count(i, q, c - 1, NY))
                        PT(SW[q][:], SS[q][:], end.to_broadcast((P, 2, CHUNK)), ALU.mult).then_inc(S["s_decayed"], 1)
                    if not last:
                        if c < 3:
                            pool.wait_ge(S["s_decayed"], count(i, 1, c - 1, NY - 1))
                            k_double(i + 1, c - 1)
                        else:
                            for q in LANES:
                                make_r(i + 1, q, 1 - parity)
                            for q in LANES:
                                make_b(i + 1, q)
                if not last:
                    for q in LANES:
                        pool.wait_ge(S["rhs_ready"], count(i, q, NCH - 1, NCH))
                        a_double(i + 1, q, 1 - parity)

            pool.wait_ge(const_landed, 16 * (len(CONST_COLUMNS) - 1))
            pool.wait_ge(blocks_multiplied, proj_v.end)
            for t in (*LWD, *TH, *KK, *K2):
                nc.gpsimd.memset(t[:, 0, 0:PAD], 0.0).then_inc(S["pads_cleared"], 1)
            for t in (*BBD, *KBD, *VBD):
                nc.gpsimd.memset(t[:], 0.0).then_inc(S["blocks_cleared"], 1)
            pool.wait_ge(blocks_multiplied, proj_r.end)
            for t in (*E[0], *E[1]):
                nc.gpsimd.memset(t[:, :, 0:1], 1.0).then_inc(S["ones_set"], 1)
            for t in (*AR[0], *AR[1]):
                nc.gpsimd.memset(t[:, 0, 1, :], 0.0).then_inc(S["blocks_cleared"], 1)
            for t in GR:
                nc.gpsimd.memset(t[:, :, 0, :], 0.0).then_inc(S["blocks_cleared"], 1)
            pool.wait_ge(S["blocks_cleared"], BLOCKS + 6)
            for q in LANES:
                k_double(0, q)
            for q in LANES:
                make_r(0, q, 0)
            for q in LANES:
                make_b(0, q)
            for q in LANES:
                a_double(0, q, 0)
            iterations(pool, middle)
            for q in LANES:
                put_out(NI - 1, q, 1)

        def scan_pe(pe):
            M = nc.tensor.matmul

            def make_zw(f, q):
                M(bank(q, 3, L), LW[0:LORA, 0, P * q:P * (q + 1)], LH[0:LORA, 0, :], start=True, stop=True)\
                    .then_inc(S["zw_made"], 1)

            def make_za(f, q):
                pe.wait_ge(S["w_tanh"], count(f, q))
                M(bank(q, 3, L), LW[0:LORA, 1, P * q:P * (q + 1)], LH[0:LORA, 1, :], start=True, stop=True)\
                    .then_inc(S["za_made"], 1)

            def sum_norm(f, q):
                pe.wait_ge(S["a_tanh"], count(f, q))
                pe.wait_ge(S["k_squared"], count(f, q))
                M(bank(q, 3, L), C["head_sum"][:], real(SQK[q]), start=True, stop=True).then_inc(S["norm_summed"], 1)

            def make_zg(f, q):
                pe.wait_ge(S["norm_eps"], count(f, q))
                for k in range(2):
                    mm = M(bank(q, 3, SEQ), LW[:, 2 + k, P * q:P * (q + 1)], LH[:, 2 + k, REAL],
                           start=(k == 0), stop=(k == 1))
                mm.then_inc(S["zg_made"], 1)

            def sum_bonus(f, q):
                pe.wait_ge(S["gate_copied"], count(f, q))
                pe.wait_ge(S["bonus_rk_made"], count(f, q))
                M(bank(q, 3, SEQ), C["head_sum"][:], flat(SQK[q])[:, CHUNK:LP], start=True, stop=True)\
                    .then_inc(S["bonus_ready"], 1)

            def gn_mean(j, q):
                pe.wait_ge(S["y_taken"], count(j, q))
                M(bank(q, 3, SEQ), C["head_mean"][:], YC[q], start=True, stop=True).then_inc(S["gn_mean"], 1)

            def gn_var(j, q):
                pe.wait_ge(S["gn_squared"], count(j, q))
                M(bank(q, 3, SEQ), C["head_mean"][:], YQ[q], start=True, stop=True).then_inc(S["gn_var"], 1)

            def turn(i, q, r):
                if r == 0:
                    pe.wait_ge(S["v_doubled"], 4 * count(i, q))
                else:
                    pe.wait_ge(S["turned_taken"], count(i, q, r - 1, len(TURNS)))
                for j, n in enumerate(TURNS[r]):
                    mm = nc.tensor.transpose(bank(q, 3, 512)[:, P * j:P * (j + 1)],
                                             matrix((VBD, BBD, KBD)[n // NCH][q], n % NCH), C["ident"][:])
                mm.then_inc(S["turned_ready"], 1)

            def gram(i, q, parity, first):
                if not first:
                    pe.wait_ge(S["y_taken"], count(i - 1, q))
                pe.wait_ge(S["b_doubled"], 2 * count(i, q))
                pe.wait_ge(S["rc_made"], count(i, q))
                pe.wait_ge(S["ac_made"], count(i, q))
                each_chunk(q, 1, lambda c: matrix(BBD[q], c), lambda c: matrix(AR[parity][q], c))
                pe.wait_ge(S["bonus_scaled"], count(i, q))
                pe.wait_ge(S["k_doubled"], 2 * count(i, q))
                each_chunk(q, 2, lambda c: matrix(KBD[q], c), lambda c: matrix(AR[parity][q], c))\
                    .then_inc(S["gram_ready"], 1)

            def beside(i, l, half, first, last):
                for q in LANES:
                    if (l, half) == (0, 1) and not first:
                        pe.wait_ge(S["turned_taken"], count(i, q, 0, len(TURNS)))
                        gn_mean(i - 1, q)
                    if (l, half) == (1, 0):
                        if not first:
                            pe.wait_ge(S["gn_centred"], count(i - 1, q))
                        turn(i, q, 1)
                    if (l, half) == (1, 1) and not first:
                        pe.wait_ge(S["turned_taken"], count(i, q, 1, len(TURNS)))
                        gn_var(i - 1, q)
                    if (l, half) == (2, 0):
                        if not first:
                            pe.wait_ge(S["gn_eps"], count(i - 1, q))
                        turn(i, q, 2)
                    if (l, half) == (2, 1) and not last:
                        pe.wait_ge(S["lora_landed"], 48 * (i + 1) + 48)
                        pe.wait_ge(S["turned_taken"], count(i, q, 2, len(TURNS)))
                        make_zw(i + 1, q)
                    if (l, half) == (3, 0):
                        if not last:
                            pe.wait_ge(S["w_tanh"], count(i + 1, q))
                        turn(i, q, 3)
                    if (l, half) == (3, 1) and not last:
                        pe.wait_ge(S["turned_taken"], count(i, q, 3, len(TURNS)))
                        make_za(i + 1, q)
                    if (l, half) == (4, 1) and not last:
                        sum_norm(i + 1, q)

            def turn_tt(i, q, c0):
                for c in range(c0, NCH):
                    at_ = 2048 * q + 2 * LP + P * c
                    mm = nc.tensor.transpose(FLAT[:, at_:at_ + P], matrix(TT[q], c), C["ident"][:])
                mm.then_inc(S["tt_turned"], 1)

            def levels(i, first, last):
                for l in range(NL):
                    c0 = first_chunk(l)
                    for q in LANES:
                        if l == 0:
                            pe.wait_ge(S["gram_taken"], 2 * count(i, q))
                            pe.wait_ge(S["tt_first"], count(i, q))
                            turn_tt(i, q, 0)
                            turn(i, q, 0)
                        pe.wait_ge(S["ti_made"], count(i, q, l, NL))
                        each_chunk(q, 0, lambda c: matrix(LT[q], c), lambda c: matrix(TI[q], c), c0)\
                            .then_inc(S["z_ready"], 1)
                    beside(i, l, 0, first, last)
                    for q in LANES:
                        pe.wait_ge(S["z_masked"], count(i, q, l, NL))
                        each_chunk(q, 0, lambda c: matrix(ZZ[q], c), lambda c: matrix(TT[q], c), c0)\
                            .then_inc(S["t_ready"], 1)
                    for q in LANES:
                        if l < NL - 1:
                            pe.wait_ge(S["tt_added"], count(i, q, l, NL))
                            turn_tt(i, q, first_chunk(l + 1))
                        if q == 0:
                            beside(i, l, 1, first, last)

            def chunks(i, parity, last):
                V, B, K = 0, NCH, 2 * NCH
                for c in range(NCH):
                    y = [bank(q, 2, NY * P)[:, P * (c - 1):P * c] for q in LANES]
                    for q in LANES:
                        if c == 0:
                            pe.wait_ge(S["turned_taken"], count(i, q, len(TURNS) - 1, len(TURNS)))
                            pe.wait_ge(S["grk_masked"], count(i, q))
                            pe.wait_ge(S["tt_added"], count(i, q, NL - 1, NL))
                        mm = M(bank(q, 0, P), matrix(GAK[q], c), matrix(TR[q], V + c), start=True, stop=(c == 0))
                        if c == 0:
                            mm.then_inc(S["rhs_ready"], 1)
                        else:
                            pe.wait_ge(S["a_doubled"], count(i, q))
                            pe.wait_ge(S["s_made"], count(i, q, c - 1, NY))
                            M(bank(q, 0, P), matrix(ABD[q], c), square_of(SS[q]), start=False, stop=True)\
                                .then_inc(S["rhs_ready"], 1)
                    for q in LANES:
                        if c:
                            M(y[q], square_of(SS[q]), matrix(AR[parity][q], c), start=True, stop=False)
                            M(y[q], matrix(TR[q], V + c), GR[q][:, c, 1:3].rearrange("p g t -> p (g t)"),
                              start=False, stop=False)
                        pe.wait_ge(S["rhs_copied"], count(i, q, c, NCH))
                        M(bank(q, 0, P), matrix(TT[q], c), square_of(RHS[q]), start=True, stop=True)\
                            .then_inc(S["u_ready"], 1)
                    for q in LANES:
                        if c < NY:
                            M(bank(q, 1, P), matrix(TR[q], K + c), matrix(TR[q], V + c), start=True, stop=False)
                        pe.wait_ge(S["u_copied"], count(i, q, c, NCH))
                        if c < NY:
                            M(bank(q, 1, P), matrix(TR[q], B + c), square_of(UU[q]), start=False, stop=True)\
                                .then_inc(S["s_ready"], 1)
                        if c:
                            M(y[q], square_of(UU[q]), GR[q][:, c, 0:2].rearrange("p g t -> p (g t)"),
                              start=False, stop=True).then_inc(S["y_ready"], 1)
                    if not last:
                        for q in LANES:
                            if c == 0:
                                make_zg(i + 1, q)
                            if c == 3:
                                sum_bonus(i + 1, q)

            def middle(i, parity, first, last):
                for q in LANES:
                    gram(i, q, parity, first)
                levels(i, first, last)
                chunks(i, parity, last)

            pe.wait_ge(lora_taken, 3)
            pe.wait_ge(projected, proj_r.projected0 + KD // 2)
            pe.wait_ge(S["lora_landed"], 48)
            for step in (make_zw, make_za, sum_norm, make_zg, sum_bonus):
                for q in LANES:
                    step(0, q)
            iterations(pe, middle)
            for step in (gn_mean, gn_var):
                for q in LANES:
                    step(NI - 1, q)
            for q in LANES:
                pe.wait_ge(S["gn_eps"], count(NI - 1, q))

        def scan_dve(dve):
            TTEN, TS, STT = nc.vector.tensor_tensor, nc.vector.tensor_scalar, nc.vector.scalar_tensor_tensor

            def pick(f, q):
                nc.vector.tensor_copy(PP[q][:, 0:NVEC], PAR[:, :, 2 * f + q])
                nc.vector.tensor_copy(PP[q][:, NVEC:NVEC + 2], HALF[:, :, 2 * f + q]).then_inc(S["vectors_picked"], 1)

            def decay(f, q):
                dve.wait_ge(S["w_tanh"], count(f, q))
                TS(real(LWD[q]), real(LWD[q]), -DECAY / 2, -DECAY / 2, ALU.mult, ALU.add).then_inc(S["decay_made"], 1)

            def cumulate(f, q):
                dve.wait_ge(S["decay_made"], count(f, q))
                nc.vector.tensor_tensor_scan(flat(CUM[q]), C["restart"][:], flat(LWD[q]), 0.0,
                                             ALU.mult, ALU.add).then_inc(S["cum_made"], 1)

            def halve_a(f, q):
                dve.wait_ge(S["a_tanh"], count(f, q))
                TS(real(AA[q]), real(AA[q]), 0.5, 0.5, ALU.mult, ALU.add).then_inc(S["a_made"], 1)

            def scale_ka(f, q):
                dve.wait_ge(S["a_made"], count(f, q))
                dve.wait_ge(S["vectors_picked"], count(f, q))
                TS(real(TH[q]), real(AA[q]), 1.0, PP[q][:, V_KA:V_KA + 1], ALU.subtract, ALU.mult)\
                    .then_inc(S["ka_made"], 1)

            def make_k2(f, q):
                dve.wait_ge(S["ka_made"], count(f, q))
                STT(out=real(K2[q]), in0=real(TH[q]), scalar=1.0, in1=KVR[:, 0, 2 * f + q, :],
                    op0=ALU.add, op1=ALU.mult).then_inc(S["k2_made"], 1)

            def norm_eps(f, q):
                dve.wait_ge(S["norm_summed"], count(f, q))
                dve.wait_ge(S["cum_made"], count(f, q))
                TS(real(RN[q]), bank(q, 3, L), 1e-12, None, ALU.add).then_inc(S["norm_eps"], 1)

            def norm_invert(f, q):
                dve.wait_ge(S["norm_rooted"], count(f, q))
                nc.vector.reciprocal(real(RN[q]), real(RN[q])).then_inc(S["norm_inverted"], 1)

            def make_kk(f, q):
                dve.wait_ge(S["norm_inverted"], count(f, q))
                STT(out=real(KK[q]), in0=KVR[:, 0, 2 * f + q, :], scalar=PP[q][:, V_KK:V_KK + 1],
                    in1=real(RN[q]), op0=ALU.mult, op1=ALU.mult).then_inc(S["kk_made"], 1)

            def bonus_rk(f, q):
                dve.wait_ge(S["norm_eps"], count(f, q))
                dve.wait_ge(S["k2_made"], count(f, q))
                STT(out=SQK[q][:, 1:NCH], in0=pair_chunks(2, 2 * f + q), scalar=PP[q][:, V_RK:V_RK + 1],
                    in1=K2[q][:, 1:NCH], op0=ALU.mult, op1=ALU.mult).then_inc(S["bonus_rk_made"], 1)

            def make_a(f, q, parity):
                dve.wait_ge(S["kk_made"], count(f, q))
                dve.wait_ge(S["e_made"], count(f, q))
                STT(out=AR[parity][q][:, :, 0, :], in0=KK[q][:], scalar=-1.0, in1=E[parity][q][:, :, 0:CHUNK],
                    op0=ALU.mult, op1=ALU.mult).then_inc(S["ac_made"], 1)

            def b_double(f, q):
                dve.wait_ge(S["ei_made"], count(f, q))
                dve.wait_ge(S["b_plain"], count(f, q))
                for h in range(2):
                    rows = slice(HEAD * h, HEAD * (h + 1))
                    TTEN(BBD[q][rows, :, h, :], TH[q][rows], EI[q][rows], ALU.mult).then_inc(S["b_doubled"], 1)

            def bonus(f, q, parity):
                dve.wait_ge(S["bonus_ready"], count(f, q))
                TTEN(BN[parity][q], KVR[:, 1, 2 * f + q, REAL], bank(q, 3, SEQ), ALU.mult)\
                    .then_inc(S["bonus_scaled"], 1)

            def gn_centre(j, q):
                dve.wait_ge(S["gn_mean"], count(j, q))
                TTEN(YC[q], YC[q], bank(q, 3, SEQ), ALU.subtract).then_inc(S["gn_centred"], 1)

            def gn_eps(j, q):
                dve.wait_ge(S["gn_var"], count(j, q))
                TS(RG[q], bank(q, 3, SEQ), GN_EPS, None, ALU.add).then_inc(S["gn_eps"], 1)

            def gn_invert(j, q):
                dve.wait_ge(S["gn_rooted"], count(j, q))
                nc.vector.reciprocal(RG[q], RG[q]).then_inc(S["gn_inverted"], 1)

            def gn_scale(j, q):
                dve.wait_ge(S["gn_inverted"], count(j, q))
                STT(out=YC[q], in0=YC[q], scalar=PAR[:, V_GN_G, bass.ds(2 * j + q, 1)], in1=RG[q],
                    op0=ALU.mult, op1=ALU.mult).then_inc(S["gn_scaled"], 1)

            def add_bonus(j, q, parity):
                dve.wait_ge(S["gn_scaled"], count(j, q))
                dve.wait_ge(S["bonus_scaled"], count(j, q))
                STT(out=YC[q], in0=YC[q], scalar=PAR[:, V_GN_B, bass.ds(2 * j + q, 1)], in1=BN[parity][q],
                    op0=ALU.add, op1=ALU.add).then_inc(S["bonus_added"], 1)

            def mask_gram(i):
                for q in LANES:
                    dve.wait_ge(S["gram_ready"], count(i, q))
                    TTEN(LT[q][:], spread(product(q, 1)[:, :, 0]), masked("bd_strict"), ALU.mult)\
                        .then_inc(S["lt_masked"], 1)
                    first_tt(i, q)

            def first_tt(i, q):
                dve.wait_ge(S["lt_masked"], count(i, q))
                TTEN(TT[q][:], LT[q][:], masked("offT1"), ALU.mult).then_inc(S["tt_off"], 1)
                dve.wait_ge(S["tt_off"], count(i, q))
                TTEN(TT[q][:], TT[q][:], masked("bd_i"), ALU.add).then_inc(S["tt_first"], 1)

            def every(step, *arguments):
                for q in LANES:
                    step(arguments[0], q, *arguments[1:])

            def beside(i, l, half, parity, first, last):
                if (l, half) == (0, 1):
                    if not first:
                        every(gn_centre, i - 1)
                    if not last:
                        every(pick, i + 1)
                if (l, half) == (1, 1) and not first:
                    every(gn_eps, i - 1)
                if (l, half) == (2, 1) and not first:
                    gn_invert(i - 1, 0)
                if (l, half) == (3, 0) and not last:
                    every(decay, i + 1)
                    every(cumulate, i + 1)
                if (l, half) == (3, 1) and not first:
                    gn_invert(i - 1, 1)
                    gn_scale(i - 1, 0)
                if (l, half) == (4, 0):
                    if not first:
                        gn_scale(i - 1, 1)
                        every(add_bonus, i - 1, 1 - parity)
                    if not last:
                        every(halve_a, i + 1)

            def levels(i, parity, first, last):
                for l in range(NL):
                    c0 = first_chunk(l)
                    for q in LANES:
                        dve.wait_ge(S["z_ready"], count(i, q, l, NL))
                        TTEN(ZZ[q][:, c0:NCH], product(q, 0, c0), masked(f"off{LEVELS[l]}", NCH - c0), ALU.mult)\
                            .then_inc(S["z_masked"], 1)
                    beside(i, l, 0, parity, first, last)
                    for q in LANES:
                        dve.wait_ge(S["t_ready"], count(i, q, l, NL))
                        TTEN(TT[q][:, c0:NCH], TT[q][:, c0:NCH], product(q, 0, c0), ALU.add)\
                            .then_inc(S["tt_added"], 1)
                    beside(i, l, 1, parity, first, last)

            def chunks(i, parity, last):
                f = i + 1
                if not last:
                    every(norm_eps, f)
                    every(scale_ka, f)
                for c in range(NY):
                    for q in LANES:
                        s = bank(q, 1, P).rearrange("p (h t) -> p h t", h=2)
                        end = E[parity][q][:, c, CHUNK:CHUNK + 1]
                        dve.wait_ge(S["s_ready"], count(i, q, c, NY))
                        if c == 0:
                            TS(SS[q][:], s, end, None, ALU.mult).then_inc(S["s_made"], 1)
                        else:
                            dve.wait_ge(S["s_decayed"], count(i, q, c - 1, NY - 1))
                            STT(out=SS[q][:], in0=s, scalar=end, in1=SW[q][:], op0=ALU.mult, op1=ALU.add)\
                                .then_inc(S["s_made"], 1)
                    if c == 0 and not last:
                        every(make_k2, f)
                        every(bonus_rk, f)
                    if c == 1 and not last:
                        norm_invert(f, 0)
                        make_kk(f, 0)
                    if c == 2 and not last:
                        norm_invert(f, 1)
                        make_kk(f, 1)
                    if c == 3 and not last:
                        for q in LANES:
                            make_a(f, q, 1 - parity)
                            b_double(f, q)
                            bonus(f, q, 1 - parity)

            def middle(i, parity, first, last):
                mask_gram(i)
                levels(i, parity, first, last)
                chunks(i, parity, last)

            dve.wait_ge(projected, proj_r.projected0 + KD // 2)
            dve.wait_ge(params_halved, 1)
            dve.wait_ge(S["pads_cleared"], PADS)
            dve.wait_ge(S["ones_set"], 4)
            every(pick, 0)
            for step in (decay, cumulate, halve_a, scale_ka, norm_eps, make_k2, bonus_rk, norm_invert, make_kk):
                every(step, 0)
            dve.wait_ge(S["blocks_cleared"], BLOCKS + 6)
            every(make_a, 0, 0)
            every(b_double, 0)
            every(bonus, 0, 0)
            iterations(dve, middle)
            every(gn_centre, NI - 1)
            split_lo(dve, w_o, 0, 0, 0)
            every(gn_eps, NI - 1)
            for k in range(KB):
                y_lo_dve(dve, k)
            split_lo(dve, w_o, 0, 0, 1)
            for step in (gn_invert, gn_scale):
                every(step, NI - 1)
            every(add_bonus, NI - 1, 1)
            for k in range(KB, 2 * KB):
                y_lo_dve(dve, k)
            split_lo(dve, w_o, 0, 0, 2)
            for k in range(2 * KB, KD):
                y_lo_dve(dve, k)

        with nc.Block() as block:
            @block.sync
            def _(sp):
                tokens = []
                for half in range(2):
                    f = slice(D // 2 * half, D // 2 * (half + 1))
                    tokens += [(TOKS[0:N_META, 0, f], meta[:, f]), (TOKS[N_META:P, 0, f], x[0:P - N_META, f]),
                               (TOKS[:, 1, f], x[P - N_META:2 * P - N_META, f]),
                               (TOKS[0:L - 2 * P, 2, f], x[2 * P - N_META:SEQ, f])]
                sp.dma_start(C["ident"][:], const["ident"]).then_inc(ident_landed, 16)
                for n, (dst, src) in enumerate(tokens):
                    sp.dma_start(dst, src).then_inc(tokens_landed[n // 4], 16)

                def vectors_and_constants():
                    row = 0
                    for v in vec:
                        for n in range(v.shape[0]):
                            r = row + n
                            sp.dma_start(VROWS[KD * (r % 8):KD * (r % 8) + KD, r // 8, :],
                                         v[n].rearrange("(k p) -> k p", p=P)).then_inc(vectors_landed, 16)
                        row += v.shape[0]
                    for name in const:
                        if name != "ident":
                            sp.dma_start(C[name][:], const[name]).then_inc(const_landed, 16)

                load_blocks(sp, in0, vectors_and_constants)
                load_blocks(sp, out0)
                column = 0
                for name, width in (("rwkv_w1", LORA), ("rwkv_a1", LORA), ("rwkv_g1", GATE)):
                    sp.dma_start(LORA1[:, :, column:column + width], w[name].rearrange("(k p) n -> p k n", p=P))\
                      .then_inc(lora1_landed, 16)
                    column += width
                for ph in (proj_k, proj_v, proj_r):
                    load_blocks(sp, ph)
                scan_sp(sp)
                sp.wait_ge(S["tt_added"], KD * NL)
                for ph in phases[-3:]:
                    load_blocks(sp, ph)
                for i in range(8):
                    kg, tt = i // 2, i % 2
                    sp.wait_ge(*out_copied(i))
                    cols = slice(4 * P * kg, 4 * P * (kg + 1))
                    sp.dma_start(out[P * tt:P * (tt + 1), cols], OUT[:, tt, cols]).then_inc(out_stored, 16)
                sp.wait_ge(out_stored, 8 * 16)

            @block.gpsimd
            def _(pool):
                nc.gpsimd.memset(ZERO[:], 0.0).then_inc(zero_set, 1)
                pool.wait_ge(zero_set, 1)
                shift_pool(pool)
                scan_pool(pool)

            @block.scalar
            def _(act):
                for kg in range(4):
                    for i in range(3 * kg, 3 * kg + 3):
                        if i % 2 == 0:
                            act.wait_ge(turned, i + 1)
                            nc.scalar.activation(turned_target(i), turned_source(i), ACT.Copy)\
                              .then_inc(turned_copied[0], 1)
                    wait_for_x(act, kg)
                    for k in range(4 * kg, 4 * kg + 4):
                        x_hi_act(act, 0, k, ALL)
                    if kg < AHEAD:
                        split_hi(act, in0, 0, 0, kg)
                with_epilogues(act, in0, split_hi, epilogue_act, ahead=AHEAD, close=False)
                with_epilogues(act, out0, split_hi, epilogue_act, after=in0)
                ln_act(act, 0, ALL)
                for k in range(KD):
                    shift_act(act, 0, k, ALL)
                for k in range(KD):
                    mix_act(act, 0, k, k % 2)
                    if k % KB == KB - 1 and k // KB < AHEAD:
                        split_hi(act, proj_k, 0, 0, k // KB)
                with_epilogues(act, proj_k, split_hi, epilogue_act, side=mix_act, ahead=AHEAD, close=False)
                lora_act(act)
                with_epilogues(act, proj_v, split_hi, epilogue_act, side=mix_act, after=proj_k, close=False)
                with_epilogues(act, proj_r, split_hi, epilogue_act, after=proj_v)
                scan_act(act)
                with_epilogues(act, w_o, split_hi, epilogue_act, ahead=AHEAD, close=False)
                split_hi(act, in1, 0, 0, 0)
                split_hi(act, in1, 0, 0, 1)
                epilogue_act(act, w_o, w_o.steps - 1, 1)
                ln_act(act, 1, REAL, lambda: split_hi(act, in1, 0, 0, 2))
                for k in range(KD + 1):
                    if k < KD:
                        shift_act(act, 1, k, REAL)
                    if k > 0:
                        act.wait_ge(ln_shifted, KD + k)
                        x_hi_act(act, 1, k - 1, REAL)
                with_epilogues(act, in1, split_hi, epilogue_act, ahead=AHEAD, close=False)
                with_epilogues(act, out1, split_hi, epilogue_act, after=in1)
                ln_act(act, 2, REAL)
                for k in range(KD):
                    shift_act(act, 2, k, REAL)
                for i in range(OUT_BY_DVE, 8):
                    act.wait_ge(out_turned, i + 1)
                    nc.scalar.activation(out_piece(i), PS[:, i], ACT.Copy).then_inc(out_copied_act, 1)

            @block.vector
            def _(dve):
                for kg in range(4):
                    for i in range(3 * kg, 3 * kg + 3):
                        if i % 2:
                            dve.wait_ge(turned, i + 1)
                            nc.vector.tensor_copy(turned_target(i), turned_source(i)).then_inc(turned_copied[1], 1)
                    for k in range(4 * kg, 4 * kg + 4):
                        x_lo_dve(dve, 0, k, ALL)
                    if kg < AHEAD:
                        split_lo(dve, in0, 0, 0, kg)
                with_epilogues(dve, in0, split_lo, epilogue_dve, late=split_hidden, ahead=AHEAD, close=False)
                with_epilogues(dve, out0, split_lo, epilogue_dve, after=in0)
                dve.wait_ge(params_turned, 1)
                nc.vector.tensor_copy(PAR[:].rearrange("p v k -> p (v k)"), PS[:, 7, 0:NVEC * KD])\
                  .then_inc(params_copied, 1)
                dve.wait_ge(params_copied, 1)
                nc.vector.tensor_scalar(HALF[:], PAR[:, V_W0:V_W0 + 2], 0.5, None, ALU.mult).then_inc(params_halved, 1)
                ln_dve(dve, 0, ALL)
                lora_dve(dve)
                for k in range(KD + 1):
                    if k < KD:
                        mix_dve(dve, 0, k, k % 2)
                    if k > 0:
                        mix_lo_dve(dve, 0, k - 1, (k - 1) % 2)
                    if k and k % KB == 0 and k // KB <= AHEAD:
                        split_lo(dve, proj_k, 0, 0, k // KB - 1)
                with_epilogues(dve, proj_k, split_lo, epilogue_dve, side=mix_lo_dve, ahead=AHEAD)
                with_epilogues(dve, proj_v, split_lo, epilogue_dve, side=mix_lo_dve)
                with_epilogues(dve, proj_r, split_lo, epilogue_dve)
                scan_dve(dve)
                with_epilogues(dve, w_o, split_lo, epilogue_dve, ahead=AHEAD, close=False)
                split_lo(dve, in1, 0, 0, 0)
                split_lo(dve, in1, 0, 0, 1)
                epilogue_dve(dve, w_o, w_o.steps - 1, 1)
                ln_dve(dve, 1, REAL, lambda: split_lo(dve, in1, 0, 0, 2))
                for k in range(KD + 2):
                    if k < KD:
                        scale_dve(dve, 1, k, REAL)
                    if k > 1:
                        x_lo_dve(dve, 1, k - 2, REAL)
                with_epilogues(dve, in1, split_lo, epilogue_dve, late=split_hidden, ahead=AHEAD, close=False)
                with_epilogues(dve, out1, split_lo, epilogue_dve, after=in1)
                ln_dve(dve, 2, REAL)
                for k in range(KD):
                    scale_dve(dve, 2, k, REAL)
                for i in range(OUT_BY_DVE):
                    dve.wait_ge(out_turned, i + 1)
                    nc.vector.tensor_copy(out_piece(i), PS[:, i]).then_inc(out_copied_dve, 1)

            @block.tensor
            def _(pe):
                pe.wait_ge(ident_landed, 16)

                def turn_tokens(g, j):
                    if g == 0:
                        for i in range(0 if j == 0 else 3 * (j + 1), min(3 * (j + 2), 12)):
                            if i % 6 == 0:
                                pe.wait_ge(tokens_landed[i // 6], 64)
                            kg, tt = i // 3, i % 3
                            rows = TOK_ROWS[tt]
                            if i >= 4:
                                pe.wait_ge(turned_copied[i % 2], i // 2 - 1)
                            for k in range(4):
                                mm = nc.tensor.transpose(PS[:, 4 + i % 4, P * k:P * k + rows],
                                                         TOKS[0:rows, tt, P * (4 * kg + k):P * (4 * kg + k + 1)],
                                                         C["ident"][0:rows, 0:rows])
                            mm.then_inc(turned, 1)
                    elif j == 3:
                        wait_for_x(pe, 3)
                        pe.wait_ge(vectors_landed, 16 * NVEC)
                        for r in range(3):
                            rows = min(P, KD * NVEC - P * r)
                            mm = nc.tensor.transpose(PS[:, 7, P * r:P * r + rows], VROWS[0:rows, r, :],
                                                     C["ident"][0:rows, 0:rows])
                        mm.then_inc(params_turned, 1)

                multiply(pe, in0, turn_tokens)
                pe.wait_ge(const_landed, 16 * (len(const) - 1))
                multiply(pe, out0)
                ln_pe(pe, 0, out0)
                lora_pe(pe)
                for ph in (proj_k, proj_v, proj_r):
                    multiply(pe, ph)
                scan_pe(pe)
                multiply(pe, w_o)
                ln_pe(pe, 1, w_o)
                for ph in (in1, out1):
                    multiply(pe, ph)
                ln_pe(pe, 2, out1)
                for i in range(8):
                    kg, tt = i // 2, i % 2
                    pe.wait_ge(ln_shifted, 2 * KD + 4 * kg + 4)
                    at_ = N_META + P * tt
                    for k in range(4):
                        mm = nc.tensor.transpose(PS[:, i, P * k:P * (k + 1)], X[:, 4 * kg + k, at_:at_ + P],
                                                 C["ident"][:])
                    mm.then_inc(out_turned, 1)


CONST_COLUMNS = {k: a.shape[1] for k, a in constants().items()}


def kernel(x, meta_tokens, ln_g, ln_b, ffn_in, ffn_out, **more):
    import concourse.bacc as bacc
    from concourse.bass_utils import run_bass_kernel_spmd

    nc = bacc.Bacc("TRN2", target_bir_lowering=False, num_devices=1)
    arrays = {"x": x[0], "meta_tokens": meta_tokens, "ln_g": ln_g[0], "ln_b": ln_b[0],
              "ffn_in": ffn_in[0], "ffn_out": ffn_out[0]}
    for name in ("rwkv_w_rkv", "rwkv_w1", "rwkv_w2", "rwkv_a1", "rwkv_a2", "rwkv_g1", "rwkv_g2", "rwkv_w_o"):
        arrays[name] = more[name]
    for name in VECTORS[2:]:
        arrays[name] = more[name].reshape(-1, D)
    arrays = {n: np.ascontiguousarray(a) for n, a in arrays.items()}
    arrays |= {"c_" + n: a for n, a in constants().items()}
    aps = {n: nc.dram_tensor("in_" + n, a.shape, F32, kind="ExternalInput").ap() for n, a in arrays.items()}
    out = nc.dram_tensor("out", (SEQ, D), F32, kind="ExternalOutput").ap()
    rwkv_layer(nc, aps["x"], aps["meta_tokens"], aps, [aps[n] for n in VECTORS],
               {n[2:]: a for n, a in aps.items() if n.startswith("c_")}, out)
    result = run_bass_kernel_spmd(nc, [{"in_" + n: a for n, a in arrays.items()}], core_ids=[0])
    return result.results[0]["out"].reshape(1, SEQ, D)
```
